# Optimizing a Trainium2 kernel written in Bass

```python
import math
import jax, jax.numpy as jnp
from jax import lax
import numpy as np

'''One inference step of a hybrid diffusion / flow-matching backbone (DEPTH post-norm layers).

Each layer: adaLN modulation -> two parallel token mixers (gated short conv, differential
attention) on the same modulated input, merged by per-channel sigmoid gates, one output
projection, DeepNorm residual + LayerNorm; then adaLN -> channel mixer (dense SwiGLU on even
layers, top-2-of-8 SwiGLU experts on odd layers) -> DeepNorm residual + LayerNorm.

Inputs:
  x_prompt (BATCH, SEQ, D_MODEL)            context tokens of new requests (group i)
  x_sample (DEC_BATCH, DEC_SEQ, D_MODEL)    noisy latent tokens on a GRID_W-wide grid (group ii)
  cache_k, cache_v (DEC_BATCH, DEPTH, N_HEADS, PAST_LEN, 2*HEAD_DIM)  cached context keys/values
  c (DEC_BATCH, D_MODEL)                    conditioning of latent requests
  c_ctx (D_MODEL,)                          learned conditioning of context tokens
  followed by the weights.
Output tuple:
  y_prompt    (BATCH, SEQ, D_MODEL)
  y_sample    (DEC_BATCH, DEC_SEQ, D_MODEL)
  new_cache_k (BATCH, DEPTH, N_HEADS, SEQ, 2*HEAD_DIM)   context keys (no position) per layer
  new_cache_v (BATCH, DEPTH, N_HEADS, SEQ, 2*HEAD_DIM)   context values per layer
'''

D_MODEL = 1024
BATCH = 1
SEQ = 128
DEPTH = 2
DEC_BATCH = 1
DEC_SEQ = 128
PAST_LEN = 128

GRID_W = 64
D_CONV = 512
N_HEADS = 8
HEAD_DIM = 64
V_DIM = 2 * HEAD_DIM
ATTN_W = N_HEADS * V_DIM
AXIS_DIM = HEAD_DIM // 2
ROPE_BASE = 10000.0
Q_BLOCK = 128
D_FF = 2816
N_EXPERTS = 8
TOP_K = 2
D_FF_EXPERT = 1408
N_DENSE = (DEPTH + 1) // 2
N_MOE = DEPTH // 2
ALPHA = (2 * DEPTH) ** 0.25
BETA = (8 * DEPTH) ** -0.25
LN_EPS = 1e-5
D_IN = 3 * D_CONV + 3 * ATTN_W + 2 * D_MODEL
IN_SPLITS = [D_CONV, 2 * D_CONV, 3 * D_CONV, 3 * D_CONV + ATTN_W, 3 * D_CONV + 2 * ATTN_W,
             3 * D_CONV + 3 * ATTN_W, 3 * D_CONV + 3 * ATTN_W + D_MODEL]

kernel_name = 'hybrid_diffusion_conv_diffattn_step'

def layer_norm(x, g, b):
    xf = x.astype(jnp.float32)
    mu = jnp.mean(xf, axis=-1, keepdims=True)
    var = jnp.mean(jnp.square(xf - mu), axis=-1, keepdims=True)
    return ((xf - mu) * lax.rsqrt(var + LN_EPS) * g + b).astype(x.dtype)

def rms_norm(x, g):
    xf = x.astype(jnp.float32)
    return (xf * lax.rsqrt(jnp.mean(jnp.square(xf), axis=-1, keepdims=True) + LN_EPS) * g).astype(x.dtype)

def modulate(x, shift, scale):
    return x * (1 + scale) + shift

def axial_angles(n_tokens):
    rows = n_tokens // GRID_W
    row = jnp.repeat(jnp.arange(rows, dtype=jnp.float32), GRID_W)
    col = jnp.tile(jnp.arange(GRID_W, dtype=jnp.float32), rows)
    inv_freq = ROPE_BASE ** (-jnp.arange(0, AXIS_DIM, 2, dtype=jnp.float32) / AXIS_DIM)
    return row[:, None] * inv_freq, col[:, None] * inv_freq

def _rot(x, cos, sin):
    x1, x2 = jnp.split(x, 2, axis=-1)
    return jnp.concatenate([x1 * cos - x2 * sin, x1 * sin + x2 * cos], axis=-1)

def axial_rope(x, ang_r, ang_c):
    shp = x.shape
    xs = x.reshape(shp[:-1] + (2, HEAD_DIM))
    cr = jnp.cos(ang_r)[:, None, :].astype(x.dtype)
    sr = jnp.sin(ang_r)[:, None, :].astype(x.dtype)
    cc = jnp.cos(ang_c)[:, None, :].astype(x.dtype)
    sc = jnp.sin(ang_c)[:, None, :].astype(x.dtype)
    xr = _rot(xs[..., :AXIS_DIM], cr, sr)
    xc = _rot(xs[..., AXIS_DIM:], cc, sc)
    return jnp.concatenate([xr, xc], axis=-1).reshape(shp)

def short_conv(u, w, b):
    up = jnp.pad(u, ((0, 0), (1, 1), (0, 0)))
    return up[:, :-2] * w[0] + up[:, 1:-1] * w[1] + up[:, 2:] * w[2] + b

def diff_attention(q, k, v, lam):
    b, h, lq, _ = q.shape
    nb = lq // Q_BLOCK
    k1, k2 = k[..., :HEAD_DIM], k[..., HEAD_DIM:]
    scale = HEAD_DIM ** -0.5
    qb = q.reshape(b, h, nb, Q_BLOCK, 2 * HEAD_DIM).transpose(2, 0, 1, 3, 4)

    def one_block(qblk):
        s1 = jnp.einsum('bhqd,bhkd->bhqk', qblk[..., :HEAD_DIM], k1).astype(jnp.float32) * scale
        s2 = jnp.einsum('bhqd,bhkd->bhqk', qblk[..., HEAD_DIM:], k2).astype(jnp.float32) * scale
        p = jax.nn.softmax(s1, axis=-1) - lam * jax.nn.softmax(s2, axis=-1)
        return jnp.einsum('bhqk,bhkd->bhqd', p.astype(v.dtype), v)

    out = lax.map(one_block, qb)
    return out.transpose(1, 2, 0, 3, 4).reshape(b, h, lq, V_DIM)

def token_mixers(h, w_in_l, conv_w_l, conv_b_l, w_conv_out_l, subln_g_l, w_attn_out_l, w_out_l,
                 lam, lam_init, ang_r, ang_c, ctx_k, ctx_v):
    b, n, _ = h.shape
    gate_b, gate_c, u, q, k, v, g_conv, g_attn = jnp.split(h @ w_in_l, IN_SPLITS, axis=-1)
    y_conv = (gate_b * short_conv(gate_c * u, conv_w_l, conv_b_l)) @ w_conv_out_l
    q = q.reshape(b, n, N_HEADS, V_DIM).transpose(0, 2, 1, 3)
    k = k.reshape(b, n, N_HEADS, V_DIM).transpose(0, 2, 1, 3)
    v = v.reshape(b, n, N_HEADS, V_DIM).transpose(0, 2, 1, 3)
    if ang_r is not None:
        q = axial_rope(q, ang_r, ang_c)
        k = axial_rope(k, ang_r, ang_c)
    if ctx_k is not None:
        k_all = jnp.concatenate([ctx_k.astype(k.dtype), k], axis=2)
        v_all = jnp.concatenate([ctx_v.astype(v.dtype), v], axis=2)
    else:
        k_all, v_all = k, v
    o = rms_norm(diff_attention(q, k_all, v_all, lam), subln_g_l) * (1 - lam_init)
    y_attn = o.transpose(0, 2, 1, 3).reshape(b, n, ATTN_W) @ w_attn_out_l
    merged = jax.nn.sigmoid(g_conv) * y_conv + jax.nn.sigmoid(g_attn) * y_attn
    return merged @ w_out_l, k, v

def swiglu(h, wg, wu, wd):
    return (jax.nn.silu(h @ wg) * (h @ wu)) @ wd

def moe_swiglu(h, router, wg, wu, wd):
    probs = jax.nn.softmax((h @ router).astype(jnp.float32), axis=-1)
    top_v, top_i = lax.top_k(probs, TOP_K)
    top_v = top_v / jnp.sum(top_v, axis=-1, keepdims=True)
    gates = jnp.sum(jax.nn.one_hot(top_i, N_EXPERTS, dtype=jnp.float32) * top_v[..., None], axis=-2).astype(h.dtype)
    out = jnp.zeros_like(h)
    for e in range(N_EXPERTS):
        out = out + gates[..., e:e + 1] * swiglu(h, wg[e], wu[e], wd[e])
    return out

def setup_inputs(seed: int = 0) -> dict:
    key = jax.random.key(seed)
    ks = iter(jax.random.split(key, 40))

    def nrm(shape, scale):
        return jax.random.normal(next(ks), shape, jnp.float32) * scale

    d = D_MODEL
    return {
        'x_prompt': nrm((BATCH, SEQ, d), 1.0),
        'x_sample': nrm((DEC_BATCH, DEC_SEQ, d), 1.0),
        'cache_k': nrm((DEC_BATCH, DEPTH, N_HEADS, PAST_LEN, V_DIM), 1.0),
        'cache_v': nrm((DEC_BATCH, DEPTH, N_HEADS, PAST_LEN, V_DIM), 1.0),
        'c': nrm((DEC_BATCH, d), 1.0),
        'c_ctx': nrm((d,), 1.0),
        'ln_in_g': 1.0 + nrm((d,), 0.02),
        'ln_in_b': nrm((d,), 0.02),
        'ada_w': nrm((DEPTH, d, 6 * d), 0.5 * d ** -0.5),
        'ada_b': nrm((DEPTH, 6 * d), 0.02),
        'w_in': nrm((DEPTH, d, D_IN), d ** -0.5),
        'conv_w': nrm((DEPTH, 3, D_CONV), 0.5),
        'conv_b': nrm((DEPTH, D_CONV), 0.02),
        'w_conv_out': nrm((DEPTH, D_CONV, d), D_CONV ** -0.5),
        'lam_q1': nrm((DEPTH, HEAD_DIM), 0.1),
        'lam_k1': nrm((DEPTH, HEAD_DIM), 0.1),
        'lam_q2': nrm((DEPTH, HEAD_DIM), 0.1),
        'lam_k2': nrm((DEPTH, HEAD_DIM), 0.1),
        'subln_g': 1.0 + nrm((DEPTH, V_DIM), 0.02),
        'w_attn_out': nrm((DEPTH, ATTN_W, d), ATTN_W ** -0.5),
        'w_out': nrm((DEPTH, d, d), BETA * d ** -0.5),
        'ln1_g': 1.0 + nrm((DEPTH, d), 0.02),
        'ln1_b': nrm((DEPTH, d), 0.02),
        'ln2_g': 1.0 + nrm((DEPTH, d), 0.02),
        'ln2_b': nrm((DEPTH, d), 0.02),
        'ffn_w_gate': nrm((N_DENSE, d, D_FF), d ** -0.5),
        'ffn_w_up': nrm((N_DENSE, d, D_FF), d ** -0.5),
        'ffn_w_down': nrm((N_DENSE, D_FF, d), BETA * D_FF ** -0.5),
        'moe_router': nrm((N_MOE, d, N_EXPERTS), d ** -0.5),
        'moe_w_gate': nrm((N_MOE, N_EXPERTS, d, D_FF_EXPERT), d ** -0.5),
        'moe_w_up': nrm((N_MOE, N_EXPERTS, d, D_FF_EXPERT), d ** -0.5),
        'moe_w_down': nrm((N_MOE, N_EXPERTS, D_FF_EXPERT, d), BETA * D_FF_EXPERT ** -0.5),
    }

def reference(x_prompt, x_sample, cache_k, cache_v, c, c_ctx, ln_in_g, ln_in_b, ada_w, ada_b,
              w_in, conv_w, conv_b, w_conv_out, lam_q1, lam_k1, lam_q2, lam_k2, subln_g,
              w_attn_out, w_out, ln1_g, ln1_b, ln2_g, ln2_b, ffn_w_gate, ffn_w_up, ffn_w_down,
              moe_router, moe_w_gate, moe_w_up, moe_w_down):
    ang_r, ang_c = axial_angles(x_sample.shape[1])
    xp = layer_norm(x_prompt, ln_in_g, ln_in_b)
    xs = layer_norm(x_sample, ln_in_g, ln_in_b)
    new_k, new_v = [], []
    for l in range(DEPTH):
        lam_init = 0.8 - 0.6 * math.exp(-0.3 * l)
        lam = (jnp.exp(jnp.sum(lam_q1[l].astype(jnp.float32) * lam_k1[l].astype(jnp.float32)))
               - jnp.exp(jnp.sum(lam_q2[l].astype(jnp.float32) * lam_k2[l].astype(jnp.float32))) + lam_init)
        mp = jnp.split(jax.nn.silu(c_ctx) @ ada_w[l] + ada_b[l], 6, axis=-1)
        ms = [m[:, None, :] for m in jnp.split(jax.nn.silu(c) @ ada_w[l] + ada_b[l], 6, axis=-1)]
        mix_w = (w_in[l], conv_w[l], conv_b[l], w_conv_out[l], subln_g[l], w_attn_out[l], w_out[l], lam, lam_init)
        m_p, k_p, v_p = token_mixers(modulate(xp, mp[0], mp[1]), *mix_w, None, None, None, None)
        new_k.append(k_p)
        new_v.append(v_p)
        xp = layer_norm(ALPHA * xp + mp[2] * m_p, ln1_g[l], ln1_b[l])
        m_s, _, _ = token_mixers(modulate(xs, ms[0], ms[1]), *mix_w, ang_r, ang_c, cache_k[:, l], cache_v[:, l])
        xs = layer_norm(ALPHA * xs + ms[2] * m_s, ln1_g[l], ln1_b[l])
        hp = modulate(xp, mp[3], mp[4])
        hs = modulate(xs, ms[3], ms[4])
        if l % 2 == 0:
            i = l // 2
            f_p = swiglu(hp, ffn_w_gate[i], ffn_w_up[i], ffn_w_down[i])
            f_s = swiglu(hs, ffn_w_gate[i], ffn_w_up[i], ffn_w_down[i])
        else:
            i = l // 2
            f_p = moe_swiglu(hp, moe_router[i], moe_w_gate[i], moe_w_up[i], moe_w_down[i])
            f_s = moe_swiglu(hs, moe_router[i], moe_w_gate[i], moe_w_up[i], moe_w_down[i])
        xp = layer_norm(ALPHA * xp + mp[5] * f_p, ln2_g[l], ln2_b[l])
        xs = layer_norm(ALPHA * xs + ms[5] * f_s, ln2_g[l], ln2_b[l])
    new_cache_k = jnp.stack(new_k, axis=1)
    new_cache_v = jnp.stack(new_v, axis=1)
    return (xp, xs, new_cache_k, new_cache_v)


_drawn_inputs = setup_inputs


def setup_inputs(seed=0):
    import zlib

    import numpy as np

    out = dict(_drawn_inputs(seed))
    spreads = {}
    factors = {'ln_in_b': 2.677,
     'conv_b': 31.312,
     'lam_q1': 7.013,
     'lam_k1': 8.0,
     'lam_q2': 6.765,
     'lam_k2': 8.0,
     'subln_g': 39.687,
     'ln_in_g': 2.774}
    for name, (base, spread) in spreads.items():
        noise = np.random.default_rng([zlib.crc32(name.encode()), seed]).standard_normal(out[name].shape)
        drawn = base * np.exp(spread * noise) if base else spread * noise
        out[name] = __import__('jax').numpy.asarray(drawn.astype(out[name].dtype))
    for name, factor in factors.items():
        out[name] = (out[name] * factor).astype(out[name].dtype)
    return out
```

```python
import math
from contextlib import ExitStack

import concourse.bass as bass
from concourse import mybir

F32 = mybir.dt.float32
F32R = mybir.dt.float32r
ALU = mybir.AluOpType
ACT = mybir.ActivationFunctionType
AX_X = mybir.AxisListType.X

P = 128
D = 1024
KD = D // P
T = 128
G = 2
DEPTH = 2
D_CONV = 512
KC = D_CONV // P
HEADS = 8
HD = 64
VD = 2 * HD
FF = 1408
KF = FF // P
NE = 8
DENSE_PARTS = 2816 // FF
COL = 512
D_IN = 6656
IN_BLOCKS = D_IN // COL
ADA_BLOCKS = 6 * D // COL
FCOL = FF // 4
ALPHA = (2 * DEPTH) ** 0.25
EPS = 1e-5
SCALE = HD ** -0.5
SLOTS = 3
PARTS = 2
UNIT = 2048
DOWN = [(0, 3), (3, 6), (6, 9), (9, 11)]
HT = [(0, 2), (2, 5), (5, 8), (8, 11)]
JOBS = HEADS * G
B_GB, B_GC, B_U, B_Q, B_K, B_V, B_GCONV, B_GATTN = 0, 1, 2, 3, 5, 7, 9, 11

V_C = 0
V_CW, V_CB, V_SG, V_LAYER = 16, 28, 32, 17
V_LN = V_CW + V_LAYER * DEPTH
V_ROWS = V_LN + 4 * 2 * KD
N_VEC = 2 + 5 * DEPTH + 8


def program(nc, a, out):
    with ExitStack() as ctx:
        def sb(name, shape, dt=F32):
            return ctx.enter_context(nc.sbuf_tensor(name, shape, dt))

        def sem(name):
            return ctx.enter_context(nc.semaphore(name))

        raw = sb("raw", [P, SLOTS, 2 * UNIT])
        w_hi = sb("w_hi", [P, PARTS, UNIT], F32R)
        w_lo = sb("w_lo", [P, PARTS, UNIT], F32R)
        xT_hi = sb("xT_hi", [P, KD, G, T], F32R)
        xT_lo = sb("xT_lo", [P, KD, G, T], F32R)
        hT_hi = sb("hT_hi", [P, KF, G, T], F32R)
        hT_lo = sb("hT_lo", [P, KF, G, T], F32R)
        work = sb("work", [P, IN_BLOCKS, G * COL])
        x = sb("x", [P, G, D])
        gate_rows = sb("gate_rows", [5, 2, D])
        cache = sb("cache", [P, 2, HEADS, VD])
        vecT = sb("vecT", [P, P])
        ident = sb("ident", [P, P])
        sel = sb("sel", [5, G, P])
        cond = sb("cond", [P, 2 * KD])
        cond_st = sb("cond_st", [P, KD, 66], F32R)
        adaT = sb("adaT", [P, 4, KD, G])
        modA = sb("modA", [P, 2, KD, G])
        modB = sb("modB", [P, 2, KD, G])
        rope = sb("rope", [P, 2, 32])
        lamv = sb("lamv", [P, 4, HD])
        lams = sb("lams", [P, 8])
        st = sb("st", [P, G, 2, 6])
        mv = sb("mv", [P, G, 2])
        sd = sb("sd", [P, G])
        rstd = sb("rstd", [P, G])
        mx = sb("mx", [P, 2, 2])
        nmx = sb("nmx", [P, 2, 2])
        esum = sb("esum", [P, 2, 2])
        rsum = sb("rsum", [P, 2, 2])
        sublng = sb("sublng", [P, DEPTH])
        osq = sb("osq", [P, JOBS])
        osd = sb("osd", [P, JOBS])
        ors = sb("ors", [P, JOBS])
        eps_c = sb("eps_c", [P, 1])
        ones = sb("ones", [P, 1])
        r_raw = sb("r_raw", [P, KD, NE])
        r_hi = sb("r_hi", [P, KD, NE], F32R)
        r_lo = sb("r_lo", [P, KD, NE], F32R)
        iota = sb("iota", [P, NE])
        rt = sb("rt", [P, 8, G, NE])
        rs = sb("rs", [P, 8, G])
        gates = sb("gates", [P, G, NE])
        pad = sb("pad", [P, G, T + 2])
        cv = sb("cv", [P, G, T])
        bank = [ctx.enter_context(nc.psum_tensor(f"bank{i}", [P, COL], F32)) for i in range(8)]

        flat = work[:, :, :].rearrange("p b n -> p (b n)")
        ada_rows = flat[0:5, 0:6 * D]
        xhat = flat[:, B_V * 1024:(B_V + 2) * 1024].rearrange("p (g d) -> p g d", g=G)
        modulated = flat[:, B_Q * 1024:(B_Q + 2) * 1024].rearrange("p (g k t) -> p g k t", g=G, k=KD)
        gate_bc = flat[:, B_K * 1024:(B_K + 2) * 1024].rearrange("p (g d) -> p g d", g=G)
        h = flat[:, B_GCONV * 1024:B_GCONV * 1024 + G * FF].rearrange("p (g f) -> p g f", g=G)
        att = flat[:, 0:2048]
        e_buf = att[:, 0:1024].rearrange("p (b s k) -> p b s k", b=2, s=2)
        p_buf = att[:, 1024:1536].rearrange("p (b k) -> p b k", b=2)
        pT_buf = att[:, 1536:2048].rearrange("p (b k) -> p b k", b=2)
        qkT = flat[:, 2048:2048 + 6 * T].rearrange("p (b k) -> p b k", b=2)
        vec_rows = flat[:, 12288:12288 + P]
        ln_gb = [flat[:, b * 1024:(b + 2) * 1024].rearrange("p (w d) -> p w d", w=2) for b in (B_GCONV, 0)]
        rope_t = flat[:, 2048:3072]

        def blk(b, g):
            return work[:, b, g * COL:(g + 1) * COL]

        def four(b):
            return b[:, :].rearrange("p (k t) -> p k t", t=T)

        def conv_res(c):
            return work[:, B_U, c * G * T:(c + 1) * G * T].rearrange("p (g t) -> p g t", g=G)

        def keys(j):
            return 2 * T if j % 8 >= 4 else T

        def s_bank(j, i):
            return bank[j % 2 + 6 * i]

        def head_of(j):
            return 4 * (j // 8) + j % 4

        def lam_init(l):
            return 0.8 - 0.6 * math.exp(-0.3 * l)

        def head(b0, j):
            return work[:, b0 + j // 8, (j % 8) * VD:(j % 8 + 1) * VD]

        raw_in = [[sem(f"raw_in{i}_{u}") for u in range(2)] for i in range(SLOTS)]
        hi_done = sem("hi_done")
        lo_done = sem("lo_done")
        parts_free = sem("parts_free")
        ada_out = sem("ada_out")
        in_out0 = sem("in_out0")
        in_out1 = sem("in_out1")
        ld_vec, ld_x, ld_small, ld_lam = sem("ld_vec"), sem("ld_x"), sem("ld_small"), sem("ld_lam")
        ld_bias, ld_cache, ld_ln = sem("ld_bias"), sem("ld_cache"), sem("ld_ln")
        stored, kv_kept = sem("stored"), sem("kv_kept")
        const_ok = sem("const_ok")
        pool_s, dve_s, act_s = sem("pool_s"), sem("dve_s"), sem("act_s")
        vec_t, vec_ok, silu_ok, cond_hi, cond_ok = (sem(n) for n in ("vec_t", "vec_ok", "silu_ok", "cond_hi", "cond_ok"))
        stats_ok, std_ok, xhat_ok, x_ok = (sem(n) for n in ("stats_ok", "std_ok", "xhat_ok", "x_ok"))
        ada_cols, coef_ok, rows_ok = sem("ada_cols"), sem("coef_ok"), sem("rows_ok")
        xhat_t, mod_act, mod_dve, mod_hi, mod_ok = (sem(n) for n in ("xhat_t", "mod_act", "mod_dve", "mod_hi", "mod_ok"))
        sig_ok, gcu_ok, conv_t, conv_f, conv_hi, conv_ok = (
            sem(n) for n in ("sig_ok", "gcu_ok", "conv_t", "conv_f", "conv_hi", "conv_ok"))
        conv_out = sem("conv_out")
        lam_dot, lam_exp, roped = sem("lam_dot"), sem("lam_exp"), sem("roped")
        j_qk, j_qkT, j_s, j_max, j_exp, j_p, j_pT, j_pTc, j_o, j_oc, j_sq = (
            sem(n) for n in ("j_qk", "j_qkT", "j_s", "j_max", "j_exp", "j_p", "j_pT", "j_pTc", "j_o", "j_oc", "j_sq"))
        osd_ok, on_ok, oT_t, oT_hi, oT_ok = (sem(n) for n in ("osd_ok", "on_ok", "oT_t", "oT_hi", "oT_ok"))
        merged, m_t, m_hi, m_ok = (sem(n) for n in ("merged", "m_t", "m_hi", "m_ok"))
        bc_mm, bc_ok, res_ok = (sem(n) for n in ("bc_mm", "bc_ok", "res_ok"))
        g_silu, h_ok, hT_t, hT_hi_ok, hT_ok = (sem(n) for n in ("g_silu", "h_ok", "hT_t", "hT_hi_ok", "hT_ok"))
        r_parts, r_mm, r_max, r_exp, gates_ok = (sem(n) for n in ("r_parts", "r_mm", "r_max", "r_exp", "gates_ok"))

        Q_IN = ADA_BLOCKS // SLOTS
        Q_PRE = Q_IN + (IN_BLOCKS + 5) // SLOTS
        Q_EXPERT = 12 // SLOTS
        turn0 = [0, Q_PRE + DENSE_PARTS * Q_EXPERT]
        KINDS = [FCOL * 4] * 8 + [(k1 - k0) * COL for k0, k1 in DOWN]
        RUNS_IN = IN_BLOCKS // SLOTS

        def multiplied(eng, q, s, unit=1):
            eng.wait_ge(parts_free, q * (2 * SLOTS) + (2 * s + unit + 1 + PARTS))

        block = ctx.enter_context(nc.Block())

        @block.sync
        def _(sp):
            def load(q, s, unit, shape, src):
                if not isinstance(q, int) or q > 0:
                    sp.wait_ge(lo_done, (q - 1) * (2 * SLOTS) + (2 * s + unit + 1))
                n = shape[0] * shape[1]
                dst = raw[:, s, unit * UNIT:unit * UNIT + n].rearrange("p (k n) -> p k n", n=shape[1])
                sp.dma_start(dst, src).then_inc(raw_in[s][unit], 16)

            def columns(q, s, w, c0, n):
                for unit in range(2):
                    load(q, s, unit, (4, n), w[unit * 4 * P:(unit + 1) * 4 * P, :]
                         .rearrange("(k p) n -> p k n", p=P)[:, :, bass.ds(c0, n)])

            def rows(q, s, w, k0, k1):
                for unit in range(2):
                    load(q, s, unit, (k1 - k0, COL), w[k0 * P:k1 * P, unit * COL:(unit + 1) * COL]
                         .rearrange("(k p) n -> p k n", p=P))

            def expert(q, wg, wu, wd):
                for c in range(4):
                    columns(q + 2 * c // SLOTS, 2 * c % SLOTS, wg, c * FCOL, FCOL)
                    columns(q + (2 * c + 1) // SLOTS, (2 * c + 1) % SLOTS, wu, c * FCOL, FCOL)
                for d, (k0, k1) in enumerate(DOWN):
                    rows(q + (8 + d) // SLOTS, (8 + d) % SLOTS, wd, k0, k1)

            for l in range(DEPTH):
                for w, q0, turns in ((a["ada_w"][l], turn0[l], Q_IN), (a["w_in"][l], turn0[l] + Q_IN, RUNS_IN)):
                    peel = int(q0 == 0)
                    for s in range(SLOTS * peel):
                        columns(0, s, w, s * COL, COL)
                    with sp.Fori(peel, turns) as i:
                        for s in range(SLOTS):
                            columns(i + q0, s, w, i * (SLOTS * COL) + s * COL, COL)
                q = turn0[l] + Q_IN + RUNS_IN
                columns(q, 0, a["w_in"][l], (IN_BLOCKS - 1) * COL, COL)
                rows(q, 1, a["w_conv_out"][l], 0, 4)
                rows(q, 2, a["w_attn_out"][l], 0, 4)
                rows(q + 1, 0, a["w_attn_out"][l], 4, 8)
                rows(q + 1, 1, a["w_out"][l], 0, 4)
                rows(q + 1, 2, a["w_out"][l], 4, 8)
                q += 2
                if l == 0:
                    for e in range(DENSE_PARTS):
                        expert(q + e * Q_EXPERT, a["ffn_w_gate"][0][:, e * FF:(e + 1) * FF],
                               a["ffn_w_up"][0][:, e * FF:(e + 1) * FF], a["ffn_w_down"][0][e * FF:(e + 1) * FF, :])
                else:
                    with sp.Fori(0, NE) as e:
                        one = [a[n][0, bass.ds(e, 1)].rearrange("e d f -> (e d) f")
                               for n in ("moe_w_gate", "moe_w_up", "moe_w_down")]
                        expert(e * Q_EXPERT + q, *one)

        @block.gpsimd
        def _(pool):
            n_self = [0]

            def then(ins):
                n_self[0] += 1
                ins.then_inc(pool_s, 1)
                pool.wait_ge(pool_s, n_self[0])

            n_vec = 0

            def vec(row, src, n):
                pool.dma_start(vec_rows[row:row + n, :], src.rearrange("(n p) -> n p", p=P)).then_inc(ld_vec, 16)

            then(pool.memset(vec_rows[:, :], 0.0))
            vec(V_C, a["c_ctx"], KD)
            vec(V_C + KD, a["c"][0], KD)
            for l in range(DEPTH):
                r = l * V_LAYER
                for w in range(3):
                    vec(V_CW + r + 4 * w, a["conv_w"][l, w], KC)
                vec(V_CB + r, a["conv_b"][l], KC)
                vec(V_SG + r, a["subln_g"][l], 1)
            for n, (g, b) in enumerate(((a["ln_in_g"], a["ln_in_b"]), (a["ln1_g"][0], a["ln1_b"][0]),
                                        (a["ln2_g"][0], a["ln2_b"][0]), (a["ln1_g"][1], a["ln1_b"][1]))):
                vec(V_LN + n * 16, g, KD)
                vec(V_LN + n * 16 + KD, b, KD)
            pool.dma_start(x[:, 0, :], a["x_prompt"][0]).then_inc(ld_x, 16)
            pool.dma_start(x[:, 1, :], a["x_sample"][0]).then_inc(ld_x, 16)
            then(pool.memset(ident[:, :], 0.0))
            then(pool.affine_select(out=ident[:, :], in_=ident[:, :], compare_op=ALU.not_equal, fill=1.0, base=0,
                                    pattern=[[-1, P]], channel_multiplier=1))
            then(pool.memset(sel[:, :, :], 1.0))
            then(pool.affine_select(out=sel[:, 0, :], in_=sel[:, 0, :], compare_op=ALU.not_equal, fill=0.0,
                                    base=-2, pattern=[[0, P]], channel_multiplier=1))
            then(pool.affine_select(out=sel[:, 0, :], in_=sel[:, 0, :], compare_op=ALU.not_equal, fill=0.0,
                                    base=-3, pattern=[[0, P]], channel_multiplier=1))
            then(pool.affine_select(out=sel[:, 1, :], in_=sel[:, 1, :], compare_op=ALU.is_ge, fill=0.0,
                                    base=-2, pattern=[[0, P]], channel_multiplier=1))
            for v in range(NE):
                then(pool.memset(iota[:, v:v + 1], float(v - NE)))
            then(pool.memset(eps_c[:, :], EPS))
            then(pool.memset(pad[:, :, :], 0.0))
            then(pool.memset(ones[:, :], 1.0))
            pool.sem_inc(const_ok, 1)
            pool.dma_start(rope[:, :, :], a["rope"]).then_inc(ld_small, 16)
            pool.dma_start(r_raw[:, :, :], a["moe_router"][0].rearrange("(k p) e -> p k e", p=P)).then_inc(ld_small, 16)

            def load_ln(n):
                g, b = [(a["ln_in_g"], a["ln_in_b"]), (a["ln1_g"][0], a["ln1_b"][0]), (a["ln2_g"][0], a["ln2_b"][0]),
                        (a["ln1_g"][1], a["ln1_b"][1]), (a["ln2_g"][1], a["ln2_b"][1])][n]
                pool.dma_start(ln_gb[n % 2][:, 0, :], g.unsqueeze(0).to_broadcast([P, D])).then_inc(ld_ln, 16)
                pool.dma_start(ln_gb[n % 2][:, 1, :], b.unsqueeze(0).to_broadcast([P, D])).then_inc(ld_ln, 16)

            def make_x(n):
                pool.wait_ge(ld_ln, 32 * (n + 1))
                for g in range(G):
                    pool.wait_ge(xhat_ok, G * n + g + 1)
                    then(pool.tensor_tensor(x[:, g, :], xhat[:, g, :], ln_gb[n % 2][:, 0, :], ALU.mult))
                    then(pool.tensor_tensor(x[:, g, :], x[:, g, :], ln_gb[n % 2][:, 1, :], ALU.add))
                pool.sem_inc(x_ok, 1)

            load_ln(0)
            for l in range(DEPTH):
                if l:
                    pool.wait_ge(lam_dot, l)
                for i, name in enumerate(("lam_q1", "lam_k1", "lam_q2", "lam_k2")):
                    pool.dma_start(lamv[:, i, :], a[name][l].unsqueeze(0).to_broadcast([P, HD])).then_inc(ld_lam, 16)
                if l:
                    pool.wait_ge(rows_ok, l)
                    pool.wait_ge(coef_ok, l)
                    pool.wait_ge(res_ok, 2 * l)
                pool.dma_start(ada_rows[4:5, :], a["ada_b"][l].unsqueeze(0)).then_inc(ld_bias, 16)
                if l:
                    pool.wait_ge(j_oc, JOBS * l)
                pool.dma_start(cache[:, 0], a["cache_k"][0, l].rearrange("h t d -> t h d")).then_inc(ld_cache, 16)
                pool.dma_start(cache[:, 1], a["cache_v"][0, l].rearrange("h t d -> t h d")).then_inc(ld_cache, 16)
                make_x(2 * l)
                pool.wait_ge(in_out0, SLOTS + IN_BLOCKS * l + B_V + 2)
                for i, (b0, o) in enumerate(((B_K, out[2]), (B_V, out[3]))):
                    for half in range(2):
                        pool.dma_start(o[0, l, 4 * half:4 * half + 4].rearrange("h t d -> t h d"),
                                       blk(b0 + half, 0).rearrange("p (h d) -> p h d", h=4)).then_inc(kv_kept, 16)
                pool.wait_ge(j_oc, JOBS * (l + 1))
                load_ln(2 * l + 1)
                make_x(2 * l + 1)
                pool.wait_ge(hT_t, 4 * (DENSE_PARTS + l * NE))
                load_ln(2 * l + 2)
            make_x(2 * DEPTH)
            pool.dma_start(out[0][0], x[:, 0, :]).then_inc(stored, 16)
            pool.dma_start(out[1][0], x[:, 1, :]).then_inc(stored, 16)
            pool.wait_ge(stored, 32)
            pool.wait_ge(kv_kept, 64 * DEPTH)

        @block.scalar
        def _(act):
            act_n = [0]

            def then(ins):
                act_n[0] += 1
                ins.then_inc(act_s, 1)
                act.wait_ge(act_s, act_n[0])

            def hi(q, s, unit, n=UNIT):
                act.wait_ge(raw_in[s][unit], q * 16 + 16)
                act.wait_ge(parts_free, q * (2 * SLOTS) + (2 * s + unit + 1))
                nc.scalar.activation(w_hi[:, unit, 0:n], raw[:, s, unit * UNIT:unit * UNIT + n], ACT.Copy)\
                    .then_inc(hi_done, 1)

            def hi_block(q, s, n=UNIT):
                hi(q, s, 0, n)
                hi(q, s, 1, n)

            def ln_std(n):
                for g in range(G):
                    act.wait_ge(stats_ok, G * n + g + 1)
                    nc.scalar.activation(sd[:, g:g + 1], mv[:, g, 1:2], ACT.Sqrt, bias=eps_c[:, 0:1]).then_inc(std_ok, 1)

            def modulate(n):
                for g in range(G):
                    act.wait_ge(xhat_t, G * n + g + 1)
                    for k in range(4):
                        ins = nc.scalar.activation(modulated[:, g, k, :], bank[2 * g][:, k * T:(k + 1) * T], ACT.Identity,
                                                   bias=modB[:, n % 2, k, g:g + 1], scale=modA[:, n % 2, k, g:g + 1])
                    ins.then_inc(mod_act, 1)
                for g in range(G):
                    act.wait_ge(mod_act, G * n + g + 1)
                    act.wait_ge(mod_dve, G * n + g + 1)
                    nc.scalar.activation(xT_hi[:, :, g, :], modulated[:, g, :, :], ACT.Copy).then_inc(mod_hi, 1)

            def gate_broadcast(n):
                for i in range(4):
                    act.wait_ge(bc_mm, 4 * n + i + 1)
                    nc.scalar.activation(gate_bc[:, i // 2, (i % 2) * COL:(i % 2 + 1) * COL], bank[i][:, :], ACT.Copy)\
                        .then_inc(bc_ok, 1)

            def expert(q, ec, behind):
                sizes = KINDS + [behind]
                for j in range(12):
                    nq, ns, n = q + (j + 1) // SLOTS, (j + 1) % SLOTS, sizes[j + 1]
                    if n:
                        hi(nq, ns, 0, n)
                    if j in (2, 4, 6, 9):
                        c = (2, 4, 6, 9).index(j)
                        k0, k1 = HT[c]
                        act.wait_ge(hT_t, ec * 4 + (c + 1))
                        for g in range(G):
                            ins = nc.scalar.activation(hT_hi[:, k0:k1, g, :],
                                                       bank[2 + g][:, 0:(k1 - k0) * T].rearrange("p (k t) -> p k t", t=T),
                                                       ACT.Copy)
                        ins.then_inc(hT_hi_ok, 1)
                    if n:
                        hi(nq, ns, 1, n)
                    if j < 8 and j % 2 == 0:
                        multiplied(act, q + j // SLOTS, j % SLOTS)
                        for g in range(G):
                            ins = nc.scalar.activation(h[:, g, j // 2 * FCOL:(j // 2 + 1) * FCOL], bank[g][:, 0:FCOL], ACT.Silu)
                        ins.then_inc(g_silu, 1)

            act.sem_inc(in_out0, SLOTS)
            act.wait_ge(const_ok, 1)
            act.wait_ge(vec_ok, 1)
            nc.scalar.activation(cond[:, :], vecT[:, V_C:V_C + 2 * KD], ACT.Silu).then_inc(silu_ok, 1)
            act.wait_ge(silu_ok, 1)
            act.wait_ge(cond_hi, 1)
            for g in range(G):
                nc.scalar.activation(cond_st[:, :, 2 * g:2 * g + 1], cond[:, g * KD:(g + 1) * KD].unsqueeze(2), ACT.Copy)\
                    .then_inc(cond_hi, 1)
            act.wait_ge(ld_small, 32)
            nc.scalar.activation(r_hi[:, :, :], r_raw[:, :, :], ACT.Copy).then_inc(r_parts, 1)
            ln_std(0)
            hi_block(0, 0)
            for l in range(DEPTH):
                q0 = turn0[l]
                with act.Fori(0, Q_IN) as i:
                    for s in range(SLOTS):
                        hi_block(i + (q0 + (s + 1) // SLOTS), (s + 1) % SLOTS)
                act.wait_ge(ada_out, ADA_BLOCKS * (l + 1) + SLOTS)
                act.wait_ge(ld_bias, 16 * (l + 1))
                nc.scalar.activation(gate_rows[:, 0, :], ada_rows[:, 2 * D:3 * D], ACT.Copy)
                nc.scalar.activation(gate_rows[:, 1, :], ada_rows[:, 5 * D:6 * D], ACT.Copy).then_inc(rows_ok, 1)
                act.wait_ge(coef_ok, l + 1)
                act.wait_ge(rows_ok, l + 1)
                modulate(2 * l)
                act.wait_ge(x_ok, 2 * l + 1)
                q0 += Q_IN
                with act.Fori(0, RUNS_IN) as i:
                    for s in range(SLOTS):
                        hi_block(i + (q0 + (s + 1) // SLOTS), (s + 1) % SLOTS)
                        multiplied(act, i + q0, s)
                        nc.scalar.activation(work[:, bass.ds(i * SLOTS + s, 1), 0:COL], bank[2 * s][:, :].unsqueeze(1),
                                             ACT.Copy).then_inc(in_out0, 1)
                q0 += RUNS_IN
                hi_block(q0, 1)
                multiplied(act, q0, 0)
                nc.scalar.activation(blk(IN_BLOCKS - 1, 0), bank[0][:, :], ACT.Copy).then_inc(in_out0, 1)
                act.wait_ge(in_out0, SLOTS + IN_BLOCKS * (l + 1))
                act.wait_ge(in_out1, SLOTS + IN_BLOCKS * (l + 1))
                for b in range(B_GCONV, IN_BLOCKS):
                    nc.scalar.activation(work[:, b, :], work[:, b, :], ACT.Sigmoid).then_inc(sig_ok, 1)
                for c in range(KC):
                    act.wait_ge(conv_f, KC * l + c + 1)
                    nc.scalar.activation(xT_hi[:, c, :, :], conv_res(c), ACT.Copy).then_inc(conv_hi, 1)
                hi_block(q0, 2)
                act.wait_ge(lam_dot, l + 1)
                nc.scalar.activation(lams[:, 2:4], lams[:, 0:2], ACT.Exp).then_inc(lam_exp, 1)
                for step in range(JOBS + 3):
                    j = step
                    if j < JOBS:
                        n = keys(j) + T
                        act.wait_ge(j_qk, JOBS * l + j + 1)
                        if j >= 2:
                            act.wait_ge(j_s, JOBS * l + j - 1)
                        nc.scalar.activation(qkT[:, j % 2, 0:n], bank[2 + j % 2][:, 0:n], ACT.Copy).then_inc(j_qkT, 1)
                    j = step - 1
                    if 0 <= j < JOBS:
                        n = keys(j)
                        act.wait_ge(j_max, JOBS * l + j + 1)
                        if j >= 2:
                            act.wait_ge(j_p, JOBS * l + j - 1)
                        for i in range(2):
                            ins = nc.scalar.activation(e_buf[:, j % 2, i, 0:n], s_bank(j, i)[:, 0:n], ACT.Exp,
                                                       bias=nmx[:, j % 2, i:i + 1], scale=SCALE,
                                                       accum_out=esum[:, j % 2, i:i + 1])
                        ins.then_inc(j_exp, 1)
                    j = step - 3
                    if 0 <= j < JOBS:
                        act.wait_ge(j_oc, JOBS * l + j + 1)
                        if JOBS * l + j:
                            act.wait_ge(j_sq, JOBS * l + j)
                        nc.scalar.activation(cv[:, 0, :], head(B_Q, j), ACT.Square, accum_out=osq[:, j:j + 1]).then_inc(j_sq, 1)
                act.wait_ge(j_sq, JOBS * (l + 1))
                nc.scalar.activation(osd[:, :], osq[:, :], ACT.Sqrt, bias=eps_c[:, 0:1], scale=1.0 / VD).then_inc(osd_ok, 1)
                for i in range(4):
                    act.wait_ge(oT_t, 4 * l + i + 1)
                    nc.scalar.activation(hT_hi[:, 4 * (i // 2):4 * (i // 2) + 4, i % 2, :], four(bank[i]), ACT.Copy,
                                         scale=sublng[:, l:l + 1]).then_inc(oT_hi, 1)
                hi_block(q0 + 1, 0)
                hi_block(q0 + 1, 1)
                for i in range(4):
                    act.wait_ge(m_t, 4 * l + i + 1)
                    nc.scalar.activation(xT_hi[:, 4 * (i % 2):4 * (i % 2) + 4, i // 2, :], four(bank[i]), ACT.Copy)\
                        .then_inc(m_hi, 1)
                act.wait_ge(kv_kept, 64 * (l + 1))
                gate_broadcast(2 * l)
                hi_block(q0 + 1, 2)
                q0 += 2
                hi_block(q0, 0, KINDS[0])
                ln_std(2 * l + 1)
                modulate(2 * l + 1)
                if l == 0:
                    for e in range(DENSE_PARTS):
                        expert(q0 + e * Q_EXPERT, e, KINDS[0] if e + 1 < DENSE_PARTS else UNIT)
                else:
                    act.wait_ge(r_max, 1)
                    for g in range(G):
                        ins = nc.scalar.activation(rt[:, 1, g, :], rt[:, 0, g, :], ACT.Exp, bias=rs[:, 0, g:g + 1],
                                                   accum_out=rs[:, 1, g:g + 1])
                    ins.then_inc(r_exp, 1)
                    with act.Fori(0, NE - 1) as e:
                        expert(e * Q_EXPERT + q0, e + DENSE_PARTS, KINDS[0])
                    expert(q0 + (NE - 1) * Q_EXPERT, DENSE_PARTS + NE - 1, None)
                gate_broadcast(2 * l + 1)
                ln_std(2 * l + 2)

        @block.vector
        def _(dve):
            dve_n = [0]
            V = nc.vector

            def then(ins):
                dve_n[0] += 1
                ins.then_inc(dve_s, 1)
                dve.wait_ge(dve_s, dve_n[0])

            def lo(q, s, unit, n=UNIT):
                dve.wait_ge(hi_done, q * (2 * SLOTS) + (2 * s + unit + 1))
                V.tensor_tensor(w_lo[:, unit, 0:n], raw[:, s, unit * UNIT:unit * UNIT + n], w_hi[:, unit, 0:n].bitcast(F32),
                                ALU.subtract).then_inc(lo_done, 1)

            def lo_block(q, s, n=UNIT):
                lo(q, s, 0, n)
                lo(q, s, 1, n)

            def layer_norm(n):
                for g in range(G):
                    for half in range(2):
                        ins = V.bn_stats(st[:, g, half, :], x[:, g, half * COL:(half + 1) * COL])
                    then(ins)
                    V.bn_aggr(mv[:, g, :], st[:, g, :, :].rearrange("p a b -> p (a b)")).then_inc(stats_ok, 1)
                for g in range(G):
                    dve.wait_ge(std_ok, G * n + g + 1)
                    then(V.reciprocal(rstd[:, g:g + 1], sd[:, g:g + 1]))
                    V.tensor_scalar(xhat[:, g, :], x[:, g, :], mv[:, g, 0:1], rstd[:, g:g + 1], ALU.subtract, ALU.mult)\
                        .then_inc(xhat_ok, 1)

            def modulate(n):
                for g in range(G):
                    dve.wait_ge(xhat_t, G * n + g + 1)
                    for k in range(4, KD):
                        ins = V.tensor_scalar(modulated[:, g, k, :], bank[2 * g + 1][:, (k - 4) * T:(k - 3) * T],
                                              modA[:, n % 2, k, g:g + 1], modB[:, n % 2, k, g:g + 1], ALU.mult, ALU.add)
                    ins.then_inc(mod_dve, 1)
                for g in range(G):
                    dve.wait_ge(mod_hi, G * n + g + 1)
                    V.tensor_tensor(xT_lo[:, :, g, :], modulated[:, g, :, :], xT_hi[:, :, g, :].bitcast(F32), ALU.subtract)\
                        .then_inc(mod_ok, 1)

            def residual(n, q):
                multiplied(dve, q, 2)
                dve.wait_ge(bc_ok, 4 * (n + 1))
                dve.wait_ge(x_ok, n + 1)
                for g in range(G):
                    for half in range(2):
                        bc = gate_bc[:, g, half * COL:(half + 1) * COL]
                        ins = V.tensor_tensor(bc, bank[4 + 2 * g + half][:, :], bc, ALU.mult)
                then(ins)
                for g in range(G):
                    ins = V.scalar_tensor_tensor(out=x[:, g, :], in0=x[:, g, :], scalar=ALPHA, in1=gate_bc[:, g, :],
                                                 op0=ALU.mult, op1=ALU.add)
                then(ins)
                dve.sem_inc(res_ok, 1)

            def expert(q, ec, behind, gate):
                sizes = KINDS + [behind]
                for j in range(12):
                    nq, ns, n = q + (j + 1) // SLOTS, (j + 1) % SLOTS, sizes[j + 1]
                    if n:
                        lo(nq, ns, 0, n)
                    if j in (2, 4, 6, 9):
                        c = (2, 4, 6, 9).index(j)
                        k0, k1 = HT[c]
                        dve.wait_ge(hT_hi_ok, ec * 4 + (c + 1))
                        for g in range(G):
                            ins = V.tensor_tensor(hT_lo[:, k0:k1, g, :],
                                                  bank[2 + g][:, 0:(k1 - k0) * T].rearrange("p (k t) -> p k t", t=T),
                                                  hT_hi[:, k0:k1, g, :].bitcast(F32), ALU.subtract)
                        ins.then_inc(hT_ok, 1)
                    if n:
                        lo(nq, ns, 1, n)
                    if j < 8 and j % 2 == 1:
                        c = j // 2
                        multiplied(dve, q + j // SLOTS, j % SLOTS)
                        dve.wait_ge(g_silu, ec * 4 + (c + 1))
                        for g in range(G):
                            hc = h[:, g, c * FCOL:(c + 1) * FCOL]
                            ins = V.scalar_tensor_tensor(out=hc, in0=hc, scalar=gate(g), in1=bank[2 + g][:, 0:FCOL],
                                                         op0=ALU.mult, op1=ALU.mult)
                        ins.then_inc(h_ok, 1)

            def route():
                E = lambda i: rt[:, i, :, :]
                B = lambda i: rs[:, i, :].unsqueeze(2).to_broadcast([P, G, NE])
                dve.wait_ge(r_mm, 1)
                then(V.tensor_copy(E(0), bank[2][:, 0:G * NE].rearrange("p (g e) -> p g e", g=G)))
                then(V.tensor_reduce(rs[:, 0, :], E(0), AX_X, ALU.max, negate=True))
                dve.sem_inc(r_max, 1)
                dve.wait_ge(r_exp, 1)
                then(V.reciprocal(rs[:, 2, :], rs[:, 1, :]))
                then(V.tensor_tensor(E(1), E(1), B(2), ALU.mult))
                far = iota[:, :].unsqueeze(1).to_broadcast([P, G, NE])
                for i, best in ((0, 3), (1, 4)):
                    then(V.tensor_reduce(rs[:, best, :], E(1), AX_X, ALU.max))
                    then(V.tensor_tensor(E(2), E(1), B(best), ALU.is_equal))
                    then(V.tensor_tensor(E(3), E(2), far, ALU.mult))
                    then(V.tensor_reduce(rs[:, 5, :], E(3), AX_X, ALU.min))
                    then(V.tensor_tensor(E(4 + i), far, B(5), ALU.is_equal))
                    if i == 0:
                        then(V.scalar_tensor_tensor(out=E(1), in0=E(4), scalar=-2.0, in1=E(1), op0=ALU.mult, op1=ALU.add))
                then(V.tensor_tensor(rs[:, 6, :], rs[:, 3, :], rs[:, 4, :], ALU.add))
                then(V.reciprocal(rs[:, 7, :], rs[:, 6, :]))
                for i in (0, 1):
                    then(V.tensor_tensor(rs[:, 3 + i, :], rs[:, 3 + i, :], rs[:, 7, :], ALU.mult))
                    then(V.tensor_tensor(E(4 + i), E(4 + i), B(3 + i), ALU.mult))
                then(V.tensor_tensor(gates[:, :, :], E(4), E(5), ALU.add))
                dve.sem_inc(gates_ok, 1)

            def rotate(b):
                v = blk(b, 1).rearrange("p (m c h i) -> p m c h i", c=2, h=2, i=16)
                x1, x2 = v[:, :, :, 0, :], v[:, :, :, 1, :]
                t4 = [rope_t[:, i * 256:(i + 1) * 256].rearrange("p (m c i) -> p m c i", c=2, i=16) for i in range(4)]
                cos = rope[:, 0, :].rearrange("p (c i) -> p c i", c=2).unsqueeze(1).to_broadcast([P, 8, 2, 16])
                sin = rope[:, 1, :].rearrange("p (c i) -> p c i", c=2).unsqueeze(1).to_broadcast([P, 8, 2, 16])
                V.tensor_tensor(t4[0], x1, cos, ALU.mult)
                V.tensor_tensor(t4[1], x2, sin, ALU.mult)
                V.tensor_tensor(t4[2], x1, sin, ALU.mult)
                then(V.tensor_tensor(t4[3], x2, cos, ALU.mult))
                V.tensor_tensor(x1, t4[0], t4[1], ALU.subtract)
                then(V.tensor_tensor(x2, t4[2], t4[3], ALU.add))

            dve.sem_inc(ada_out, SLOTS)
            dve.sem_inc(in_out1, SLOTS)
            V.memset(cond_st[:, :, :].bitcast(F32), 0.0).then_inc(cond_hi, 1)
            dve.wait_ge(vec_t, 1)
            V.tensor_copy(vecT[:, :], bank[7][:, 0:P]).then_inc(vec_ok, 1)
            dve.wait_ge(ld_x, 32)
            layer_norm(0)
            dve.wait_ge(cond_hi, 1 + G)
            for g in range(G):
                V.tensor_tensor(cond_st[:, :, 2 * g + 1:2 * g + 2], cond[:, g * KD:(g + 1) * KD].unsqueeze(2),
                                cond_st[:, :, 2 * g:2 * g + 1].bitcast(F32), ALU.subtract).then_inc(cond_ok, 1)
            dve.wait_ge(r_parts, 1)
            V.tensor_tensor(r_lo[:, :, :], r_raw[:, :, :], r_hi[:, :, :].bitcast(F32), ALU.subtract).then_inc(r_parts, 1)
            dve.wait_ge(const_ok, 1)
            dve.wait_ge(vec_ok, 1)
            for l in range(DEPTH):
                then(V.tensor_scalar(sublng[:, l:l + 1], vecT[:, V_SG + V_LAYER * l:V_SG + V_LAYER * l + 1],
                                     1.0 - lam_init(l), None, ALU.mult))
            lo_block(0, 0)
            for l in range(DEPTH):
                q0 = turn0[l]
                with dve.Fori(0, Q_IN) as i:
                    for s in range(SLOTS):
                        lo_block(i + (q0 + (s + 1) // SLOTS), (s + 1) % SLOTS)
                        multiplied(dve, i + q0, s)
                        V.tensor_copy(ada_rows[0:4, bass.ds(i * (SLOTS * COL) + s * COL, COL)], bank[4 + s][0:4, :])\
                            .then_inc(ada_out, 1)
                dve.wait_ge(ada_cols, l + 1)
                then(V.tensor_copy(adaT[:, :, :, :].rearrange("p v k g -> p (v k g)"), bank[7][:, 0:4 * KD * G]))
                for i in range(2):
                    ln = V_LN + (2 * l + i) * 2 * KD
                    ln_g = vecT[:, ln:ln + KD].unsqueeze(2).to_broadcast([P, KD, G])
                    ln_b = vecT[:, ln + KD:ln + 2 * KD].unsqueeze(2).to_broadcast([P, KD, G])
                    V.scalar_tensor_tensor(out=modA[:, i], in0=adaT[:, 2 * i + 1], scalar=1.0, in1=ln_g, op0=ALU.add, op1=ALU.mult)
                    then(V.scalar_tensor_tensor(out=modB[:, i], in0=adaT[:, 2 * i + 1], scalar=1.0, in1=ln_b, op0=ALU.add,
                                                op1=ALU.mult))
                    then(V.tensor_tensor(modB[:, i], modB[:, i], adaT[:, 2 * i], ALU.add))
                dve.sem_inc(coef_ok, 1)
                modulate(2 * l)
                dve.wait_ge(ld_lam, 64 * (l + 1))
                for i in range(2):
                    ins = V.tensor_tensor_reduce(out=lamv[:, 2 * i, :], in0=lamv[:, 2 * i, :], in1=lamv[:, 2 * i + 1, :], scale=1.0,
                                                 scalar=0.0, op0=ALU.mult, op1=ALU.add, accum_out=lams[:, i:i + 1])
                ins.then_inc(lam_dot, 1)
                dve.wait_ge(x_ok, 2 * l + 1)
                q0 += Q_IN
                with dve.Fori(0, RUNS_IN) as i:
                    for s in range(SLOTS):
                        lo_block(i + (q0 + (s + 1) // SLOTS), (s + 1) % SLOTS)
                        multiplied(dve, i + q0, s)
                        V.tensor_copy(work[:, bass.ds(i * SLOTS + s, 1), COL:2 * COL], bank[2 * s + 1][:, :].unsqueeze(1))\
                            .then_inc(in_out1, 1)
                q0 += RUNS_IN
                lo_block(q0, 1)
                multiplied(dve, q0, 0)
                V.tensor_copy(blk(IN_BLOCKS - 1, 1), bank[1][:, :]).then_inc(in_out1, 1)
                dve.wait_ge(in_out0, SLOTS + IN_BLOCKS * (l + 1))
                dve.wait_ge(in_out1, SLOTS + IN_BLOCKS * (l + 1))
                then(V.tensor_tensor(work[:, B_GC, :], work[:, B_GC, :], work[:, B_U, :], ALU.mult))
                dve.sem_inc(gcu_ok, 1)
                dve.wait_ge(ld_small, 32)
                for b in (B_Q, B_Q + 1, B_K, B_K + 1):
                    rotate(b)
                dve.sem_inc(roped, 1)
                for c in range(KC):
                    dve.wait_ge(conv_t, KC * l + c + 1)
                    w = [vecT[:, V_CW + V_LAYER * l + 4 * i + c:V_CW + V_LAYER * l + 4 * i + c + 1] for i in range(3)]
                    bias = vecT[:, V_CB + V_LAYER * l + c:V_CB + V_LAYER * l + c + 1]
                    t = bank[c][:, :].rearrange("p (w g t) -> p w g t", w=2, g=G)
                    then(V.tensor_copy(pad[:, :, 1:T + 1], t[:, 1]))
                    then(V.tensor_scalar(cv[:, :, :], pad[:, :, 0:T], w[0], bias, ALU.mult, ALU.add))
                    then(V.scalar_tensor_tensor(out=cv[:, :, :], in0=pad[:, :, 1:T + 1], scalar=w[1], in1=cv[:, :, :],
                                                op0=ALU.mult, op1=ALU.add))
                    then(V.scalar_tensor_tensor(out=cv[:, :, :], in0=pad[:, :, 2:T + 2], scalar=w[2], in1=cv[:, :, :],
                                                op0=ALU.mult, op1=ALU.add))
                    V.tensor_tensor(conv_res(c), t[:, 0], cv[:, :, :], ALU.mult).then_inc(conv_f, 1)
                for c in range(KC):
                    dve.wait_ge(conv_hi, KC * l + c + 1)
                    V.tensor_tensor(xT_lo[:, c, :, :], conv_res(c), xT_hi[:, c, :, :].bitcast(F32), ALU.subtract)\
                        .then_inc(conv_ok, 1)
                lo_block(q0, 2)
                multiplied(dve, q0, 1)
                dve.wait_ge(sig_ok, 4 * (l + 1))
                for g in range(G):
                    for half in range(2):
                        ins = V.tensor_tensor(blk(B_GCONV + half, g), bank[4 + 2 * g + half][:, :], blk(B_GCONV + half, g), ALU.mult)
                then(ins)
                dve.sem_inc(conv_out, 1)
                dve.wait_ge(lam_exp, l + 1)
                then(V.tensor_tensor(lams[:, 4:5], lams[:, 3:4], lams[:, 2:3], ALU.subtract))
                then(V.tensor_scalar(lams[:, 4:5], lams[:, 4:5], -lam_init(l), None, ALU.add))
                for step in range(JOBS + 3):
                    j = step - 1
                    if 0 <= j < JOBS:
                        n, y = keys(j), j % 2
                        dve.wait_ge(j_s, JOBS * l + j + 1)
                        for i in range(2):
                            ins = V.tensor_reduce(mx[:, y, i:i + 1], s_bank(j, i)[:, 0:n], AX_X, ALU.max)
                        then(ins)
                        V.tensor_scalar(nmx[:, y, :], mx[:, y, :], -SCALE, None, ALU.mult).then_inc(j_max, 1)
                    j = step - 2
                    if 0 <= j < JOBS:
                        y = j % 2
                        dve.wait_ge(j_pT, JOBS * l + j + 1)
                        V.tensor_copy(pT_buf[:, y, 0:keys(j)], bank[4 + y][:, 0:keys(j)]).then_inc(j_pTc, 1)
                    j = step - 1
                    if 0 <= j < JOBS:
                        dve.wait_ge(j_exp, JOBS * l + j + 1)
                        y = j % 2
                        then(V.reciprocal(rsum[:, y, :], esum[:, y, :]))
                        then(V.tensor_tensor(rsum[:, y, 1:2], rsum[:, y, 1:2], lams[:, 4:5], ALU.mult))
                        n = keys(j)
                        then(V.tensor_scalar(p_buf[:, y, 0:n], e_buf[:, y, 0, 0:n], rsum[:, y, 0:1], None, ALU.mult))
                        V.scalar_tensor_tensor(out=p_buf[:, y, 0:n], in0=e_buf[:, y, 1, 0:n], scalar=rsum[:, y, 1:2],
                                               in1=p_buf[:, y, 0:n], op0=ALU.mult, op1=ALU.add).then_inc(j_p, 1)
                    j = step - 3
                    if 0 <= j < JOBS:
                        dve.wait_ge(j_o, JOBS * l + j + 1)
                        V.tensor_copy(head(B_Q, j), bank[4 + j % 2][:, 2 * T:2 * T + VD]).then_inc(j_oc, 1)
                dve.wait_ge(osd_ok, l + 1)
                dve.wait_ge(j_oc, JOBS * (l + 1))
                then(V.reciprocal(ors[:, :], osd[:, :]))
                for half in range(2):
                    o = work[:, B_Q + half, :].rearrange("p (j d) -> p j d", j=8)
                    V.tensor_tensor(o, o, ors[:, 8 * half:8 * half + 8].unsqueeze(2).to_broadcast([P, 8, VD]), ALU.mult)\
                        .then_inc(on_ok, 1)
                for i in range(4):
                    dve.wait_ge(oT_hi, 4 * l + i + 1)
                    at = (slice(None), slice(4 * (i // 2), 4 * (i // 2) + 4), i % 2, slice(None))
                    V.scalar_tensor_tensor(out=hT_lo[at], in0=four(bank[i]), scalar=sublng[:, l:l + 1],
                                           in1=hT_hi[at].bitcast(F32), op0=ALU.mult, op1=ALU.subtract).then_inc(oT_ok, 1)
                lo_block(q0 + 1, 0)
                lo_block(q0 + 1, 1)
                multiplied(dve, q0 + 1, 0)
                for g in range(G):
                    for half in range(2):
                        ins = V.tensor_tensor(blk(B_GATTN + half, g), bank[4 + 2 * g + half][:, :], blk(B_GATTN + half, g), ALU.mult)
                then(ins)
                for half in range(2):
                    V.tensor_tensor(work[:, B_GCONV + half, :], work[:, B_GCONV + half, :], work[:, B_GATTN + half, :], ALU.add)\
                        .then_inc(merged, 1)
                for i in range(4):
                    dve.wait_ge(m_hi, 4 * l + i + 1)
                    at = (slice(None), slice(4 * (i % 2), 4 * (i % 2) + 4), i // 2, slice(None))
                    V.tensor_tensor(xT_lo[at], four(bank[i]), xT_hi[at].bitcast(F32), ALU.subtract).then_inc(m_ok, 1)
                lo_block(q0 + 1, 2)
                q0 += 2
                lo_block(q0, 0, KINDS[0])
                residual(2 * l, q0 - 1)
                dve.wait_ge(kv_kept, 64 * (l + 1))
                layer_norm(2 * l + 1)
                modulate(2 * l + 1)
                if l == 0:
                    for e in range(DENSE_PARTS):
                        expert(q0 + e * Q_EXPERT, e, KINDS[0] if e + 1 < DENSE_PARTS else UNIT, lambda g: ones[:, 0:1])
                else:
                    route()
                    dve.wait_ge(gates_ok, 1)
                    with dve.Fori(0, NE - 1) as e:
                        expert(e * Q_EXPERT + q0, e + DENSE_PARTS, KINDS[0], lambda g: gates[:, g, bass.ds(e, 1)])
                    expert(q0 + (NE - 1) * Q_EXPERT, DENSE_PARTS + NE - 1, None, lambda g: gates[:, g, NE - 1:NE])
                residual(2 * l + 1, q0 + [DENSE_PARTS, NE][l] * Q_EXPERT - 1)
                layer_norm(2 * l + 2)

        @block.tensor
        def _(pe):
            def mm3(o, hi, lo, wh, wl, start, stop):
                pe.matmul(o, hi, wh, start=start, stop=False)
                pe.matmul(o, lo, wh, start=False, stop=False)
                return pe.matmul(o, hi, wl, start=False, stop=stop)

            def unit_ready(q, s, unit):
                pe.wait_ge(lo_done, q * (2 * SLOTS) + (2 * s + unit + 1))

            def part(w, unit, k, n):
                return w[:, unit, k * n:(k + 1) * n]

            def columns(q, s, unit, outs, n):
                unit_ready(q, s, unit)
                for k in range(4):
                    kk = 4 * unit + k
                    for g in range(G):
                        ins = mm3(outs[g], xT_hi[:, kk, g, :], xT_lo[:, kk, g, :], part(w_hi, unit, k, n),
                                  part(w_lo, unit, k, n), kk == 0, kk == KD - 1)
                return ins

            def rows(q, s, outs, lhs_hi, lhs_lo, k0, k1, start, stop):
                for unit in range(2):
                    unit_ready(q, s, unit)
                    for k in range(k0, k1):
                        for g in range(G):
                            ins = mm3(outs[2 * g + unit][:, :], lhs_hi[:, k, g, :], lhs_lo[:, k, g, :],
                                      part(w_hi, unit, k - k0, COL), part(w_lo, unit, k - k0, COL),
                                      start and k == k0, stop and k == k1 - 1)
                    ins.then_inc(parts_free, 1)
                    yield unit

            def row_block(*args):
                for _ in rows(*args):
                    pass

            def transpose_xhat(n):
                for g in range(G):
                    pe.wait_ge(xhat_ok, G * n + g + 1)
                    for k in range(KD):
                        ins = pe.transpose(bank[2 * g + k // 4][:, (k % 4) * T:(k % 4 + 1) * T],
                                           xhat[:, g, k * P:(k + 1) * P], ident[:, :])
                    ins.then_inc(xhat_t, 1)

            def gate_broadcast(n):
                for i in range(4):
                    pe.matmul(bank[i][:, :], sel[:, i // 2, :], gate_rows[:, n % 2, (i % 2) * COL:(i % 2 + 1) * COL],
                              start=True, stop=True).then_inc(bc_mm, 1)

            def expert(q, ec, start, stop):
                def transpose_h(c):
                    k0, k1 = HT[c]
                    pe.wait_ge(h_ok, ec * 4 + (c + 1))
                    for g in range(G):
                        for k in range(k0, k1):
                            ins = pe.transpose(bank[2 + g][:, (k - k0) * T:(k - k0 + 1) * T], h[:, g, k * P:(k + 1) * P],
                                               ident[:, :])
                    ins.then_inc(hT_t, 1)

                for j in range(8):
                    jq, js, c = q + j // SLOTS, j % SLOTS, j // 2
                    if j % 2 == 0:
                        if c:
                            pe.wait_ge(g_silu, ec * 4 + c)
                        outs = [bank[g][:, 0:FCOL] for g in range(G)]
                        columns(jq, js, 0, outs, FCOL).then_inc(parts_free, 1)
                        if c:
                            transpose_h(c - 1)
                        columns(jq, js, 1, outs, FCOL).then_inc(parts_free, 1)
                    else:
                        if c:
                            pe.wait_ge(hT_ok, ec * 4 + c)
                        outs = [bank[2 + g][:, 0:FCOL] for g in range(G)]
                        columns(jq, js, 0, outs, FCOL).then_inc(parts_free, 1)
                        columns(jq, js, 1, outs, FCOL).then_inc(parts_free, 1)
                for d, (k0, k1) in enumerate(DOWN):
                    if d == 2:
                        pe.wait_ge(hT_ok, ec * 4 + 4)
                    for unit in rows(q + (8 + d) // SLOTS, (8 + d) % SLOTS, bank[4:8], hT_hi, hT_lo, k0, k1,
                                     start and d == 0, stop and d == 3):
                        if d == 1 and unit == 0:
                            transpose_h(3)

            pe.sem_inc(parts_free, PARTS)
            pe.wait_ge(const_ok, 1)
            pe.wait_ge(ld_vec, 16 * N_VEC)
            pe.transpose(bank[7][:, 0:P], vec_rows[:, :], ident[:, :]).then_inc(vec_t, 1)
            pe.wait_ge(cond_ok, G)
            for l in range(DEPTH):
                q0 = turn0[l]
                if l:
                    pe.wait_ge(res_ok, 2 * l)
                with pe.Fori(0, Q_IN) as i:
                    for s in range(SLOTS):
                        pe.wait_ge(ada_out, i * SLOTS + (ADA_BLOCKS * l + s + 1))
                        for unit in range(2):
                            unit_ready(i + q0, s, unit)
                            for k in range(4):
                                for w in (w_hi, w_lo):
                                    ins = pe.matmul(bank[4 + s][0:66, :], cond_st[:, 4 * unit + k, :], part(w, unit, k, COL),
                                                    start=unit + k == 0 and w is w_hi, stop=unit * k == 3 and w is w_lo)
                            ins.then_inc(parts_free, 1)
                pe.wait_ge(ada_out, ADA_BLOCKS * (l + 1) + SLOTS)
                pe.wait_ge(ld_bias, 16 * (l + 1))
                pe.wait_ge(vec_ok, 1)
                for v, vec in enumerate((0, 1, 3, 4)):
                    for k in range(KD):
                        c0 = vec * D + k * P
                        ins = pe.matmul(bank[7][:, (v * KD + k) * G:(v * KD + k + 1) * G], ada_rows[:, c0:c0 + P],
                                        sel[:, :, 0], start=True, stop=True)
                ins.then_inc(ada_cols, 1)
                transpose_xhat(2 * l)
                pe.wait_ge(mod_ok, G * (2 * l + 1))
                q0 += Q_IN

                def in_block(q, s, j):
                    pe.wait_ge(in_out0, j)
                    pe.wait_ge(in_out1, j)
                    for unit in range(2):
                        columns(q, s, unit, [bank[2 * s][:, :], bank[2 * s + 1][:, :]], COL).then_inc(parts_free, 1)

                with pe.Fori(0, RUNS_IN) as i:
                    for s in range(SLOTS):
                        in_block(i + q0, s, i * SLOTS + (IN_BLOCKS * l + s + 1))
                q0 += RUNS_IN
                in_block(q0, 0, IN_BLOCKS * (l + 1))
                pe.wait_ge(in_out0, SLOTS + IN_BLOCKS * (l + 1))
                pe.wait_ge(in_out1, SLOTS + IN_BLOCKS * (l + 1))
                pe.wait_ge(gcu_ok, l + 1)
                for c in range(KC):
                    for i, b in enumerate((B_GB, B_GC)):
                        for g in range(G):
                            ins = pe.transpose(bank[c][:, (2 * i + g) * T:(2 * i + g + 1) * T],
                                               work[:, b, g * COL + c * P:g * COL + (c + 1) * P], ident[:, :])
                    ins.then_inc(conv_t, 1)
                pe.wait_ge(conv_ok, KC * (l + 1))
                row_block(q0, 1, bank[4:8], xT_hi, xT_lo, 0, 4, True, True)
                pe.wait_ge(conv_out, l + 1)
                pe.wait_ge(roped, l + 1)
                pe.wait_ge(ld_cache, 32 * (l + 1))
                for step in range(JOBS + 3):
                    j = step
                    if j < JOBS:
                        if j >= 2:
                            pe.wait_ge(j_qkT, JOBS * l + j - 1)
                        o = bank[2 + j % 2]
                        pe.transpose(o[:, 0:T], head(B_Q, j), ident[:, :])
                        ins = pe.transpose(o[:, T:2 * T], head(B_K, j), ident[:, :])
                        if keys(j) > T:
                            ins = pe.transpose(o[:, 2 * T:3 * T], cache[:, 0, head_of(j), :], ident[:, :])
                        ins.then_inc(j_qk, 1)
                    j = step - 1
                    if 0 <= j < JOBS:
                        n, y = keys(j), j % 2
                        pe.wait_ge(j_qkT, JOBS * l + j + 1)
                        if j >= 2:
                            pe.wait_ge(j_exp, JOBS * l + j - 1)
                        for i in range(2):
                            r = slice(HD * i, HD * (i + 1))
                            ins = pe.matmul(s_bank(j, i)[:, 0:n], qkT[r, y, 0:T], qkT[r, y, T:T + n], start=True, stop=True)
                        ins.then_inc(j_s, 1)
                    j = step - 2
                    if 0 <= j < JOBS:
                        y = j % 2
                        pe.wait_ge(j_p, JOBS * l + j + 1)
                        if j >= 2:
                            pe.wait_ge(j_oc, JOBS * l + j - 1)
                        for k in range(keys(j) // T):
                            ins = pe.transpose(bank[4 + y][:, k * T:(k + 1) * T], p_buf[:, y, k * T:(k + 1) * T], ident[:, :])
                        ins.then_inc(j_pT, 1)
                    j = step - 3
                    if 0 <= j < JOBS:
                        y = j % 2
                        pe.wait_ge(j_pTc, JOBS * l + j + 1)
                        vs = [head(B_V, j)] + [cache[:, 1, head_of(j), :]] * (keys(j) > T)
                        for k, v in enumerate(vs):
                            ins = pe.matmul(bank[4 + y][:, 2 * T:2 * T + VD], pT_buf[:, y, k * T:(k + 1) * T], v,
                                            start=k == 0, stop=k == len(vs) - 1)
                        ins.then_inc(j_o, 1)
                for i in range(4):
                    if i % 2 == 0:
                        pe.wait_ge(on_ok, 2 * l + i // 2 + 1)
                    for k in range(4):
                        ins = pe.transpose(bank[i][:, k * T:(k + 1) * T], head(B_Q, 4 * i + k), ident[:, :])
                    ins.then_inc(oT_t, 1)
                pe.wait_ge(oT_ok, 4 * (l + 1))
                row_block(q0, 2, bank[4:8], hT_hi, hT_lo, 0, 4, True, False)
                row_block(q0 + 1, 0, bank[4:8], hT_hi, hT_lo, 4, 8, False, True)
                pe.wait_ge(merged, 2 * (l + 1))
                for i in range(4):
                    for k in range(4):
                        ins = pe.transpose(bank[i][:, k * T:(k + 1) * T],
                                           work[:, B_GCONV + i % 2, (i // 2) * COL + k * P:(i // 2) * COL + (k + 1) * P], ident[:, :])
                    ins.then_inc(m_t, 1)
                pe.wait_ge(m_ok, 4 * (l + 1))
                pe.wait_ge(rows_ok, l + 1)
                gate_broadcast(2 * l)
                row_block(q0 + 1, 1, bank[4:8], xT_hi, xT_lo, 0, 4, True, False)
                row_block(q0 + 1, 2, bank[4:8], xT_hi, xT_lo, 4, 8, False, True)
                q0 += 2
                pe.wait_ge(bc_ok, 4 * (2 * l + 1))
                transpose_xhat(2 * l + 1)
                pe.wait_ge(mod_ok, G * (2 * l + 2))
                if l == 0:
                    for e in range(DENSE_PARTS):
                        expert(q0 + e * Q_EXPERT, e, e == 0, e == DENSE_PARTS - 1)
                else:
                    pe.wait_ge(r_parts, 2)
                    for g in range(G):
                        for k in range(KD):
                            ins = mm3(bank[2][:, g * NE:(g + 1) * NE], xT_hi[:, k, g, :], xT_lo[:, k, g, :], r_hi[:, k, :],
                                      r_lo[:, k, :], k == 0, k == KD - 1)
                    ins.then_inc(r_mm, 1)
                    pe.wait_ge(gates_ok, 1)
                    expert(q0, DENSE_PARTS, True, False)
                    with pe.Fori(1, NE - 1) as e:
                        expert(e * Q_EXPERT + q0, e + DENSE_PARTS, False, False)
                    expert(q0 + (NE - 1) * Q_EXPERT, DENSE_PARTS + NE - 1, False, True)
                gate_broadcast(2 * l + 1)


_INS = ["x_prompt", "x_sample", "cache_k", "cache_v", "c", "c_ctx", "ln_in_g", "ln_in_b", "ada_w", "ada_b", "w_in",
        "conv_w", "conv_b", "w_conv_out", "lam_q1", "lam_k1", "lam_q2", "lam_k2", "subln_g", "w_attn_out", "w_out",
        "ln1_g", "ln1_b", "ln2_g", "ln2_b", "ffn_w_gate", "ffn_w_up", "ffn_w_down", "moe_router", "moe_w_gate",
        "moe_w_up", "moe_w_down"]
_OUTS = [(1, T, D), (1, T, D), (1, DEPTH, HEADS, T, VD), (1, DEPTH, HEADS, T, VD)]


def rope_table():
    import numpy as np
    f = np.float32
    inv = (f(10000.0) ** (-np.arange(0, 32, 2, dtype=f) / f(32))).astype(f)
    row = np.repeat(np.arange(T // 64, dtype=f), 64)[:, None] * inv
    col = np.tile(np.arange(64, dtype=f), T // 64)[:, None] * inv
    ang = np.concatenate([row, col], axis=1).astype(np.float64)
    return np.stack([np.cos(ang), np.sin(ang)], axis=1).astype(f)


def kernel(**inputs):
    import numpy as np
    import concourse.bacc as bacc
    from concourse.bass_utils import run_bass_kernel_spmd as run

    nc = bacc.Bacc("TRN2", target_bir_lowering=False, num_devices=1)
    arrays, args = {}, {}
    for name, value in [(n, inputs[n]) for n in _INS] + [("rope", rope_table())]:
        v = np.ascontiguousarray(value)
        arrays[f"in_{name}"] = v
        args[name] = nc.dram_tensor(f"in_{name}", v.shape, mybir.dt.from_np(v.dtype), kind="ExternalInput").ap()
    outs = [nc.dram_tensor(f"out_{i}", s, F32, kind="ExternalOutput").ap() for i, s in enumerate(_OUTS)]
    program(nc, args, outs)
    r = run(nc, [arrays], core_ids=[0])
    return tuple(r.results[0][f"out_{i}"] for i in range(len(_OUTS)))
```

```python
import math
from contextlib import ExitStack

import concourse.bass as bass
from concourse import mybir

F32 = mybir.dt.float32
F32R = mybir.dt.float32r
ALU = mybir.AluOpType
ACT = mybir.ActivationFunctionType
AX_X = mybir.AxisListType.X

P = 128
D = 1024
KD = D // P
T = 128
G = 2
DEPTH = 2
D_CONV = 512
KC = D_CONV // P
HEADS = 8
HD = 64
VD = 2 * HD
FF = 1408
KF = FF // P
NE = 8
DENSE_PARTS = 2816 // FF
COL = 512
D_IN = 6656
IN_BLOCKS = D_IN // COL
ADA_BLOCKS = 6 * D // COL
FCOL = FF // 4
ALPHA = (2 * DEPTH) ** 0.25
EPS = 1e-5
SCALE = HD ** -0.5
SLOTS = 3
PARTS = 4
UNIT = 1024
DOWN = [(0, 3), (3, 6), (6, 9), (9, 11)]
HT = [(0, 2), (2, 5), (5, 8), (8, 11)]
JOBS = HEADS * G
PASSES = NE + 3
FAR = 4096.0
B_GB, B_GC, B_U, B_Q, B_K, B_V, B_GCONV, B_GATTN = 0, 1, 2, 3, 5, 7, 9, 11

V_C = 0
V_CW, V_CB, V_SG, V_LAYER = 16, 28, 32, 17
V_LN = V_CW + V_LAYER * DEPTH
V_ROWS = V_LN + 4 * 2 * KD
N_VEC = 2 + 5 * DEPTH + 8


def program(nc, a, out):
    with ExitStack() as ctx:
        def sb(name, shape, dt=F32):
            return ctx.enter_context(nc.sbuf_tensor(name, shape, dt))

        def sem(name):
            return ctx.enter_context(nc.semaphore(name))

        raw = sb("raw", [P, SLOTS, PARTS * UNIT])
        w_hi = sb("w_hi", [P, PARTS, UNIT], F32R)
        w_lo = sb("w_lo", [P, PARTS, UNIT], F32R)
        xT_hi = sb("xT_hi", [P, KD, G, T], F32R)
        xT_lo = sb("xT_lo", [P, KD, G, T], F32R)
        hT_hi = sb("hT_hi", [P, KF, G, T], F32R)
        hT_lo = sb("hT_lo", [P, KF, G, T], F32R)
        work = sb("work", [P, IN_BLOCKS, G * COL])
        x = sb("x", [P, G, D])
        cache = sb("cache", [P, 2, HEADS, VD])
        vecT = sb("vecT", [P, P])
        ident = sb("ident", [P, P])
        sel = sb("sel", [5, G, P])
        cond = sb("cond", [P, 2 * KD])
        cond_st = sb("cond_st", [P, KD, 66], F32R)
        adaT = sb("adaT", [P, DEPTH, 6, KD, G])
        modA = sb("modA", [P, 2, KD, G])
        modB = sb("modB", [P, 2, KD, G])
        rope = sb("rope", [P, 2, 32])
        lamv = sb("lamv", [P, 4, HD])
        lams = sb("lams", [P, 8])
        st = sb("st", [P, G, 2, 6])
        mv = sb("mv", [P, G, 2])
        sd = sb("sd", [P, G])
        rstd = sb("rstd", [P, G])
        mx = sb("mx", [P, 2, 2])
        nmx = sb("nmx", [P, 2, 2])
        esum = sb("esum", [P, 2, 2])
        rsum = sb("rsum", [P, 2, 2])
        sublng = sb("sublng", [P, DEPTH])
        osq = sb("osq", [P, JOBS])
        osd = sb("osd", [P, JOBS])
        ors = sb("ors", [P, JOBS])
        eps_c = sb("eps_c", [P, 1])
        ones = sb("ones", [P, 1])
        r_raw = sb("r_raw", [P, KD, NE])
        r_hi = sb("r_hi", [P, KD, NE], F32R)
        r_lo = sb("r_lo", [P, KD, NE], F32R)
        iota = sb("iota", [P, NE])
        rt = sb("rt", [P, 8, G, NE])
        rs = sb("rs", [P, 8, G])
        gates = sb("gates", [P, G, NE])
        one_hot = sb("one_hot", [P, G, NE])
        before = sb("before", [P, P])
        all_ones = sb("all_ones", [P, P])
        slot_no = sb("slot_no", [P, P])
        pos_tab = sb("pos_tab", [P, G, PASSES])
        gate_tab = sb("gate_tab", [P, G, PASSES])
        over = sb("over", [P, 4, NE])
        plan_f = sb("plan_f", [P, 8])
        plan = sb("plan", [P, 8], mybir.dt.int32)
        gate_col = sb("gate_col", [P, G])
        gate_slot = sb("gate_slot", [P, 1])
        pad = sb("pad", [P, G, T + 2])
        cv = sb("cv", [P, G, T])
        bank = [ctx.enter_context(nc.psum_tensor(f"bank{i}", [P, COL], F32)) for i in range(8)]

        flat = work[:, :, :].rearrange("p b n -> p (b n)")
        ada_rows = flat[0:5, 0:6 * D]
        xhat = flat[:, B_V * 1024:(B_V + 2) * 1024].rearrange("p (g d) -> p g d", g=G)
        modulated = flat[:, B_Q * 1024:(B_Q + 2) * 1024].rearrange("p (g k t) -> p g k t", g=G, k=KD)
        gate_bc = flat[:, B_K * 1024:(B_K + 2) * 1024].rearrange("p (g d) -> p g d", g=G)
        h = flat[:, B_GCONV * 1024:B_GCONV * 1024 + G * FF].rearrange("p (g f) -> p g f", g=G)
        tokens = gate_bc
        select = flat[:, 2048:2048 + G * T].rearrange("p (g s) -> p g s", g=G)
        y_hi, y_lo = (w[:, 0:KD, 1, :] for w in (hT_hi, hT_lo))
        selT = hT_hi[:, KD:KD + G, 1, :]
        att = flat[:, 0:2048]
        e_buf = att[:, 0:1024].rearrange("p (b s k) -> p b s k", b=2, s=2)
        p_buf = att[:, 1024:1536].rearrange("p (b k) -> p b k", b=2)
        pT_buf = att[:, 1536:2048].rearrange("p (b k) -> p b k", b=2)
        qkT = flat[:, 2048:2048 + 6 * T].rearrange("p (b k) -> p b k", b=2)
        vec_rows = flat[:, 12288:12288 + P]
        ln_gb = [flat[:, b * 1024:(b + 2) * 1024].rearrange("p (w d) -> p w d", w=2) for b in (B_GCONV, 0, B_GCONV, 0, B_GATTN)]
        rope_t = flat[:, 2048:3072]

        slot_i = flat[:, 12544:12544 + P].bitcast(mybir.dt.int32)

        def blk(b, g):
            return work[:, b, g * COL:(g + 1) * COL]

        def four(b):
            return b[:, :].rearrange("p (k t) -> p k t", t=T)

        def conv_res(c):
            return work[:, B_U, c * G * T:(c + 1) * G * T].rearrange("p (g t) -> p g t", g=G)

        def keys(j):
            return 2 * T if j % 8 >= 4 else T

        def s_bank(j, i):
            return bank[j % 2 + 6 * i]

        def head_of(j):
            return 4 * (j // 8) + j % 4

        def lam_init(l):
            return 0.8 - 0.6 * math.exp(-0.3 * l)

        def head(b0, j):
            return work[:, b0 + j // 8, (j % 8) * VD:(j % 8 + 1) * VD]

        raw_in = [[sem(f"raw_in{i}_{u}") for u in range(2)] for i in range(SLOTS)]
        hi_done = sem("hi_done")
        lo_done = sem("lo_done")
        parts_free = sem("parts_free")
        ada_out = sem("ada_out")
        in_out0 = sem("in_out0")
        in_out1 = sem("in_out1")
        ld_vec, ld_x, ld_small, ld_lam = sem("ld_vec"), sem("ld_x"), sem("ld_small"), sem("ld_lam")
        ld_bias, ld_cache, ld_ln = sem("ld_bias"), sem("ld_cache"), sem("ld_ln")
        stored, kv_kept = sem("stored"), sem("kv_kept")
        const_ok = sem("const_ok")
        pool_s, dve_s, act_s = sem("pool_s"), sem("dve_s"), sem("act_s")
        vec_t, vec_ok, silu_ok, cond_hi, cond_ok = (sem(n) for n in ("vec_t", "vec_ok", "silu_ok", "cond_hi", "cond_ok"))
        stats_ok, std_ok, xhat_ok, x_ok = (sem(n) for n in ("stats_ok", "std_ok", "xhat_ok", "x_ok"))
        ada_cols, coef_ok = sem("ada_cols"), sem("coef_ok")
        xhat_t, mod_act, mod_dve, mod_hi, mod_ok = (sem(n) for n in ("xhat_t", "mod_act", "mod_dve", "mod_hi", "mod_ok"))
        sig_ok, gcu_ok, conv_t, conv_f, conv_hi, conv_ok = (
            sem(n) for n in ("sig_ok", "gcu_ok", "conv_t", "conv_f", "conv_hi", "conv_ok"))
        conv_out = sem("conv_out")
        lam_dot, lam_exp, roped = sem("lam_dot"), sem("lam_exp"), sem("roped")
        j_qk, j_qkT, j_s, j_max, j_exp, j_p, j_pT, j_pTc, j_o, j_oc, j_sq = (
            sem(n) for n in ("j_qk", "j_qkT", "j_s", "j_max", "j_exp", "j_p", "j_pT", "j_pTc", "j_o", "j_oc", "j_sq"))
        osd_ok, on_ok, oT_t, oT_hi, oT_ok = (sem(n) for n in ("osd_ok", "on_ok", "oT_t", "oT_hi", "oT_ok"))
        merged, m_t, m_hi, m_ok = (sem(n) for n in ("merged", "m_t", "m_hi", "m_ok"))
        bc_mm, bc_ok, res_ok = (sem(n) for n in ("bc_mm", "bc_ok", "res_ok"))
        g_silu, h_ok, hT_t, hT_hi_ok, hT_ok = (sem(n) for n in ("g_silu", "h_ok", "hT_t", "hT_hi_ok", "hT_ok"))
        xt_t, xt_ok, mask_ok, pos_mm, plan_ok, sel_ok = (sem(n) for n in ("xt_t", "xt_ok", "mask_ok", "pos_mm", "plan_ok", "sel_ok"))
        gx_mm, gx_hi, gx_ok, st_t, st_ok, ge_ok = (sem(n) for n in ("gx_mm", "gx_hi", "gx_ok", "st_t", "st_ok", "ge_ok"))
        y_hi_ok, y_ok, y_zero, scattered = (sem(n) for n in ("y_hi_ok", "y_ok", "y_zero", "scattered"))
        r_parts, r_mm, r_max, r_exp = (sem(n) for n in ("r_parts", "r_mm", "r_max", "r_exp"))

        Q_IN = ADA_BLOCKS // SLOTS
        Q_PRE = Q_IN + (IN_BLOCKS + 5) // SLOTS
        Q_EXPERT = 12 // SLOTS
        turn0 = [0, Q_PRE + DENSE_PARTS * Q_EXPERT]
        FULL = (COL, 4)
        KINDS = [(FCOL, 4)] * 8 + [(COL, k1 - k0) for k0, k1 in DOWN]

        def cut(kind, unit):
            n, chunks = kind
            first = 2 if chunks > 2 else 1
            return (0, first * n) if unit % 2 == 0 else (first * n, (chunks - first) * n)

        RUNS_IN = IN_BLOCKS // SLOTS

        def t_bank(c):
            return bank[(1, 3, 1, 2)[c]]

        def multiplied(eng, q, s, unit=PARTS - 1):
            eng.wait_ge(parts_free, q * (PARTS * SLOTS) + (PARTS * s + unit + 1 + PARTS))

        block = ctx.enter_context(nc.Block())

        @block.sync
        def _(sp):
            def load(q, s, half, shape, src):
                if not isinstance(q, int) or q > 0:
                    sp.wait_ge(lo_done, (q - 1) * (PARTS * SLOTS) + (PARTS * s + 2 * half + 2))
                n = shape[0] * shape[1]
                dst = raw[:, s, 2 * half * UNIT:2 * half * UNIT + n].rearrange("p (k n) -> p k n", n=shape[1])
                sp.dma_start(dst, src).then_inc(raw_in[s][half], 16)

            def columns(q, s, w, c0, n):
                for half in range(2):
                    load(q, s, half, (4, n), w[half * 4 * P:(half + 1) * 4 * P, :]
                         .rearrange("(k p) n -> p k n", p=P)[:, :, bass.ds(c0, n)])

            def rows(q, s, w, k0, k1):
                for half in range(2):
                    load(q, s, half, (k1 - k0, COL), w[k0 * P:k1 * P, half * COL:(half + 1) * COL]
                         .rearrange("(k p) n -> p k n", p=P))

            def expert(q, wg, wu, wd):
                for c in range(4):
                    columns(q + 2 * c // SLOTS, 2 * c % SLOTS, wg, c * FCOL, FCOL)
                    columns(q + (2 * c + 1) // SLOTS, (2 * c + 1) % SLOTS, wu, c * FCOL, FCOL)
                for d, (k0, k1) in enumerate(DOWN):
                    rows(q + (8 + d) // SLOTS, (8 + d) % SLOTS, wd, k0, k1)

            for l in range(DEPTH):
                for w, q0, turns in ((a["ada_w"][l], turn0[l], Q_IN), (a["w_in"][l], turn0[l] + Q_IN, RUNS_IN)):
                    peel = int(q0 == 0)
                    for s in range(SLOTS * peel):
                        columns(0, s, w, s * COL, COL)
                    with sp.Fori(peel, turns) as i:
                        for s in range(SLOTS):
                            columns(i + q0, s, w, i * (SLOTS * COL) + s * COL, COL)
                q = turn0[l] + Q_IN + RUNS_IN
                columns(q, 0, a["w_in"][l], (IN_BLOCKS - 1) * COL, COL)
                rows(q, 1, a["w_conv_out"][l], 0, 4)
                rows(q, 2, a["w_attn_out"][l], 0, 4)
                rows(q + 1, 0, a["w_attn_out"][l], 4, 8)
                rows(q + 1, 1, a["w_out"][l], 0, 4)
                rows(q + 1, 2, a["w_out"][l], 4, 8)
                q += 2
                if l == 0:
                    for e in range(DENSE_PARTS):
                        expert(q + e * Q_EXPERT, a["ffn_w_gate"][0][:, e * FF:(e + 1) * FF],
                               a["ffn_w_up"][0][:, e * FF:(e + 1) * FF], a["ffn_w_down"][0][e * FF:(e + 1) * FF, :])
                else:
                    def one(p, e):
                        expert(p * Q_EXPERT + q, *(a[n][0, bass.ds(e, 1)].rearrange("e d f -> (e d) f")
                                                   for n in ("moe_w_gate", "moe_w_up", "moe_w_down")))

                    with sp.Fori(0, NE - 1) as p:
                        one(p, p)
                    sp.wait_ge(plan_ok, 1)
                    last_pass = sp.value_load(plan[0:1, 0:1], min_val=NE - 1, max_val=PASSES - 1)
                    with sp.Fori(NE - 1, last_pass + 1) as p:
                        one(p, sp.value_load(plan[0:1, bass.ds(p - (NE - 2), 1)], min_val=0, max_val=NE - 1))

        @block.gpsimd
        def _(pool):
            n_self = [0]

            def then(ins):
                n_self[0] += 1
                ins.then_inc(pool_s, 1)
                pool.wait_ge(pool_s, n_self[0])

            n_vec = 0

            def vec(row, src, n):
                pool.dma_start(vec_rows[row:row + n, :], src.rearrange("(n p) -> n p", p=P)).then_inc(ld_vec, 16)

            then(pool.memset(vec_rows[:, :], 0.0))
            vec(V_C, a["c_ctx"], KD)
            vec(V_C + KD, a["c"][0], KD)
            for l in range(DEPTH):
                r = l * V_LAYER
                for w in range(3):
                    vec(V_CW + r + 4 * w, a["conv_w"][l, w], KC)
                vec(V_CB + r, a["conv_b"][l], KC)
                vec(V_SG + r, a["subln_g"][l], 1)
            for n, (g, b) in enumerate(((a["ln_in_g"], a["ln_in_b"]), (a["ln1_g"][0], a["ln1_b"][0]),
                                        (a["ln2_g"][0], a["ln2_b"][0]), (a["ln1_g"][1], a["ln1_b"][1]))):
                vec(V_LN + n * 16, g, KD)
                vec(V_LN + n * 16 + KD, b, KD)
            pool.dma_start(x[:, 0, :], a["x_prompt"][0]).then_inc(ld_x, 16)
            pool.dma_start(x[:, 1, :], a["x_sample"][0]).then_inc(ld_x, 16)
            then(pool.memset(ident[:, :], 0.0))
            then(pool.affine_select(out=ident[:, :], in_=ident[:, :], compare_op=ALU.not_equal, fill=1.0, base=0,
                                    pattern=[[-1, P]], channel_multiplier=1))
            then(pool.memset(sel[:, :, :], 1.0))
            then(pool.affine_select(out=sel[:, 0, :], in_=sel[:, 0, :], compare_op=ALU.not_equal, fill=0.0,
                                    base=-2, pattern=[[0, P]], channel_multiplier=1))
            then(pool.affine_select(out=sel[:, 0, :], in_=sel[:, 0, :], compare_op=ALU.not_equal, fill=0.0,
                                    base=-3, pattern=[[0, P]], channel_multiplier=1))
            then(pool.affine_select(out=sel[:, 1, :], in_=sel[:, 1, :], compare_op=ALU.is_ge, fill=0.0,
                                    base=-2, pattern=[[0, P]], channel_multiplier=1))
            for v in range(NE):
                then(pool.memset(iota[:, v:v + 1], float(v - NE)))
            then(pool.memset(all_ones[:, :], 1.0))
            then(pool.affine_select(out=before[:, :], in_=all_ones[:, :], compare_op=ALU.is_gt, fill=0.0, base=0,
                                    pattern=[[1, P]], channel_multiplier=-1))
            then(pool.iota(slot_i, pattern=[[1, P]], base=0, channel_multiplier=0))
            then(pool.tensor_copy(slot_no[:, :], slot_i))
            then(pool.memset(eps_c[:, :], EPS))
            then(pool.memset(pad[:, :, :], 0.0))
            then(pool.memset(ones[:, :], 1.0))
            pool.sem_inc(const_ok, 1)
            pool.dma_start(rope[:, :, :], a["rope"]).then_inc(ld_small, 16)
            pool.dma_start(r_raw[:, :, :], a["moe_router"][0].rearrange("(k p) e -> p k e", p=P)).then_inc(ld_small, 16)

            def load_ln(n):
                g, b = [(a["ln_in_g"], a["ln_in_b"]), (a["ln1_g"][0], a["ln1_b"][0]), (a["ln2_g"][0], a["ln2_b"][0]),
                        (a["ln1_g"][1], a["ln1_b"][1]), (a["ln2_g"][1], a["ln2_b"][1])][n]
                pool.dma_start(ln_gb[n][:, 0, :], g.unsqueeze(0).to_broadcast([P, D])).then_inc(ld_ln, 16)
                pool.dma_start(ln_gb[n][:, 1, :], b.unsqueeze(0).to_broadcast([P, D])).then_inc(ld_ln, 16)

            def make_x(n):
                pool.wait_ge(ld_ln, 32 * (n + 1))
                for g in range(G):
                    pool.wait_ge(xhat_ok, G * n + g + 1)
                    then(pool.tensor_tensor(x[:, g, :], xhat[:, g, :], ln_gb[n][:, 0, :], ALU.mult))
                    then(pool.tensor_tensor(x[:, g, :], x[:, g, :], ln_gb[n][:, 1, :], ALU.add))
                pool.sem_inc(x_ok, 1)

            load_ln(0)
            for l in range(DEPTH):
                if l:
                    pool.wait_ge(lam_dot, l)
                for i, name in enumerate(("lam_q1", "lam_k1", "lam_q2", "lam_k2")):
                    pool.dma_start(lamv[:, i, :], a[name][l].unsqueeze(0).to_broadcast([P, HD])).then_inc(ld_lam, 16)
                if l:
                    pool.wait_ge(coef_ok, l)
                    pool.wait_ge(res_ok, 2 * l)
                pool.dma_start(ada_rows[4:5, :], a["ada_b"][l].unsqueeze(0)).then_inc(ld_bias, 16)
                if l:
                    pool.wait_ge(j_oc, JOBS * l)
                pool.dma_start(cache[:, 0], a["cache_k"][0, l].rearrange("h t d -> t h d")).then_inc(ld_cache, 16)
                pool.dma_start(cache[:, 1], a["cache_v"][0, l].rearrange("h t d -> t h d")).then_inc(ld_cache, 16)
                make_x(2 * l)
                pool.wait_ge(in_out0, SLOTS + IN_BLOCKS * l + B_V + 2)
                for i, (b0, o) in enumerate(((B_K, out[2]), (B_V, out[3]))):
                    for half in range(2):
                        pool.dma_start(o[0, l, 4 * half:4 * half + 4].rearrange("h t d -> t h d"),
                                       blk(b0 + half, 0).rearrange("p (h d) -> p h d", h=4)).then_inc(kv_kept, 16)
                pool.wait_ge(j_oc, JOBS * (l + 1))
                load_ln(2 * l + 1)
                make_x(2 * l + 1)
                if l == 0:
                    pool.wait_ge(hT_t, 4 * DENSE_PARTS)
                else:
                    pool.wait_ge(m_ok, 4 * DEPTH)
                load_ln(2 * l + 2)
            make_x(2 * DEPTH)
            pool.dma_start(out[0][0], x[:, 0, :]).then_inc(stored, 16)
            pool.dma_start(out[1][0], x[:, 1, :]).then_inc(stored, 16)
            pool.wait_ge(stored, 32)
            pool.wait_ge(kv_kept, 64 * DEPTH)

        @block.scalar
        def _(act):
            act_n = [0]

            def then(ins):
                act_n[0] += 1
                ins.then_inc(act_s, 1)
                act.wait_ge(act_s, act_n[0])

            def hi(q, s, units=range(PARTS), kind=FULL):
                for unit in units:
                    at, n = cut(kind, unit)
                    if unit % 2 == 0:
                        act.wait_ge(raw_in[s][unit // 2], q * 16 + 16)
                    act.wait_ge(parts_free, q * (PARTS * SLOTS) + (PARTS * s + unit + 1))
                    at += unit // 2 * 2 * UNIT
                    nc.scalar.activation(w_hi[:, unit, 0:n], raw[:, s, at:at + n], ACT.Copy).then_inc(hi_done, 1)

            def ln_std(n):
                for g in range(G):
                    act.wait_ge(stats_ok, G * n + g + 1)
                    nc.scalar.activation(sd[:, g:g + 1], mv[:, g, 1:2], ACT.Sqrt, bias=eps_c[:, 0:1]).then_inc(std_ok, 1)

            def modulate(n):
                for g in range(G):
                    act.wait_ge(xhat_t, G * n + g + 1)
                    for k in range(4):
                        ins = nc.scalar.activation(modulated[:, g, k, :], bank[2 * g][:, k * T:(k + 1) * T], ACT.Identity,
                                                   bias=modB[:, n % 2, k, g:g + 1], scale=modA[:, n % 2, k, g:g + 1])
                    ins.then_inc(mod_act, 1)
                for g in range(G):
                    act.wait_ge(mod_act, G * n + g + 1)
                    act.wait_ge(mod_dve, G * n + g + 1)
                    nc.scalar.activation(xT_hi[:, :, g, :], modulated[:, g, :, :], ACT.Copy).then_inc(mod_hi, 1)

            def gate_broadcast(n):
                for i in range(4):
                    act.wait_ge(bc_mm, 4 * n + i + 1)
                    nc.scalar.activation(gate_bc[:, i // 2, (i % 2) * COL:(i % 2 + 1) * COL], bank[i][:, :], ACT.Copy)\
                        .then_inc(bc_ok, 1)

            def expert(q, ec, behind):
                sizes = KINDS + [behind]
                for j in range(12):
                    nq, ns, n = q + (j + 1) // SLOTS, (j + 1) % SLOTS, sizes[j + 1]
                    if n:
                        hi(nq, ns, (0, 1), n)
                    if j in (2, 4, 6, 9):
                        c = (2, 4, 6, 9).index(j)
                        k0, k1 = HT[c]
                        act.wait_ge(hT_t, ec * 4 + (c + 1))
                        for g in range(G):
                            ins = nc.scalar.activation(hT_hi[:, k0:k1, g, :],
                                                       bank[2 + g][:, 0:(k1 - k0) * T].rearrange("p (k t) -> p k t", t=T),
                                                       ACT.Copy)
                        ins.then_inc(hT_hi_ok, 1)
                    if n:
                        hi(nq, ns, (2, 3), n)
                    if j < 8 and j % 2 == 0:
                        multiplied(act, q + j // SLOTS, j % SLOTS)
                        for g in range(G):
                            ins = nc.scalar.activation(h[:, g, j // 2 * FCOL:(j // 2 + 1) * FCOL], bank[g][:, 0:FCOL], ACT.Silu)
                        ins.then_inc(g_silu, 1)

            def gathered(p):
                for i in range(2):
                    act.wait_ge(gx_mm, p + 1)
                    nc.scalar.activation(xT_hi[:, 4 * i:4 * i + 4, 0, :], four(bank[2 * i]), ACT.Copy).then_inc(gx_hi, 1)

            def one_pass(q, p, last):
                kinds = KINDS + [KINDS[0]]
                for j in range(12):
                    nq, ns = q + (j + 1) // SLOTS, (j + 1) % SLOTS
                    ahead = j < 11 or not last
                    if ahead:
                        hi(nq, ns, (0, 1), kinds[j + 1])
                    if j in (2, 4, 6, 9):
                        c = (2, 4, 6, 9).index(j)
                        k0, k1 = HT[c]
                        act.wait_ge(hT_t, (p + DENSE_PARTS) * 4 + (c + 1))
                        nc.scalar.activation(hT_hi[:, k0:k1, 0, :], t_bank(c)[:, 0:(k1 - k0) * T].rearrange("p (k t) -> p k t", t=T),
                                             ACT.Copy).then_inc(hT_hi_ok, 1)
                    if j == 1:
                        act.wait_ge(st_t, p + 1)
                        nc.scalar.activation(selT, bank[3][:, 0:G * T].rearrange("p (g t) -> p g t", g=G), ACT.Copy)\
                            .then_inc(st_ok, 1)
                    if j == 10 and not last:
                        gathered(p + 1)
                    if j == 11:
                        multiplied(act, q + 3, 2, 1)
                        nc.scalar.activation(y_hi[:, 0:4], four(bank[1]), ACT.Copy).then_inc(y_hi_ok, 1)
                    if ahead:
                        hi(nq, ns, (2, 3), kinds[j + 1])
                    if j == 11:
                        multiplied(act, q + 3, 2)
                        nc.scalar.activation(y_hi[:, 4:8], four(bank[3]), ACT.Copy).then_inc(y_hi_ok, 1)
                    if j < 8 and j % 2 == 0:
                        multiplied(act, q + j // SLOTS, j % SLOTS)
                        nc.scalar.activation(h[:, 0, j // 2 * FCOL:(j // 2 + 1) * FCOL], bank[0][:, 0:FCOL], ACT.Silu)\
                            .then_inc(g_silu, 1)

            act.sem_inc(in_out0, SLOTS)
            act.wait_ge(const_ok, 1)
            act.wait_ge(vec_ok, 1)
            nc.scalar.activation(cond[:, :], vecT[:, V_C:V_C + 2 * KD], ACT.Silu).then_inc(silu_ok, 1)
            act.wait_ge(silu_ok, 1)
            act.wait_ge(cond_hi, 1)
            for g in range(G):
                nc.scalar.activation(cond_st[:, :, 2 * g:2 * g + 1], cond[:, g * KD:(g + 1) * KD].unsqueeze(2), ACT.Copy)\
                    .then_inc(cond_hi, 1)
            act.wait_ge(ld_small, 32)
            nc.scalar.activation(r_hi[:, :, :], r_raw[:, :, :], ACT.Copy).then_inc(r_parts, 1)
            ln_std(0)
            hi(0, 0)
            for l in range(DEPTH):
                q0 = turn0[l]
                with act.Fori(0, Q_IN) as i:
                    for s in range(SLOTS):
                        hi(i + (q0 + (s + 1) // SLOTS), (s + 1) % SLOTS)
                act.wait_ge(coef_ok, l + 1)
                modulate(2 * l)
                act.wait_ge(x_ok, 2 * l + 1)
                q0 += Q_IN
                with act.Fori(0, RUNS_IN) as i:
                    for s in range(SLOTS):
                        hi(i + (q0 + (s + 1) // SLOTS), (s + 1) % SLOTS)
                        multiplied(act, i + q0, s)
                        nc.scalar.activation(work[:, bass.ds(i * SLOTS + s, 1), 0:COL], bank[2 * s][:, :].unsqueeze(1),
                                             ACT.Copy).then_inc(in_out0, 1)
                q0 += RUNS_IN
                hi(q0, 1)
                multiplied(act, q0, 0)
                nc.scalar.activation(blk(IN_BLOCKS - 1, 0), bank[0][:, :], ACT.Copy).then_inc(in_out0, 1)
                act.wait_ge(in_out0, SLOTS + IN_BLOCKS * (l + 1))
                act.wait_ge(in_out1, SLOTS + IN_BLOCKS * (l + 1))
                for b in range(B_GCONV, IN_BLOCKS):
                    nc.scalar.activation(work[:, b, :], work[:, b, :], ACT.Sigmoid).then_inc(sig_ok, 1)
                for c in range(KC):
                    act.wait_ge(conv_f, KC * l + c + 1)
                    nc.scalar.activation(xT_hi[:, c, :, :], conv_res(c), ACT.Copy).then_inc(conv_hi, 1)
                hi(q0, 2)
                act.wait_ge(lam_dot, l + 1)
                nc.scalar.activation(lams[:, 2:4], lams[:, 0:2], ACT.Exp).then_inc(lam_exp, 1)
                for step in range(JOBS + 3):
                    j = step
                    if j < JOBS:
                        n = keys(j) + T
                        act.wait_ge(j_qk, JOBS * l + j + 1)
                        if j >= 2:
                            act.wait_ge(j_s, JOBS * l + j - 1)
                        nc.scalar.activation(qkT[:, j % 2, 0:n], bank[2 + j % 2][:, 0:n], ACT.Copy).then_inc(j_qkT, 1)
                    j = step - 1
                    if 0 <= j < JOBS:
                        n = keys(j)
                        act.wait_ge(j_max, JOBS * l + j + 1)
                        if j >= 2:
                            act.wait_ge(j_p, JOBS * l + j - 1)
                        for i in range(2):
                            ins = nc.scalar.activation(e_buf[:, j % 2, i, 0:n], s_bank(j, i)[:, 0:n], ACT.Exp,
                                                       bias=nmx[:, j % 2, i:i + 1], scale=SCALE,
                                                       accum_out=esum[:, j % 2, i:i + 1])
                        ins.then_inc(j_exp, 1)
                    j = step - 3
                    if 0 <= j < JOBS:
                        act.wait_ge(j_oc, JOBS * l + j + 1)
                        if JOBS * l + j:
                            act.wait_ge(j_sq, JOBS * l + j)
                        nc.scalar.activation(cv[:, 0, :], head(B_Q, j), ACT.Square, accum_out=osq[:, j:j + 1]).then_inc(j_sq, 1)
                act.wait_ge(j_sq, JOBS * (l + 1))
                nc.scalar.activation(osd[:, :], osq[:, :], ACT.Sqrt, bias=eps_c[:, 0:1], scale=1.0 / VD).then_inc(osd_ok, 1)
                for i in range(4):
                    act.wait_ge(oT_t, 4 * l + i + 1)
                    nc.scalar.activation(hT_hi[:, 4 * (i // 2):4 * (i // 2) + 4, i % 2, :], four(bank[i]), ACT.Copy,
                                         scale=sublng[:, l:l + 1]).then_inc(oT_hi, 1)
                hi(q0 + 1, 0)
                hi(q0 + 1, 1)
                for i in range(4):
                    act.wait_ge(m_t, 4 * l + i + 1)
                    nc.scalar.activation(xT_hi[:, 4 * (i % 2):4 * (i % 2) + 4, i // 2, :], four(bank[i]), ACT.Copy)\
                        .then_inc(m_hi, 1)
                act.wait_ge(kv_kept, 64 * (l + 1))
                gate_broadcast(2 * l)
                hi(q0 + 1, 2)
                q0 += 2
                hi(q0, 0, kind=KINDS[0])
                ln_std(2 * l + 1)
                modulate(2 * l + 1)
                if l == 0:
                    for e in range(DENSE_PARTS):
                        expert(q0 + e * Q_EXPERT, e, KINDS[0] if e + 1 < DENSE_PARTS else FULL)
                else:
                    act.wait_ge(r_max, 1)
                    for g in range(G):
                        ins = nc.scalar.activation(rt[:, 1, g, :], rt[:, 0, g, :], ACT.Exp, bias=rs[:, 0, g:g + 1],
                                                   accum_out=rs[:, 1, g:g + 1])
                    ins.then_inc(r_exp, 1)
                    for i in range(2):
                        act.wait_ge(xt_t, i + 1)
                        nc.scalar.activation(tokens[:, 0, i * COL:(i + 1) * COL], bank[4 + i][:, :], ACT.Copy).then_inc(xt_ok, 1)
                    act.wait_ge(plan_ok, 1)
                    last_pass = act.value_load(plan[0:1, 0:1], min_val=NE - 1, max_val=PASSES - 1)
                    gathered(0)
                    with act.Fori(0, last_pass) as p:
                        one_pass(p * Q_EXPERT + q0, p, False)
                    one_pass(last_pass * Q_EXPERT + q0, last_pass, True)
                gate_broadcast(2 * l + 1)
                ln_std(2 * l + 2)

        @block.vector
        def _(dve):
            dve_n = [0]
            V = nc.vector

            def then(ins):
                dve_n[0] += 1
                ins.then_inc(dve_s, 1)
                dve.wait_ge(dve_s, dve_n[0])

            def lo(q, s, units=range(PARTS), kind=FULL):
                for unit in units:
                    at, n = cut(kind, unit)
                    dve.wait_ge(hi_done, q * (PARTS * SLOTS) + (PARTS * s + unit + 1))
                    at += unit // 2 * 2 * UNIT
                    V.tensor_tensor(w_lo[:, unit, 0:n], raw[:, s, at:at + n], w_hi[:, unit, 0:n].bitcast(F32),
                                    ALU.subtract).then_inc(lo_done, 1)

            def layer_norm(n):
                for g in range(G):
                    for half in range(2):
                        ins = V.bn_stats(st[:, g, half, :], x[:, g, half * COL:(half + 1) * COL])
                    then(ins)
                    V.bn_aggr(mv[:, g, :], st[:, g, :, :].rearrange("p a b -> p (a b)")).then_inc(stats_ok, 1)
                for g in range(G):
                    dve.wait_ge(std_ok, G * n + g + 1)
                    then(V.reciprocal(rstd[:, g:g + 1], sd[:, g:g + 1]))
                    V.tensor_scalar(xhat[:, g, :], x[:, g, :], mv[:, g, 0:1], rstd[:, g:g + 1], ALU.subtract, ALU.mult)\
                        .then_inc(xhat_ok, 1)

            def modulate(n):
                for g in range(G):
                    dve.wait_ge(xhat_t, G * n + g + 1)
                    for k in range(4, KD):
                        ins = V.tensor_scalar(modulated[:, g, k, :], bank[2 * g + 1][:, (k - 4) * T:(k - 3) * T],
                                              modA[:, n % 2, k, g:g + 1], modB[:, n % 2, k, g:g + 1], ALU.mult, ALU.add)
                    ins.then_inc(mod_dve, 1)
                for g in range(G):
                    dve.wait_ge(mod_hi, G * n + g + 1)
                    V.tensor_tensor(xT_lo[:, :, g, :], modulated[:, g, :, :], xT_hi[:, :, g, :].bitcast(F32), ALU.subtract)\
                        .then_inc(mod_ok, 1)

            def residual(n):
                dve.wait_ge(bc_ok, 4 * (n + 1))
                dve.wait_ge(x_ok, n + 1)
                for g in range(G):
                    for half in range(2):
                        bc = gate_bc[:, g, half * COL:(half + 1) * COL]
                        ins = V.tensor_tensor(bc, bank[4 + 2 * g + half][:, :], bc, ALU.mult)
                then(ins)
                for g in range(G):
                    ins = V.scalar_tensor_tensor(out=x[:, g, :], in0=x[:, g, :], scalar=ALPHA, in1=gate_bc[:, g, :],
                                                 op0=ALU.mult, op1=ALU.add)
                then(ins)
                dve.sem_inc(res_ok, 1)

            def expert(q, ec, behind):
                sizes = KINDS + [behind]
                for j in range(12):
                    nq, ns, n = q + (j + 1) // SLOTS, (j + 1) % SLOTS, sizes[j + 1]
                    if n:
                        lo(nq, ns, (0, 1), n)
                    if j in (2, 4, 6, 9):
                        c = (2, 4, 6, 9).index(j)
                        k0, k1 = HT[c]
                        dve.wait_ge(hT_hi_ok, ec * 4 + (c + 1))
                        for g in range(G):
                            ins = V.tensor_tensor(hT_lo[:, k0:k1, g, :],
                                                  bank[2 + g][:, 0:(k1 - k0) * T].rearrange("p (k t) -> p k t", t=T),
                                                  hT_hi[:, k0:k1, g, :].bitcast(F32), ALU.subtract)
                        ins.then_inc(hT_ok, 1)
                    if n:
                        lo(nq, ns, (2, 3), n)
                    if j < 8 and j % 2 == 1:
                        c = j // 2
                        multiplied(dve, q + j // SLOTS, j % SLOTS)
                        dve.wait_ge(g_silu, ec * 4 + (c + 1))
                        for g in range(G):
                            hc = h[:, g, c * FCOL:(c + 1) * FCOL]
                            ins = V.tensor_tensor(hc, hc, bank[2 + g][:, 0:FCOL], ALU.mult)
                        ins.then_inc(h_ok, 1)

            def route():
                E = lambda i: rt[:, i, :, :]
                B = lambda i: rs[:, i, :].unsqueeze(2).to_broadcast([P, G, NE])
                dve.wait_ge(r_mm, 1)
                then(V.tensor_copy(E(0), bank[2][:, 0:G * NE].rearrange("p (g e) -> p g e", g=G)))
                then(V.tensor_reduce(rs[:, 0, :], E(0), AX_X, ALU.max, negate=True))
                dve.sem_inc(r_max, 1)
                dve.wait_ge(r_exp, 1)
                then(V.reciprocal(rs[:, 2, :], rs[:, 1, :]))
                then(V.tensor_tensor(E(1), E(1), B(2), ALU.mult))
                far = iota[:, :].unsqueeze(1).to_broadcast([P, G, NE])
                for i, best in ((0, 3), (1, 4)):
                    then(V.tensor_reduce(rs[:, best, :], E(1), AX_X, ALU.max))
                    then(V.tensor_tensor(E(2), E(1), B(best), ALU.is_equal))
                    then(V.tensor_tensor(E(3), E(2), far, ALU.mult))
                    then(V.tensor_reduce(rs[:, 5, :], E(3), AX_X, ALU.min))
                    then(V.tensor_tensor(E(4 + i), far, B(5), ALU.is_equal))
                    if i == 1:
                        then(V.tensor_tensor(one_hot[:, :, :], E(4), E(5), ALU.add))
                        dve.sem_inc(mask_ok, 1)
                    if i == 0:
                        then(V.scalar_tensor_tensor(out=E(1), in0=E(4), scalar=-2.0, in1=E(1), op0=ALU.mult, op1=ALU.add))
                then(V.tensor_tensor(rs[:, 6, :], rs[:, 3, :], rs[:, 4, :], ALU.add))
                then(V.reciprocal(rs[:, 7, :], rs[:, 6, :]))
                for i in (0, 1):
                    then(V.tensor_tensor(rs[:, 3 + i, :], rs[:, 3 + i, :], rs[:, 7, :], ALU.mult))
                    then(V.tensor_tensor(E(4 + i), E(4 + i), B(3 + i), ALU.mult))
                then(V.tensor_tensor(gates[:, :, :], E(4), E(5), ALU.add))

            def make_plan():
                posm = pos_tab[:, :, 0:NE]
                then(V.tensor_scalar(posm, one_hot[:, :, :], FAR, -FAR, ALU.mult, ALU.add))
                V.tensor_copy(gate_tab[:, :, 0:NE], gates[:, :, :])
                dve.wait_ge(pos_mm, 1)
                then(V.tensor_tensor(posm, posm, bank[2][:, 64:64 + G * NE].rearrange("p (g e) -> p g e", g=G), ALU.add))
                ov, rank, chosen, junk = (over[:, i, :] for i in range(4))
                V.tensor_scalar(ov, bank[2][:, 64 + G * NE:64 + (G + 1) * NE], float(T), None, ALU.is_gt)
                then(V.memset(rank[:, 0:1], 0.0))
                for e in range(1, NE):
                    then(V.tensor_tensor(rank[:, e:e + 1], rank[:, e - 1:e], ov[:, e - 1:e], ALU.add))
                V.memset(plan_f[:, 1:2], float(NE - 1))
                V.memset(plan_f[:, 5:8], 0.0)
                V.scalar_tensor_tensor(out=plan_f[:, 0:1], in0=rank[:, NE - 1:NE], scalar=float(NE - 1), in1=ov[:, NE - 1:NE],
                                       op0=ALU.add, op1=ALU.add)
                for i in range(PASSES - NE):
                    then(V.scalar_tensor_tensor(out=chosen, in0=rank, scalar=float(i), in1=ov, op0=ALU.is_equal, op1=ALU.mult))
                    sums = [(iota[:, :], float(NE), plan_f[:, 2 + i:3 + i])]
                    for g in range(G):
                        sums.append((pos_tab[:, g, 0:NE], -float(T), pos_tab[:, g, NE + i:NE + i + 1]))
                        sums.append((gate_tab[:, g, 0:NE], 0.0, gate_tab[:, g, NE + i:NE + i + 1]))
                    for v, start, to in sums:
                        then(V.tensor_tensor_reduce(out=junk, in0=chosen, in1=v, scale=1.0, scalar=start, op0=ALU.mult,
                                                    op1=ALU.add, accum_out=to))
                then(V.tensor_copy(plan[:, :], plan_f[:, :]))
                dve.sem_inc(plan_ok, 1)

            def selection(p):
                at = bass.ds(p, 1)
                V.tensor_copy(gate_col[:, :].unsqueeze(2), gate_tab[:, :, at])
                for g in range(G):
                    ins = V.tensor_scalar(select[:, g, :], slot_no[:, :], pos_tab[:, g, at], None, ALU.is_equal)
                ins.then_inc(sel_ok, 1)

            def gathered(p):
                for i in range(2):
                    dve.wait_ge(gx_hi, p * 2 + (i + 1))
                    V.tensor_tensor(xT_lo[:, 4 * i:4 * i + 4, 0, :], four(bank[2 * i]),
                                    xT_hi[:, 4 * i:4 * i + 4, 0, :].bitcast(F32), ALU.subtract).then_inc(gx_ok, 1)

            def one_pass(q, p, last):
                kinds = KINDS + [KINDS[0]]
                for j in range(12):
                    nq, ns = q + (j + 1) // SLOTS, (j + 1) % SLOTS
                    ahead = j < 11 or not last
                    if ahead:
                        lo(nq, ns, (0, 1), kinds[j + 1])
                    if j in (2, 4, 6, 9):
                        c = (2, 4, 6, 9).index(j)
                        k0, k1 = HT[c]
                        dve.wait_ge(hT_hi_ok, (p + DENSE_PARTS) * 4 + (c + 1))
                        V.tensor_tensor(hT_lo[:, k0:k1, 0, :], t_bank(c)[:, 0:(k1 - k0) * T].rearrange("p (k t) -> p k t", t=T),
                                        hT_hi[:, k0:k1, 0, :].bitcast(F32), ALU.subtract).then_inc(hT_ok, 1)
                    if j == 1:
                        dve.wait_ge(st_ok, p + 1)
                        V.tensor_copy(gate_slot[:, :], bank[3][:, G * T:G * T + 1]).then_inc(ge_ok, 1)
                    if j == 8 and not last:
                        selection(p + 1)
                    if j == 10 and not last:
                        gathered(p + 1)
                    if j == 11:
                        dve.wait_ge(y_hi_ok, p * 2 + 1)
                        V.tensor_tensor(y_lo[:, 0:4], four(bank[1]), y_hi[:, 0:4].bitcast(F32), ALU.subtract).then_inc(y_ok, 1)
                    if ahead:
                        lo(nq, ns, (2, 3), kinds[j + 1])
                    if j == 11:
                        dve.wait_ge(y_hi_ok, p * 2 + 2)
                        V.tensor_tensor(y_lo[:, 4:8], four(bank[3]), y_hi[:, 4:8].bitcast(F32), ALU.subtract).then_inc(y_ok, 1)
                    if j < 8 and j % 2 == 1:
                        c = j // 2
                        multiplied(dve, q + j // SLOTS, j % SLOTS)
                        dve.wait_ge(g_silu, (p + DENSE_PARTS) * 4 + (c + 1))
                        dve.wait_ge(ge_ok, p + 1)
                        hc = h[:, 0, c * FCOL:(c + 1) * FCOL]
                        V.scalar_tensor_tensor(out=hc, in0=hc, scalar=gate_slot[:, 0:1], in1=bank[2][:, 0:FCOL],
                                               op0=ALU.mult, op1=ALU.mult).then_inc(h_ok, 1)

            def rotate(b):
                v = blk(b, 1).rearrange("p (m c h i) -> p m c h i", c=2, h=2, i=16)
                x1, x2 = v[:, :, :, 0, :], v[:, :, :, 1, :]
                t4 = [rope_t[:, i * 256:(i + 1) * 256].rearrange("p (m c i) -> p m c i", c=2, i=16) for i in range(4)]
                cos = rope[:, 0, :].rearrange("p (c i) -> p c i", c=2).unsqueeze(1).to_broadcast([P, 8, 2, 16])
                sin = rope[:, 1, :].rearrange("p (c i) -> p c i", c=2).unsqueeze(1).to_broadcast([P, 8, 2, 16])
                V.tensor_tensor(t4[0], x1, cos, ALU.mult)
                V.tensor_tensor(t4[1], x2, sin, ALU.mult)
                V.tensor_tensor(t4[2], x1, sin, ALU.mult)
                then(V.tensor_tensor(t4[3], x2, cos, ALU.mult))
                V.tensor_tensor(x1, t4[0], t4[1], ALU.subtract)
                then(V.tensor_tensor(x2, t4[2], t4[3], ALU.add))

            dve.sem_inc(ada_out, SLOTS)
            dve.sem_inc(in_out1, SLOTS)
            V.memset(cond_st[:, :, :].bitcast(F32), 0.0).then_inc(cond_hi, 1)
            dve.wait_ge(vec_t, 1)
            V.tensor_copy(vecT[:, :], bank[7][:, 0:P]).then_inc(vec_ok, 1)
            dve.wait_ge(ld_x, 32)
            layer_norm(0)
            dve.wait_ge(cond_hi, 1 + G)
            for g in range(G):
                V.tensor_tensor(cond_st[:, :, 2 * g + 1:2 * g + 2], cond[:, g * KD:(g + 1) * KD].unsqueeze(2),
                                cond_st[:, :, 2 * g:2 * g + 1].bitcast(F32), ALU.subtract).then_inc(cond_ok, 1)
            dve.wait_ge(r_parts, 1)
            V.tensor_tensor(r_lo[:, :, :], r_raw[:, :, :], r_hi[:, :, :].bitcast(F32), ALU.subtract).then_inc(r_parts, 1)
            dve.wait_ge(const_ok, 1)
            dve.wait_ge(vec_ok, 1)
            for l in range(DEPTH):
                then(V.tensor_scalar(sublng[:, l:l + 1], vecT[:, V_SG + V_LAYER * l:V_SG + V_LAYER * l + 1],
                                     1.0 - lam_init(l), None, ALU.mult))
            lo(0, 0)
            for l in range(DEPTH):
                q0 = turn0[l]
                with dve.Fori(0, Q_IN) as i:
                    for s in range(SLOTS):
                        lo(i + (q0 + (s + 1) // SLOTS), (s + 1) % SLOTS)
                        multiplied(dve, i + q0, s)
                        V.tensor_copy(ada_rows[0:4, bass.ds(i * (SLOTS * COL) + s * COL, COL)], bank[4 + s][0:4, :])\
                            .then_inc(ada_out, 1)
                dve.wait_ge(ada_cols, l + 1)
                then(V.tensor_copy(adaT[:, l].rearrange("p v k g -> p (v k g)"), bank[7][:, 0:6 * KD * G]))
                for i in range(2):
                    ln = V_LN + (2 * l + i) * 2 * KD
                    ln_g = vecT[:, ln:ln + KD].unsqueeze(2).to_broadcast([P, KD, G])
                    ln_b = vecT[:, ln + KD:ln + 2 * KD].unsqueeze(2).to_broadcast([P, KD, G])
                    V.scalar_tensor_tensor(out=modA[:, i], in0=adaT[:, l, 3 * i + 1], scalar=1.0, in1=ln_g, op0=ALU.add, op1=ALU.mult)
                    then(V.scalar_tensor_tensor(out=modB[:, i], in0=adaT[:, l, 3 * i + 1], scalar=1.0, in1=ln_b, op0=ALU.add,
                                                op1=ALU.mult))
                    then(V.tensor_tensor(modB[:, i], modB[:, i], adaT[:, l, 3 * i], ALU.add))
                dve.sem_inc(coef_ok, 1)
                modulate(2 * l)
                dve.wait_ge(ld_lam, 64 * (l + 1))
                for i in range(2):
                    ins = V.tensor_tensor_reduce(out=lamv[:, 2 * i, :], in0=lamv[:, 2 * i, :], in1=lamv[:, 2 * i + 1, :], scale=1.0,
                                                 scalar=0.0, op0=ALU.mult, op1=ALU.add, accum_out=lams[:, i:i + 1])
                ins.then_inc(lam_dot, 1)
                dve.wait_ge(x_ok, 2 * l + 1)
                q0 += Q_IN
                with dve.Fori(0, RUNS_IN) as i:
                    for s in range(SLOTS):
                        lo(i + (q0 + (s + 1) // SLOTS), (s + 1) % SLOTS)
                        multiplied(dve, i + q0, s)
                        V.tensor_copy(work[:, bass.ds(i * SLOTS + s, 1), COL:2 * COL], bank[2 * s + 1][:, :].unsqueeze(1))\
                            .then_inc(in_out1, 1)
                q0 += RUNS_IN
                lo(q0, 1)
                multiplied(dve, q0, 0)
                V.tensor_copy(blk(IN_BLOCKS - 1, 1), bank[1][:, :]).then_inc(in_out1, 1)
                dve.wait_ge(in_out0, SLOTS + IN_BLOCKS * (l + 1))
                dve.wait_ge(in_out1, SLOTS + IN_BLOCKS * (l + 1))
                then(V.tensor_tensor(work[:, B_GC, :], work[:, B_GC, :], work[:, B_U, :], ALU.mult))
                dve.sem_inc(gcu_ok, 1)
                dve.wait_ge(ld_small, 32)
                for b in (B_Q, B_Q + 1, B_K, B_K + 1):
                    rotate(b)
                dve.sem_inc(roped, 1)
                for c in range(KC):
                    dve.wait_ge(conv_t, KC * l + c + 1)
                    w = [vecT[:, V_CW + V_LAYER * l + 4 * i + c:V_CW + V_LAYER * l + 4 * i + c + 1] for i in range(3)]
                    bias = vecT[:, V_CB + V_LAYER * l + c:V_CB + V_LAYER * l + c + 1]
                    t = bank[c][:, :].rearrange("p (w g t) -> p w g t", w=2, g=G)
                    then(V.tensor_copy(pad[:, :, 1:T + 1], t[:, 1]))
                    then(V.tensor_scalar(cv[:, :, :], pad[:, :, 0:T], w[0], bias, ALU.mult, ALU.add))
                    then(V.scalar_tensor_tensor(out=cv[:, :, :], in0=pad[:, :, 1:T + 1], scalar=w[1], in1=cv[:, :, :],
                                                op0=ALU.mult, op1=ALU.add))
                    then(V.scalar_tensor_tensor(out=cv[:, :, :], in0=pad[:, :, 2:T + 2], scalar=w[2], in1=cv[:, :, :],
                                                op0=ALU.mult, op1=ALU.add))
                    V.tensor_tensor(conv_res(c), t[:, 0], cv[:, :, :], ALU.mult).then_inc(conv_f, 1)
                for c in range(KC):
                    dve.wait_ge(conv_hi, KC * l + c + 1)
                    V.tensor_tensor(xT_lo[:, c, :, :], conv_res(c), xT_hi[:, c, :, :].bitcast(F32), ALU.subtract)\
                        .then_inc(conv_ok, 1)
                lo(q0, 2)
                multiplied(dve, q0, 1)
                dve.wait_ge(sig_ok, 4 * (l + 1))
                for g in range(G):
                    for half in range(2):
                        ins = V.tensor_tensor(blk(B_GCONV + half, g), bank[4 + 2 * g + half][:, :], blk(B_GCONV + half, g), ALU.mult)
                then(ins)
                dve.sem_inc(conv_out, 1)
                dve.wait_ge(lam_exp, l + 1)
                then(V.tensor_tensor(lams[:, 4:5], lams[:, 3:4], lams[:, 2:3], ALU.subtract))
                then(V.tensor_scalar(lams[:, 4:5], lams[:, 4:5], -lam_init(l), None, ALU.add))
                for step in range(JOBS + 3):
                    j = step - 1
                    if 0 <= j < JOBS:
                        n, y = keys(j), j % 2
                        dve.wait_ge(j_s, JOBS * l + j + 1)
                        for i in range(2):
                            ins = V.tensor_reduce(mx[:, y, i:i + 1], s_bank(j, i)[:, 0:n], AX_X, ALU.max)
                        then(ins)
                        V.tensor_scalar(nmx[:, y, :], mx[:, y, :], -SCALE, None, ALU.mult).then_inc(j_max, 1)
                    j = step - 2
                    if 0 <= j < JOBS:
                        y = j % 2
                        dve.wait_ge(j_pT, JOBS * l + j + 1)
                        V.tensor_copy(pT_buf[:, y, 0:keys(j)], bank[4 + y][:, 0:keys(j)]).then_inc(j_pTc, 1)
                    j = step - 1
                    if 0 <= j < JOBS:
                        dve.wait_ge(j_exp, JOBS * l + j + 1)
                        y = j % 2
                        then(V.reciprocal(rsum[:, y, :], esum[:, y, :]))
                        then(V.tensor_tensor(rsum[:, y, 1:2], rsum[:, y, 1:2], lams[:, 4:5], ALU.mult))
                        n = keys(j)
                        then(V.tensor_scalar(p_buf[:, y, 0:n], e_buf[:, y, 0, 0:n], rsum[:, y, 0:1], None, ALU.mult))
                        V.scalar_tensor_tensor(out=p_buf[:, y, 0:n], in0=e_buf[:, y, 1, 0:n], scalar=rsum[:, y, 1:2],
                                               in1=p_buf[:, y, 0:n], op0=ALU.mult, op1=ALU.add).then_inc(j_p, 1)
                    j = step - 3
                    if 0 <= j < JOBS:
                        dve.wait_ge(j_o, JOBS * l + j + 1)
                        V.tensor_copy(head(B_Q, j), bank[4 + j % 2][:, 2 * T:2 * T + VD]).then_inc(j_oc, 1)
                dve.wait_ge(osd_ok, l + 1)
                dve.wait_ge(j_oc, JOBS * (l + 1))
                then(V.reciprocal(ors[:, :], osd[:, :]))
                for half in range(2):
                    o = work[:, B_Q + half, :].rearrange("p (j d) -> p j d", j=8)
                    V.tensor_tensor(o, o, ors[:, 8 * half:8 * half + 8].unsqueeze(2).to_broadcast([P, 8, VD]), ALU.mult)\
                        .then_inc(on_ok, 1)
                for i in range(4):
                    dve.wait_ge(oT_hi, 4 * l + i + 1)
                    at = (slice(None), slice(4 * (i // 2), 4 * (i // 2) + 4), i % 2, slice(None))
                    V.scalar_tensor_tensor(out=hT_lo[at], in0=four(bank[i]), scalar=sublng[:, l:l + 1],
                                           in1=hT_hi[at].bitcast(F32), op0=ALU.mult, op1=ALU.subtract).then_inc(oT_ok, 1)
                lo(q0 + 1, 0)
                lo(q0 + 1, 1)
                multiplied(dve, q0 + 1, 0)
                for g in range(G):
                    for half in range(2):
                        ins = V.tensor_tensor(blk(B_GATTN + half, g), bank[4 + 2 * g + half][:, :], blk(B_GATTN + half, g), ALU.mult)
                then(ins)
                for half in range(2):
                    V.tensor_tensor(work[:, B_GCONV + half, :], work[:, B_GCONV + half, :], work[:, B_GATTN + half, :], ALU.add)\
                        .then_inc(merged, 1)
                for i in range(4):
                    dve.wait_ge(m_hi, 4 * l + i + 1)
                    at = (slice(None), slice(4 * (i % 2), 4 * (i % 2) + 4), i // 2, slice(None))
                    V.tensor_tensor(xT_lo[at], four(bank[i]), xT_hi[at].bitcast(F32), ALU.subtract).then_inc(m_ok, 1)
                lo(q0 + 1, 2)
                q0 += 2
                lo(q0, 0, kind=KINDS[0])
                multiplied(dve, q0 - 1, 2)
                residual(2 * l)
                dve.wait_ge(kv_kept, 64 * (l + 1))
                layer_norm(2 * l + 1)
                modulate(2 * l + 1)
                if l == 0:
                    for e in range(DENSE_PARTS):
                        expert(q0 + e * Q_EXPERT, e, KINDS[0] if e + 1 < DENSE_PARTS else FULL)
                    multiplied(dve, q0 + DENSE_PARTS * Q_EXPERT - 1, 2)
                else:
                    route()
                    V.memset(y_hi.bitcast(F32), 0.0).then_inc(y_zero, 1)
                    for i in range(2):
                        dve.wait_ge(xt_t, 2 + i + 1)
                        V.tensor_copy(tokens[:, 1, i * COL:(i + 1) * COL], bank[6 + i][:, :]).then_inc(xt_ok, 1)
                    make_plan()
                    last_pass = dve.value_load(plan[0:1, 0:1], min_val=NE - 1, max_val=PASSES - 1)
                    selection(0)
                    gathered(0)
                    with dve.Fori(0, last_pass) as p:
                        one_pass(p * Q_EXPERT + q0, p, False)
                    one_pass(last_pass * Q_EXPERT + q0, last_pass, True)
                    dve.wait_ge(scattered, 1)
                residual(2 * l + 1)
                layer_norm(2 * l + 2)

        @block.tensor
        def _(pe):
            def mm3(o, hi, lo, wh, wl, start, stop):
                pe.matmul(o, hi, wh, start=start, stop=False)
                pe.matmul(o, lo, wh, start=False, stop=False)
                return pe.matmul(o, hi, wl, start=False, stop=stop)

            def unit_ready(q, s, unit):
                pe.wait_ge(lo_done, q * (PARTS * SLOTS) + (PARTS * s + unit + 1))

            def part(w, unit, k, n):
                return w[:, unit, k * n:(k + 1) * n]

            def columns(q, s, units, outs, n, lhs=None):
                for unit in units:
                    unit_ready(q, s, unit)
                    for k in range(2):
                        kk = 2 * unit + k
                        for g, o in enumerate(outs):
                            ins = mm3(o, xT_hi[:, kk, g, :], xT_lo[:, kk, g, :], part(w_hi, unit, k, n),
                                      part(w_lo, unit, k, n), kk == 0, kk == KD - 1)
                    ins.then_inc(parts_free, 1)

            def rows(q, s, outs, lhs_hi, lhs_lo, k0, k1, start, stop):
                first = cut((1, k1 - k0), 0)[1]
                for unit in range(PARTS):
                    unit_ready(q, s, unit)
                    c0, c1 = (k0, k0 + first) if unit % 2 == 0 else (k0 + first, k1)
                    for k in range(c0, c1):
                        for g, o in enumerate(outs):
                            ins = mm3(o[unit // 2][:, :], lhs_hi[:, k, g, :], lhs_lo[:, k, g, :],
                                      part(w_hi, unit, k - c0, COL), part(w_lo, unit, k - c0, COL),
                                      start and k == k0, stop and k == k1 - 1)
                    ins.then_inc(parts_free, 1)
                    yield unit

            def row_block(*args):
                for _ in rows(*args):
                    pass

            def transpose_xhat(n):
                for g in range(G):
                    pe.wait_ge(xhat_ok, G * n + g + 1)
                    for k in range(KD):
                        ins = pe.transpose(bank[2 * g + k // 4][:, (k % 4) * T:(k % 4 + 1) * T],
                                           xhat[:, g, k * P:(k + 1) * P], ident[:, :])
                    ins.then_inc(xhat_t, 1)

            def gate_broadcast(n):
                for i in range(4):
                    for k in range(4):
                        col = adaT[:, n // 2, 2 + 3 * (n % 2), 4 * (i % 2) + k, i // 2:i // 2 + 1]
                        ins = pe.matmul(bank[i][:, k * P:(k + 1) * P], col.to_broadcast([P, T]), ident[:, :],
                                        start=True, stop=True)
                    ins.then_inc(bc_mm, 1)

            def expert(q, ec, start, stop):
                def transpose_h(c):
                    k0, k1 = HT[c]
                    pe.wait_ge(h_ok, ec * 4 + (c + 1))
                    for g in range(G):
                        for k in range(k0, k1):
                            ins = pe.transpose(bank[2 + g][:, (k - k0) * T:(k - k0 + 1) * T], h[:, g, k * P:(k + 1) * P],
                                               ident[:, :])
                    ins.then_inc(hT_t, 1)

                for j in range(8):
                    jq, js, c = q + j // SLOTS, j % SLOTS, j // 2
                    if j % 2 == 0:
                        if c:
                            pe.wait_ge(g_silu, ec * 4 + c)
                        outs = [bank[g][:, 0:FCOL] for g in range(G)]
                        columns(jq, js, (0, 1), outs, FCOL)
                        if c:
                            transpose_h(c - 1)
                        columns(jq, js, (2, 3), outs, FCOL)
                    else:
                        if c:
                            pe.wait_ge(hT_ok, ec * 4 + c)
                        outs = [bank[2 + g][:, 0:FCOL] for g in range(G)]
                        columns(jq, js, range(PARTS), outs, FCOL)
                for d, (k0, k1) in enumerate(DOWN):
                    if d == 2:
                        pe.wait_ge(hT_ok, ec * 4 + 4)
                    for unit in rows(q + (8 + d) // SLOTS, (8 + d) % SLOTS, ACC, hT_hi, hT_lo, k0, k1,
                                     start and d == 0, stop and d == 3):
                        if d == 1 and unit == 1:
                            transpose_h(3)

            def gather(p):
                pe.wait_ge(sel_ok, p + 1)
                for k in range(KD):
                    for g in range(G):
                        ins = pe.matmul(bank[k // 4 * 2][:, (k % 4) * T:(k % 4 + 1) * T], tokens[:, g, k * P:(k + 1) * P],
                                        select[:, g, :], start=g == 0, stop=g == G - 1)
                ins.then_inc(gx_mm, 1)

            def scatter(p, last):
                pe.wait_ge(st_ok, p + 1)
                pe.wait_ge(y_ok, p * 2 + 2)
                for g in range(G):
                    for half in range(2):
                        at = slice(4 * half, 4 * half + 4)
                        pe.matmul(ACC[g][half][:, :], selT[:, g, :], y_hi[:, at], start=False, stop=False)
                        ins = pe.matmul(ACC[g][half][:, :], selT[:, g, :], y_lo[:, at], start=False, stop=last)
                if last:
                    ins.then_inc(scattered, 1)

            def one_pass(q, p, first, last):
                hc = (p + DENSE_PARTS) * 4
                for j in range(8):
                    jq, js, c = q + j // SLOTS, j % SLOTS, j // 2
                    if j % 2 == 0:
                        if c == 0:
                            pe.wait_ge(gx_ok, p * 2 + 2)
                        else:
                            pe.wait_ge(g_silu, hc + c)
                        columns(jq, js, (0, 1), [bank[0][:, 0:FCOL]], FCOL)
                        if c:
                            transpose_h(c - 1, hc, p)
                        columns(jq, js, (2, 3), [bank[0][:, 0:FCOL]], FCOL)
                        if c == 0 and not first:
                            scatter(p - 1, False)
                    else:
                        columns(jq, js, (0, 1), [bank[2][:, 0:FCOL]], FCOL)
                        if c == 0:
                            for g in range(G):
                                pe.transpose(bank[3][:, g * T:(g + 1) * T], select[:, g, :], ident[:, :])
                            for g in range(G):
                                ins = pe.matmul(bank[3][:, G * T:G * T + 1], select[:, g, :], gate_col[:, g:g + 1],
                                                start=g == 0, stop=g == G - 1)
                            ins.then_inc(st_t, 1)
                        columns(jq, js, (2, 3), [bank[2][:, 0:FCOL]], FCOL)
                for d, (k0, k1) in enumerate(DOWN):
                    if d in (0, 2):
                        pe.wait_ge(hT_ok, hc + (3 + d // 2))
                    for unit in rows(q + (8 + d) // SLOTS, (8 + d) % SLOTS, [[bank[1], bank[3]]], hT_hi, hT_lo, k0, k1,
                                     d == 0, d == 3):
                        if d == 1 and unit == 1:
                            transpose_h(3, hc, p)
                        if d == 2 and unit == 1 and not last:
                            gather(p + 1)

            def transpose_h(c, hc, p):
                k0, k1 = HT[c]
                pe.wait_ge(h_ok, hc + (c + 1))
                if c == 1:
                    pe.wait_ge(st_ok, p + 1)
                    pe.wait_ge(ge_ok, p + 1)
                if c == 2:
                    pe.wait_ge(hT_ok, hc + 1)
                for k in range(k0, k1):
                    ins = pe.transpose(t_bank(c)[:, (k - k0) * T:(k - k0 + 1) * T], h[:, 0, k * P:(k + 1) * P], ident[:, :])
                ins.then_inc(hT_t, 1)

            ACC = [bank[4:6], bank[6:8]]
            pe.sem_inc(parts_free, PARTS)
            pe.wait_ge(const_ok, 1)
            pe.wait_ge(ld_vec, 16 * N_VEC)
            pe.transpose(bank[7][:, 0:P], vec_rows[:, :], ident[:, :]).then_inc(vec_t, 1)
            pe.wait_ge(cond_ok, G)
            for l in range(DEPTH):
                q0 = turn0[l]
                if l:
                    pe.wait_ge(res_ok, 2 * l)
                with pe.Fori(0, Q_IN) as i:
                    for s in range(SLOTS):
                        pe.wait_ge(ada_out, i * SLOTS + (ADA_BLOCKS * l + s + 1))
                        for unit in range(PARTS):
                            unit_ready(i + q0, s, unit)
                            for k in range(2):
                                kk = 2 * unit + k
                                for w in (w_hi, w_lo):
                                    ins = pe.matmul(bank[4 + s][0:66, :], cond_st[:, kk, :], part(w, unit, k, COL),
                                                    start=kk == 0 and w is w_hi, stop=kk == KD - 1 and w is w_lo)
                            ins.then_inc(parts_free, 1)
                pe.wait_ge(ada_out, ADA_BLOCKS * (l + 1) + SLOTS)
                pe.wait_ge(ld_bias, 16 * (l + 1))
                pe.wait_ge(vec_ok, 1)
                for v in range(6 * KD):
                    ins = pe.matmul(bank[7][:, v * G:(v + 1) * G], ada_rows[:, v * P:(v + 1) * P], sel[:, :, 0],
                                    start=True, stop=True)
                ins.then_inc(ada_cols, 1)
                transpose_xhat(2 * l)
                pe.wait_ge(mod_ok, G * (2 * l + 1))
                q0 += Q_IN

                def in_block(q, s, j):
                    pe.wait_ge(in_out0, j)
                    pe.wait_ge(in_out1, j)
                    columns(q, s, range(PARTS), [bank[2 * s][:, :], bank[2 * s + 1][:, :]], COL)

                with pe.Fori(0, RUNS_IN) as i:
                    for s in range(SLOTS):
                        in_block(i + q0, s, i * SLOTS + (IN_BLOCKS * l + s + 1))
                q0 += RUNS_IN
                in_block(q0, 0, IN_BLOCKS * (l + 1))
                pe.wait_ge(in_out0, SLOTS + IN_BLOCKS * (l + 1))
                pe.wait_ge(in_out1, SLOTS + IN_BLOCKS * (l + 1))
                pe.wait_ge(gcu_ok, l + 1)
                for c in range(KC):
                    for i, b in enumerate((B_GB, B_GC)):
                        for g in range(G):
                            ins = pe.transpose(bank[c][:, (2 * i + g) * T:(2 * i + g + 1) * T],
                                               work[:, b, g * COL + c * P:g * COL + (c + 1) * P], ident[:, :])
                    ins.then_inc(conv_t, 1)
                pe.wait_ge(conv_ok, KC * (l + 1))
                row_block(q0, 1, ACC, xT_hi, xT_lo, 0, 4, True, True)
                pe.wait_ge(conv_out, l + 1)
                pe.wait_ge(roped, l + 1)
                pe.wait_ge(ld_cache, 32 * (l + 1))
                for step in range(JOBS + 3):
                    j = step
                    if j < JOBS:
                        if j >= 2:
                            pe.wait_ge(j_qkT, JOBS * l + j - 1)
                        o = bank[2 + j % 2]
                        pe.transpose(o[:, 0:T], head(B_Q, j), ident[:, :])
                        ins = pe.transpose(o[:, T:2 * T], head(B_K, j), ident[:, :])
                        if keys(j) > T:
                            ins = pe.transpose(o[:, 2 * T:3 * T], cache[:, 0, head_of(j), :], ident[:, :])
                        ins.then_inc(j_qk, 1)
                    j = step - 1
                    if 0 <= j < JOBS:
                        n, y = keys(j), j % 2
                        pe.wait_ge(j_qkT, JOBS * l + j + 1)
                        if j >= 2:
                            pe.wait_ge(j_exp, JOBS * l + j - 1)
                        for i in range(2):
                            r = slice(HD * i, HD * (i + 1))
                            ins = pe.matmul(s_bank(j, i)[:, 0:n], qkT[r, y, 0:T], qkT[r, y, T:T + n], start=True, stop=True)
                        ins.then_inc(j_s, 1)
                    j = step - 2
                    if 0 <= j < JOBS:
                        y = j % 2
                        pe.wait_ge(j_p, JOBS * l + j + 1)
                        if j >= 2:
                            pe.wait_ge(j_oc, JOBS * l + j - 1)
                        for k in range(keys(j) // T):
                            ins = pe.transpose(bank[4 + y][:, k * T:(k + 1) * T], p_buf[:, y, k * T:(k + 1) * T], ident[:, :])
                        ins.then_inc(j_pT, 1)
                    j = step - 3
                    if 0 <= j < JOBS:
                        y = j % 2
                        pe.wait_ge(j_pTc, JOBS * l + j + 1)
                        vs = [head(B_V, j)] + [cache[:, 1, head_of(j), :]] * (keys(j) > T)
                        for k, v in enumerate(vs):
                            ins = pe.matmul(bank[4 + y][:, 2 * T:2 * T + VD], pT_buf[:, y, k * T:(k + 1) * T], v,
                                            start=k == 0, stop=k == len(vs) - 1)
                        ins.then_inc(j_o, 1)
                for i in range(4):
                    if i % 2 == 0:
                        pe.wait_ge(on_ok, 2 * l + i // 2 + 1)
                    for k in range(4):
                        ins = pe.transpose(bank[i][:, k * T:(k + 1) * T], head(B_Q, 4 * i + k), ident[:, :])
                    ins.then_inc(oT_t, 1)
                pe.wait_ge(oT_ok, 4 * (l + 1))
                row_block(q0, 2, ACC, hT_hi, hT_lo, 0, 4, True, False)
                row_block(q0 + 1, 0, ACC, hT_hi, hT_lo, 4, 8, False, True)
                pe.wait_ge(merged, 2 * (l + 1))
                for i in range(4):
                    for k in range(4):
                        ins = pe.transpose(bank[i][:, k * T:(k + 1) * T],
                                           work[:, B_GCONV + i % 2, (i // 2) * COL + k * P:(i // 2) * COL + (k + 1) * P], ident[:, :])
                    ins.then_inc(m_t, 1)
                pe.wait_ge(m_ok, 4 * (l + 1))
                gate_broadcast(2 * l)
                row_block(q0 + 1, 1, ACC, xT_hi, xT_lo, 0, 4, True, False)
                row_block(q0 + 1, 2, ACC, xT_hi, xT_lo, 4, 8, False, True)
                q0 += 2
                pe.wait_ge(bc_ok, 4 * (2 * l + 1))
                transpose_xhat(2 * l + 1)
                pe.wait_ge(mod_ok, G * (2 * l + 2))
                if l == 0:
                    for e in range(DENSE_PARTS):
                        expert(q0 + e * Q_EXPERT, e, e == 0, e == DENSE_PARTS - 1)
                else:
                    pe.wait_ge(r_parts, 2)
                    for g in range(G):
                        for k in range(KD):
                            ins = mm3(bank[2][:, g * NE:(g + 1) * NE], xT_hi[:, k, g, :], xT_lo[:, k, g, :], r_hi[:, k, :],
                                      r_lo[:, k, :], k == 0, k == KD - 1)
                    ins.then_inc(r_mm, 1)
                    for g in range(G):
                        for k in range(KD):
                            ins = pe.transpose(bank[4 + 2 * g + k // 4][:, (k % 4) * T:(k % 4 + 1) * T], modulated[:, g, k, :],
                                               ident[:, :])
                            if k % 4 == 3:
                                ins.then_inc(xt_t, 1)
                    pe.wait_ge(mask_ok, 1)
                    for i, terms in enumerate((((before, 0),), ((all_ones, 0), (before, 1)), ((all_ones, 0), (all_ones, 1)))):
                        for t, (m, g) in enumerate(terms):
                            ins = pe.matmul(bank[2][:, 64 + i * NE:64 + (i + 1) * NE], m[:, :], one_hot[:, g, :],
                                            start=t == 0, stop=t == len(terms) - 1)
                    ins.then_inc(pos_mm, 1)
                    pe.wait_ge(xt_ok, 4)
                    pe.wait_ge(y_zero, 1)
                    for g in range(G):
                        for half in range(2):
                            pe.matmul(ACC[g][half][:, :], xT_hi[:, 0, 0, :], y_hi[:, 4 * half:4 * half + 4], start=True, stop=False)
                    pe.wait_ge(plan_ok, 1)
                    last_pass = pe.value_load(plan[0:1, 0:1], min_val=NE - 1, max_val=PASSES - 1)
                    gather(0)
                    one_pass(q0, 0, True, False)
                    with pe.Fori(1, last_pass) as p:
                        one_pass(p * Q_EXPERT + q0, p, False, False)
                    one_pass(last_pass * Q_EXPERT + q0, last_pass, False, True)
                    scatter(last_pass, True)
                gate_broadcast(2 * l + 1)


_INS = ["x_prompt", "x_sample", "cache_k", "cache_v", "c", "c_ctx", "ln_in_g", "ln_in_b", "ada_w", "ada_b", "w_in",
        "conv_w", "conv_b", "w_conv_out", "lam_q1", "lam_k1", "lam_q2", "lam_k2", "subln_g", "w_attn_out", "w_out",
        "ln1_g", "ln1_b", "ln2_g", "ln2_b", "ffn_w_gate", "ffn_w_up", "ffn_w_down", "moe_router", "moe_w_gate",
        "moe_w_up", "moe_w_down"]
_OUTS = [(1, T, D), (1, T, D), (1, DEPTH, HEADS, T, VD), (1, DEPTH, HEADS, T, VD)]


def rope_table():
    import numpy as np
    f = np.float32
    inv = (f(10000.0) ** (-np.arange(0, 32, 2, dtype=f) / f(32))).astype(f)
    row = np.repeat(np.arange(T // 64, dtype=f), 64)[:, None] * inv
    col = np.tile(np.arange(64, dtype=f), T // 64)[:, None] * inv
    ang = np.concatenate([row, col], axis=1).astype(np.float64)
    return np.stack([np.cos(ang), np.sin(ang)], axis=1).astype(f)


def kernel(**inputs):
    import numpy as np
    import concourse.bacc as bacc
    from concourse.bass_utils import run_bass_kernel_spmd as run

    nc = bacc.Bacc("TRN2", target_bir_lowering=False, num_devices=1)
    arrays, args = {}, {}
    for name, value in [(n, inputs[n]) for n in _INS] + [("rope", rope_table())]:
        v = np.ascontiguousarray(value)
        arrays[f"in_{name}"] = v
        args[name] = nc.dram_tensor(f"in_{name}", v.shape, mybir.dt.from_np(v.dtype), kind="ExternalInput").ap()
    outs = [nc.dram_tensor(f"out_{i}", s, F32, kind="ExternalOutput").ap() for i, s in enumerate(_OUTS)]
    program(nc, args, outs)
    r = run(nc, [arrays], core_ids=[0])
    return tuple(r.results[0][f"out_{i}"] for i in range(len(_OUTS)))
```

```python
import math
from contextlib import ExitStack

import concourse.bass as bass
from concourse import mybir

F32 = mybir.dt.float32
F32R = mybir.dt.float32r
ALU = mybir.AluOpType
ACT = mybir.ActivationFunctionType
AX_X = mybir.AxisListType.X

P = 128
D = 1024
KD = D // P
T = 128
G = 2
DEPTH = 2
D_CONV = 512
KC = D_CONV // P
HEADS = 8
HD = 64
VD = 2 * HD
FF = 1408
KF = FF // P
NE = 8
DENSE_PARTS = 2816 // FF
COL = 512
D_IN = 6656
IN_BLOCKS = D_IN // COL
ADA_BLOCKS = 6 * D // COL
FCOL = FF // 4
ALPHA = (2 * DEPTH) ** 0.25
EPS = 1e-5
SCALE = HD ** -0.5
SLOTS = 3
PARTS = 4
UNIT = 1024
DOWN = [(0, 3), (3, 6), (6, 9), (9, 11)]
HT = [(0, 2), (2, 5), (5, 8), (8, 11)]
JOBS = HEADS * G
PASSES = NE + 3
FAR = 4096.0
B_GB, B_GC, B_U, B_Q, B_K, B_V, B_GCONV, B_GATTN = 0, 1, 2, 3, 5, 7, 9, 11

V_CW, V_CB, V_SG, V_LAYER = 0, 12, 16, 17
V_LN = V_CW + V_LAYER * DEPTH
N_VEC = 5 * DEPTH + 8 + 1


def program(nc, a, out):
    with ExitStack() as ctx:
        def sb(name, shape, dt=F32):
            return ctx.enter_context(nc.sbuf_tensor(name, shape, dt))

        def sem(name):
            return ctx.enter_context(nc.semaphore(name))

        raw = sb("raw", [P, SLOTS, PARTS * UNIT])
        w_hi = sb("w_hi", [P, PARTS, UNIT], F32R)
        w_lo = sb("w_lo", [P, PARTS, UNIT], F32R)
        xT_hi = sb("xT_hi", [P, KD, G, T], F32R)
        xT_lo = sb("xT_lo", [P, KD, G, T], F32R)
        hT_hi = sb("hT_hi", [P, KF, G, T], F32R)
        hT_lo = sb("hT_lo", [P, KF, G, T], F32R)
        work = sb("work", [P, IN_BLOCKS, G * COL])
        x = sb("x", [P, G, D])
        cache = sb("cache", [P, 2, HEADS, VD])
        vecT = sb("vecT", [P, P])
        biasT = sb("biasT", [P, P])
        ident = sb("ident", [P, P])
        sel = sb("sel", [4, G, 2])
        ada_rows = sb("ada_rows", [4, SLOTS, COL])
        cond = sb("cond", [P, 2 * KD])
        cond_st = sb("cond_st", [P, KD, 66], F32R)
        adaT = sb("adaT", [P, DEPTH, 6, KD, G])
        modA = sb("modA", [P, 2 * DEPTH, KD, G])
        modB = sb("modB", [P, 2 * DEPTH, KD, G])
        rope = sb("rope", [P, 2, 32])
        lamv = sb("lamv", [P, 4, HD])
        lams = sb("lams", [P, 8])
        st = sb("st", [P, G, 2, 6])
        mv = sb("mv", [P, G, 2])
        sd = sb("sd", [P, G])
        rstd = sb("rstd", [P, G])
        mx = sb("mx", [P, 2, 2])
        nmx = sb("nmx", [P, 2, 2])
        esum = sb("esum", [P, 2, 2])
        rsum = sb("rsum", [P, 2, 2])
        sublng = sb("sublng", [P, DEPTH])
        osq = sb("osq", [P, JOBS])
        osd = sb("osd", [P, JOBS])
        ors = sb("ors", [P, JOBS])
        eps_c = sb("eps_c", [P, 1])
        r_raw = sb("r_raw", [P, KD, NE])
        r_hi = sb("r_hi", [P, KD, 66], F32R)
        r_lo = sb("r_lo", [P, KD, 66], F32R)
        iota = sb("iota", [P, NE])
        rt = sb("rt", [P, 8, G, NE])
        rs = sb("rs", [P, 8, G])
        gates = sb("gates", [P, G, NE])
        one_hot = sb("one_hot", [P, G, NE])
        before = sb("before", [P, P])
        all_ones = sb("all_ones", [P, P])
        slot_no = sb("slot_no", [P, P])
        pos_tab = sb("pos_tab", [P, G, PASSES])
        gate_tab = sb("gate_tab", [P, G, PASSES])
        over = sb("over", [P, 4, NE])
        plan_f = sb("plan_f", [P, 8])
        plan = sb("plan", [P, 8], mybir.dt.int32)
        gate_col = sb("gate_col", [P, G])
        gate_slot = sb("gate_slot", [P, 1])
        pad = sb("pad", [P, G, T + 2])
        cv = sb("cv", [P, G, T])
        bank = [ctx.enter_context(nc.psum_tensor(f"bank{i}", [P, COL], F32)) for i in range(8)]

        flat = work[:, :, :].rearrange("p b n -> p (b n)")
        xhat = flat[:, B_V * 1024:(B_V + 2) * 1024].rearrange("p (g d) -> p g d", g=G)
        modulated = flat[:, B_Q * 1024:(B_Q + 2) * 1024].rearrange("p (g k t) -> p g k t", g=G, k=KD)
        gate_bc = [[flat[:, b * 1024:(b + 1) * 1024] for b in bs] for bs in ((B_K, B_K + 1), (B_U, B_GATTN + 1))]
        h = flat[:, B_GCONV * 1024:B_GCONV * 1024 + G * FF].rearrange("p (g f) -> p g f", g=G)
        tokens = flat[:, B_K * 1024:(B_K + 2) * 1024].rearrange("p (g d) -> p g d", g=G)
        select = flat[:, B_GCONV * 1024 + FF:B_GCONV * 1024 + FF + G * T].rearrange("p (g s) -> p g s", g=G)
        logits = flat[0:NE, B_GCONV * 1024 + FF + G * T:B_GCONV * 1024 + FF + 2 * G * T]
        y_hi, y_lo = (w[:, 0:KD, 1, :] for w in (hT_hi, hT_lo))
        selT = hT_hi[:, KD:KD + G, 1, :]
        att = flat[:, 0:2048]
        e_buf = att[:, 0:1024].rearrange("p (b s k) -> p b s k", b=2, s=2)
        p_buf = att[:, 1024:1536].rearrange("p (b k) -> p b k", b=2)
        pT_buf = att[:, 1536:2048].rearrange("p (b k) -> p b k", b=2)
        qkT = flat[:, 2048:2048 + 6 * T].rearrange("p (b k) -> p b k", b=2)
        vec_rows, bias_rows, c_rows = (flat[:, 12288 + i * P:12288 + (i + 1) * P] for i in range(3))
        ln_gb = [flat[:, b * 1024:(b + 2) * 1024].rearrange("p (w d) -> p w d", w=2) for b in (B_GCONV, 0, 0, 0, 0)]
        rope_t = flat[:, 12288:13312]

        slot_i = flat[:, 12288 + 3 * P:12288 + 4 * P].bitcast(mybir.dt.int32)

        def blk(b, g):
            return work[:, b, g * COL:(g + 1) * COL]

        def four(b):
            return b[:, :].rearrange("p (k t) -> p k t", t=T)

        def conv_res(c):
            return work[:, B_U, c * G * T:(c + 1) * G * T].rearrange("p (g t) -> p g t", g=G)

        def keys(j):
            return 2 * T if j % 8 >= 4 else T

        def s_bank(j, i):
            return bank[j % 2 + 6 * i]

        def head_of(j):
            return 4 * (j // 8) + j % 4

        def lam_init(l):
            return 0.8 - 0.6 * math.exp(-0.3 * l)

        def head(b0, j):
            return work[:, b0 + j // 8, (j % 8) * VD:(j % 8 + 1) * VD]

        raw_in = [[sem(f"raw_in{i}_{u}") for u in range(2)] for i in range(SLOTS)]
        hi_done = sem("hi_done")
        lo_done = sem("lo_done")
        parts_free = sem("parts_free")
        ada_out = sem("ada_out")
        in_out0 = sem("in_out0")
        in_out1 = sem("in_out1")
        ld_vec, ld_x, ld_small, ld_lam = sem("ld_vec"), sem("ld_x"), sem("ld_small"), sem("ld_lam")
        ld_c, ld_cache, ld_ln = sem("ld_c"), sem("ld_cache"), sem("ld_ln")
        stored, kv_kept = sem("stored"), sem("kv_kept")
        ident_ok, const_ok = sem("ident_ok"), sem("const_ok")
        pool_s, dve_s, act_s = sem("pool_s"), sem("dve_s"), sem("act_s")
        c_zero, c_t, silu_ok, cond_hi, cond_ok = (sem(n) for n in ("c_zero", "c_t", "silu_ok", "cond_hi", "cond_ok"))
        vec_t, vec_ok = sem("vec_t"), sem("vec_ok")
        stats_ok, std_ok, xhat_ok, x_ok = (sem(n) for n in ("stats_ok", "std_ok", "xhat_ok", "x_ok"))
        ada_cols, ada_kept, coef_ok = sem("ada_cols"), sem("ada_kept"), sem("coef_ok")
        xhat_t, mod_act, mod_dve, mod_hi, mod_ok = (sem(n) for n in ("xhat_t", "mod_act", "mod_dve", "mod_hi", "mod_ok"))
        gcu_ok, conv_t, conv_f, conv_hi, conv_ok = (
            sem(n) for n in ("gcu_ok", "conv_t", "conv_f", "conv_hi", "conv_ok"))
        conv_out = sem("conv_out")
        lam_dot, lam_exp, roped = sem("lam_dot"), sem("lam_exp"), sem("roped")
        j_qk, j_qkT, j_s, j_max, j_exp, j_p, j_pT, j_pTc, j_o, j_oc, j_sq = (
            sem(n) for n in ("j_qk", "j_qkT", "j_s", "j_max", "j_exp", "j_p", "j_pT", "j_pTc", "j_o", "j_oc", "j_sq"))
        osd_ok, on_ok, oT_t, oT_hi, oT_ok = (sem(n) for n in ("osd_ok", "on_ok", "oT_t", "oT_hi", "oT_ok"))
        merged, m_t, m_hi, m_ok = (sem(n) for n in ("merged", "m_t", "m_hi", "m_ok"))
        bc_mm, bc_ok = sem("bc_mm"), sem("bc_ok")
        g_silu, h_ok, hT_t, hT_hi_ok, hT_ok = (sem(n) for n in ("g_silu", "h_ok", "hT_t", "hT_hi_ok", "hT_ok"))
        xt_t, xt_ok, mask_ok, pos_mm, plan_ok, sel_ok = (sem(n) for n in ("xt_t", "xt_ok", "mask_ok", "pos_mm", "plan_ok", "sel_ok"))
        pos_read = sem("pos_read")
        gx_mm, gx_hi, gx_ok, st_t, st_ok, ge_ok = (sem(n) for n in ("gx_mm", "gx_hi", "gx_ok", "st_t", "st_ok", "ge_ok"))
        y_hi_ok, y_ok, y_zero, scattered = (sem(n) for n in ("y_hi_ok", "y_ok", "y_zero", "scattered"))
        r_zero, r_parts, r_mm, r_row, r_col, r_max, r_exp = (
            sem(n) for n in ("r_zero", "r_parts", "r_mm", "r_row", "r_col", "r_max", "r_exp"))

        Q_ADA = ADA_BLOCKS // SLOTS
        Q_PRE = (IN_BLOCKS + 5) // SLOTS
        Q_EXPERT = 12 // SLOTS
        turn0 = [DEPTH * Q_ADA, DEPTH * Q_ADA + Q_PRE + DENSE_PARTS * Q_EXPERT]
        FULL = (COL, 4)
        KINDS = [(FCOL, 4)] * 8 + [(COL, k1 - k0) for k0, k1 in DOWN]

        def cut(kind, unit):
            n, chunks = kind
            first = 2 if chunks > 2 else 1
            return (0, first * n) if unit % 2 == 0 else (first * n, (chunks - first) * n)

        RUNS_IN = IN_BLOCKS // SLOTS
        RUNS_QKV = (B_GCONV - B_Q) // SLOTS

        def t_bank(c):
            return bank[(1, 3, 1, 2)[c]]

        def multiplied(eng, q, s, unit=PARTS - 1):
            eng.wait_ge(parts_free, q * (PARTS * SLOTS) + (PARTS * s + unit + 1 + PARTS))

        block = ctx.enter_context(nc.Block())

        @block.sync
        def _(sp):
            def load(q, s, half, shape, src):
                if not isinstance(q, int) or q > 0:
                    sp.wait_ge(lo_done, (q - 1) * (PARTS * SLOTS) + (PARTS * s + 2 * half + 2))
                n = shape[0] * shape[1]
                dst = raw[:, s, 2 * half * UNIT:2 * half * UNIT + n].rearrange("p (k n) -> p k n", n=shape[1])
                sp.dma_start(dst, src).then_inc(raw_in[s][half], 16)

            def columns(q, s, w, c0, n):
                for half in range(2):
                    load(q, s, half, (4, n), w[half * 4 * P:(half + 1) * 4 * P, :]
                         .rearrange("(k p) n -> p k n", p=P)[:, :, bass.ds(c0, n)])

            def rows(q, s, w, k0, k1):
                for half in range(2):
                    load(q, s, half, (k1 - k0, COL), w[k0 * P:k1 * P, half * COL:(half + 1) * COL]
                         .rearrange("(k p) n -> p k n", p=P))

            def expert(q, wg, wu, wd):
                for c in range(4):
                    columns(q + 2 * c // SLOTS, 2 * c % SLOTS, wg, c * FCOL, FCOL)
                    columns(q + (2 * c + 1) // SLOTS, (2 * c + 1) % SLOTS, wu, c * FCOL, FCOL)
                for d, (k0, k1) in enumerate(DOWN):
                    rows(q + (8 + d) // SLOTS, (8 + d) % SLOTS, wd, k0, k1)

            for s in range(SLOTS):
                columns(0, s, a["ada_w"][0], s * COL, COL)
            for l in range(DEPTH):
                with sp.Fori(int(l == 0), Q_ADA) as i:
                    for s in range(SLOTS):
                        columns(i + Q_ADA * l, s, a["ada_w"][l], i * (SLOTS * COL) + s * COL, COL)
            for l in range(DEPTH):
                with sp.Fori(0, RUNS_QKV) as i:
                    for s in range(SLOTS):
                        columns(i + turn0[l], s, a["w_in"][l], i * (SLOTS * COL) + (B_Q + s) * COL, COL)
                for turn, b in ((RUNS_QKV, B_GB), (RUNS_QKV + 1, B_GCONV)):
                    for s in range(SLOTS):
                        columns(turn0[l] + turn, s, a["w_in"][l], (b + s) * COL, COL)
                q = turn0[l] + RUNS_IN
                columns(q, 0, a["w_in"][l], (IN_BLOCKS - 1) * COL, COL)
                rows(q, 1, a["w_conv_out"][l], 0, 4)
                rows(q, 2, a["w_attn_out"][l], 0, 4)
                rows(q + 1, 0, a["w_attn_out"][l], 4, 8)
                rows(q + 1, 1, a["w_out"][l], 0, 4)
                rows(q + 1, 2, a["w_out"][l], 4, 8)
                q += 2
                if l == 0:
                    for e in range(DENSE_PARTS):
                        expert(q + e * Q_EXPERT, a["ffn_w_gate"][0][:, e * FF:(e + 1) * FF],
                               a["ffn_w_up"][0][:, e * FF:(e + 1) * FF], a["ffn_w_down"][0][e * FF:(e + 1) * FF, :])
                else:
                    def one(p, e):
                        expert(p * Q_EXPERT + q, *(a[n][0, bass.ds(e, 1)].rearrange("e d f -> (e d) f")
                                                   for n in ("moe_w_gate", "moe_w_up", "moe_w_down")))

                    with sp.Fori(0, NE - 1) as p:
                        one(p, p)
                    sp.wait_ge(plan_ok, 1)
                    last_pass = sp.value_load(plan[0:1, 0:1], min_val=NE - 1, max_val=PASSES - 1)
                    with sp.Fori(NE - 1, last_pass + 1) as p:
                        one(p, sp.value_load(plan[0:1, bass.ds(p - (NE - 2), 1)], min_val=0, max_val=NE - 1))

        @block.gpsimd
        def _(pool):
            n_self = [0]

            def then(ins):
                n_self[0] += 1
                ins.then_inc(pool_s, 1)
                pool.wait_ge(pool_s, n_self[0])

            def vec(row, src, n):
                pool.dma_start(vec_rows[row:row + n, :], src.rearrange("(n p) -> n p", p=P)).then_inc(ld_vec, 16)

            then(pool.memset(ident[:, :], 0.0))
            then(pool.affine_select(out=ident[:, :], in_=ident[:, :], compare_op=ALU.not_equal, fill=1.0, base=0,
                                    pattern=[[-1, P]], channel_multiplier=1))
            pool.sem_inc(ident_ok, 1)
            then(pool.memset(sel[:, :, :], 1.0))
            then(pool.affine_select(out=sel[:, 0, :], in_=sel[:, 0, :], compare_op=ALU.not_equal, fill=0.0,
                                    base=-2, pattern=[[0, 2]], channel_multiplier=1))
            then(pool.affine_select(out=sel[:, 0, :], in_=sel[:, 0, :], compare_op=ALU.not_equal, fill=0.0,
                                    base=-3, pattern=[[0, 2]], channel_multiplier=1))
            then(pool.affine_select(out=sel[:, 1, :], in_=sel[:, 1, :], compare_op=ALU.is_ge, fill=0.0,
                                    base=-2, pattern=[[0, 2]], channel_multiplier=1))
            then(pool.memset(eps_c[:, :], EPS))
            pool.sem_inc(const_ok, 1)
            pool.dma_start(x[:, 0, :], a["x_prompt"][0]).then_inc(ld_x, 16)
            pool.dma_start(x[:, 1, :], a["x_sample"][0]).then_inc(ld_x, 16)
            then(pool.memset(vec_rows[:, :], 0.0))
            then(pool.memset(bias_rows[:, :], 0.0))
            pool.dma_start(bias_rows[0:DEPTH * 6 * KD, :], a["ada_b"].rearrange("l (n p) -> (l n) p", p=P)).then_inc(ld_vec, 16)
            for l in range(DEPTH):
                r = l * V_LAYER
                for w in range(3):
                    vec(V_CW + r + 4 * w, a["conv_w"][l, w], KC)
                vec(V_CB + r, a["conv_b"][l], KC)
                vec(V_SG + r, a["subln_g"][l], 1)
            for n, (g, b) in enumerate(((a["ln_in_g"], a["ln_in_b"]), (a["ln1_g"][0], a["ln1_b"][0]),
                                        (a["ln2_g"][0], a["ln2_b"][0]), (a["ln1_g"][1], a["ln1_b"][1]))):
                vec(V_LN + n * 16, g, KD)
                vec(V_LN + n * 16 + KD, b, KD)
            for v in range(NE):
                then(pool.memset(iota[:, v:v + 1], float(v - NE)))
            then(pool.memset(all_ones[:, :], 1.0))
            then(pool.affine_select(out=before[:, :], in_=all_ones[:, :], compare_op=ALU.is_gt, fill=0.0, base=0,
                                    pattern=[[1, P]], channel_multiplier=-1))
            then(pool.iota(slot_i, pattern=[[1, P]], base=0, channel_multiplier=0))
            then(pool.tensor_copy(slot_no[:, :], slot_i))
            then(pool.memset(pad[:, :, :], 0.0))
            pool.sem_inc(const_ok, 1)
            pool.dma_start(rope[:, :, :], a["rope"]).then_inc(ld_small, 16)
            pool.dma_start(r_raw[:, :, :], a["moe_router"][0].rearrange("(k p) e -> p k e", p=P)).then_inc(ld_small, 16)

            def rests(q, s, kind=FULL):
                pool.wait_ge(lo_done, q * (PARTS * SLOTS) + PARTS * s)
                for unit in range(PARTS):
                    at, n = cut(kind, unit)
                    pool.wait_ge(hi_done, q * (PARTS * SLOTS) + (PARTS * s + unit + 1))
                    at += unit // 2 * 2 * UNIT
                    pool.tensor_tensor(w_lo[:, unit, 0:n], raw[:, s, at:at + n], w_hi[:, unit, 0:n].bitcast(F32), ALU.subtract)\
                        .then_inc(lo_done, 1)

            def load_ln(n):
                g, b = [(a["ln_in_g"], a["ln_in_b"]), (a["ln1_g"][0], a["ln1_b"][0]), (a["ln2_g"][0], a["ln2_b"][0]),
                        (a["ln1_g"][1], a["ln1_b"][1]), (a["ln2_g"][1], a["ln2_b"][1])][n]
                pool.dma_start(ln_gb[n][:, 0, :], g.unsqueeze(0).to_broadcast([P, D])).then_inc(ld_ln, 16)
                pool.dma_start(ln_gb[n][:, 1, :], b.unsqueeze(0).to_broadcast([P, D])).then_inc(ld_ln, 16)

            def make_x(n):
                pool.wait_ge(ld_ln, 32 * (n + 1))
                for g in range(G):
                    pool.wait_ge(xhat_ok, G * n + g + 1)
                    then(pool.tensor_tensor(x[:, g, :], xhat[:, g, :], ln_gb[n][:, 0, :], ALU.mult))
                    then(pool.tensor_tensor(x[:, g, :], x[:, g, :], ln_gb[n][:, 1, :], ALU.add))
                pool.sem_inc(x_ok, 1)

            load_ln(0)
            for l in range(DEPTH):
                if l:
                    pool.wait_ge(lam_dot, l)
                for i, name in enumerate(("lam_q1", "lam_k1", "lam_q2", "lam_k2")):
                    pool.dma_start(lamv[:, i, :], a[name][l].unsqueeze(0).to_broadcast([P, HD])).then_inc(ld_lam, 16)
                if l:
                    pool.wait_ge(j_oc, JOBS * l)
                pool.dma_start(cache[:, 0], a["cache_k"][0, l].rearrange("h t d -> t h d")).then_inc(ld_cache, 16)
                pool.dma_start(cache[:, 1], a["cache_v"][0, l].rearrange("h t d -> t h d")).then_inc(ld_cache, 16)
                make_x(2 * l)
                pool.wait_ge(in_out0, SLOTS + IN_BLOCKS * l + RUNS_QKV * SLOTS)
                for i, (b0, o) in enumerate(((B_K, out[2]), (B_V, out[3]))):
                    for half in range(2):
                        pool.dma_start(o[0, l, 4 * half:4 * half + 4].rearrange("h t d -> t h d"),
                                       blk(b0 + half, 0).rearrange("p (h d) -> p h d", h=4)).then_inc(kv_kept, 16)
                rests(turn0[l] + RUNS_IN, 2)
                pool.wait_ge(j_oc, JOBS * (l + 1))
                load_ln(2 * l + 1)
                tail = turn0[l] + RUNS_IN + 1
                rests(tail, 1)
                rests(tail + 1, 0, KINDS[0])
                make_x(2 * l + 1)
                load_ln(2 * l + 2)
                if l == 0:
                    rests(turn0[1], 0)
            for g in range(G):
                pool.wait_ge(x_ok, 2 * DEPTH + g + 1)
                pool.dma_start(out[g][0], x[:, g, :]).then_inc(stored, 16)
            pool.wait_ge(stored, 16 * G)
            pool.wait_ge(kv_kept, 64 * DEPTH)

        @block.scalar
        def _(act):
            act_n = [0]

            def then(ins):
                act_n[0] += 1
                ins.then_inc(act_s, 1)
                act.wait_ge(act_s, act_n[0])

            def hi(q, s, units=range(PARTS), kind=FULL):
                for unit in units:
                    at, n = cut(kind, unit)
                    if unit % 2 == 0:
                        act.wait_ge(raw_in[s][unit // 2], q * 16 + 16)
                    act.wait_ge(parts_free, q * (PARTS * SLOTS) + (PARTS * s + unit + 1))
                    at += unit // 2 * 2 * UNIT
                    nc.scalar.activation(w_hi[:, unit, 0:n], raw[:, s, at:at + n], ACT.Copy).then_inc(hi_done, 1)

            def ln_std(n):
                for g in range(G):
                    act.wait_ge(stats_ok, G * n + g + 1)
                    nc.scalar.activation(sd[:, g:g + 1], mv[:, g, 1:2], ACT.Sqrt, bias=eps_c[:, 0:1]).then_inc(std_ok, 1)

            def modulate(n):
                for g in range(G):
                    act.wait_ge(xhat_t, G * n + g + 1)
                    for k in range(4):
                        ins = nc.scalar.activation(modulated[:, g, k, :], bank[2 * g][:, k * T:(k + 1) * T], ACT.Identity,
                                                   bias=modB[:, n, k, g:g + 1], scale=modA[:, n, k, g:g + 1])
                    ins.then_inc(mod_act, 1)
                    act.wait_ge(mod_act, G * n + g + 1)
                    act.wait_ge(mod_dve, G * n + g + 1)
                    nc.scalar.activation(xT_hi[:, :, g, :], modulated[:, g, :, :], ACT.Copy).then_inc(mod_hi, 1)

            def gate_broadcast(n):
                for i in range(4):
                    act.wait_ge(bc_mm, 4 * n + i + 1)
                    nc.scalar.activation(gate_bc[n % 2][i // 2][:, (i % 2) * COL:(i % 2 + 1) * COL], bank[i][:, :], ACT.Copy)\
                        .then_inc(bc_ok, 1)

            def expert(q, ec, behind):
                sizes = KINDS + [behind]
                for j in range(12):
                    nq, ns, n = q + (j + 1) // SLOTS, (j + 1) % SLOTS, sizes[j + 1]
                    if n:
                        hi(nq, ns, (0, 1), n)
                    if j in (2, 4, 6, 9):
                        c = (2, 4, 6, 9).index(j)
                        k0, k1 = HT[c]
                        act.wait_ge(hT_t, ec * 4 + (c + 1))
                        for g in range(G):
                            ins = nc.scalar.activation(hT_hi[:, k0:k1, g, :],
                                                       bank[2 + g][:, 0:(k1 - k0) * T].rearrange("p (k t) -> p k t", t=T),
                                                       ACT.Copy)
                        ins.then_inc(hT_hi_ok, 1)
                    if n:
                        hi(nq, ns, (2, 3), n)
                    if j < 8 and j % 2 == 0:
                        multiplied(act, q + j // SLOTS, j % SLOTS)
                        for g in range(G):
                            ins = nc.scalar.activation(h[:, g, j // 2 * FCOL:(j // 2 + 1) * FCOL], bank[g][:, 0:FCOL], ACT.Silu)
                        ins.then_inc(g_silu, 1)

            def gathered(p):
                for i in range(2):
                    act.wait_ge(gx_mm, p + 1)
                    nc.scalar.activation(xT_hi[:, 4 * i:4 * i + 4, 0, :], four(bank[2 * i]), ACT.Copy).then_inc(gx_hi, 1)

            def one_pass(q, p, last):
                kinds = KINDS + [KINDS[0]]
                for j in range(12):
                    nq, ns = q + (j + 1) // SLOTS, (j + 1) % SLOTS
                    ahead = j < 11 or not last
                    if ahead:
                        hi(nq, ns, (0, 1), kinds[j + 1])
                    if j in (2, 4, 6, 9):
                        c = (2, 4, 6, 9).index(j)
                        k0, k1 = HT[c]
                        act.wait_ge(hT_t, (p + DENSE_PARTS) * 4 + (c + 1))
                        nc.scalar.activation(hT_hi[:, k0:k1, 0, :], t_bank(c)[:, 0:(k1 - k0) * T].rearrange("p (k t) -> p k t", t=T),
                                             ACT.Copy).then_inc(hT_hi_ok, 1)
                    if j == 1:
                        act.wait_ge(st_t, p + 1)
                        nc.scalar.activation(selT, bank[3][:, 0:G * T].rearrange("p (g t) -> p g t", g=G), ACT.Copy)\
                            .then_inc(st_ok, 1)
                    if j == 10 and not last:
                        gathered(p + 1)
                    if j == 11:
                        multiplied(act, q + 3, 2, 1)
                        nc.scalar.activation(y_hi[:, 0:4], four(bank[1]), ACT.Copy).then_inc(y_hi_ok, 1)
                    if ahead:
                        hi(nq, ns, (2, 3), kinds[j + 1])
                    if j == 11:
                        multiplied(act, q + 3, 2)
                        nc.scalar.activation(y_hi[:, 4:8], four(bank[3]), ACT.Copy).then_inc(y_hi_ok, 1)
                    if j < 8 and j % 2 == 0:
                        multiplied(act, q + j // SLOTS, j % SLOTS)
                        nc.scalar.activation(h[:, 0, j // 2 * FCOL:(j // 2 + 1) * FCOL], bank[0][:, 0:FCOL], ACT.Silu)\
                            .then_inc(g_silu, 1)

            act.sem_inc(in_out0, SLOTS)
            act.sem_inc(ada_out, SLOTS)
            act.wait_ge(c_zero, 1)
            act.dma_start(c_rows[0:KD, :], a["c_ctx"].rearrange("(n p) -> n p", p=P)).then_inc(ld_c, 16)
            act.dma_start(c_rows[KD:2 * KD, :], a["c"][0].rearrange("(n p) -> n p", p=P)).then_inc(ld_c, 16)
            act.wait_ge(c_t, 1)
            nc.scalar.activation(cond[:, :], bank[7][:, 0:2 * KD], ACT.Silu).then_inc(silu_ok, 1)
            act.wait_ge(silu_ok, 1)
            act.wait_ge(cond_hi, 1)
            for g in range(G):
                nc.scalar.activation(cond_st[:, :, 2 * g:2 * g + 1], cond[:, g * KD:(g + 1) * KD].unsqueeze(2), ACT.Copy)\
                    .then_inc(cond_hi, 1)

            def ada_turn(q):
                for s in range(SLOTS):
                    hi(q + (s + 1) // SLOTS, (s + 1) % SLOTS)
                    multiplied(act, q, s)
                    nc.scalar.activation(ada_rows[:, s, :], bank[4 + s][0:4, :], ACT.Copy).then_inc(ada_out, 1)

            hi(0, 0)
            ada_turn(0)
            act.wait_ge(const_ok, 1)
            ln_std(0)
            with act.Fori(1, DEPTH * Q_ADA) as i:
                ada_turn(i)
            act.wait_ge(ld_small, 32)
            act.wait_ge(r_zero, 1)
            nc.scalar.activation(r_hi[:, :, 0:NE], r_raw[:, :, :], ACT.Copy).then_inc(r_parts, 1)
            for l in range(DEPTH):
                q0 = turn0[l]
                act.wait_ge(coef_ok, l + 1)
                modulate(2 * l)
                act.wait_ge(x_ok, 2 * l + 1)

                def copied(q, s, b):
                    hi(q + (s + 1) // SLOTS, (s + 1) % SLOTS)
                    multiplied(act, q, s)
                    nc.scalar.activation(work[:, b, 0:COL], bank[2 * s][:, :].unsqueeze(1), ACT.Copy).then_inc(in_out0, 1)

                def gate(q, s, b):
                    multiplied(act, q, s)
                    for g, kept in enumerate((in_out0, in_out1)):
                        nc.scalar.activation(blk(b, g), bank[2 * s + g][:, :], ACT.Sigmoid).then_inc(kept, 1)

                with act.Fori(0, RUNS_QKV) as i:
                    for s in range(SLOTS):
                        copied(i + q0, s, bass.ds(i * SLOTS + (B_Q + s), 1))
                q0 += RUNS_QKV
                for s in range(SLOTS):
                    copied(q0, s, slice(B_GB + s, B_GB + s + 1))
                q0 += 1
                def conv_parts(chunks):
                    for c in chunks:
                        act.wait_ge(conv_f, KC * l + c + 1)
                        nc.scalar.activation(hT_hi[:, c, :, :], conv_res(c), ACT.Copy).then_inc(conv_hi, 1)

                for s in range(SLOTS):
                    hi(q0 + (s + 1) // SLOTS, (s + 1) % SLOTS)
                    gate(q0, s, B_GCONV + s)
                conv_parts((0, 1, 2, 3))
                q0 += 1
                hi(q0, 1)
                gate(q0, 0, IN_BLOCKS - 1)
                act.wait_ge(lam_dot, l + 1)
                nc.scalar.activation(lams[:, 2:4], lams[:, 0:2], ACT.Exp).then_inc(lam_exp, 1)
                hi(q0, 2)
                for step in range(JOBS + 4):
                    j = step
                    if j < JOBS:
                        n = keys(j) + T
                        act.wait_ge(j_qk, JOBS * l + j + 1)
                        if j >= 2:
                            act.wait_ge(j_s, JOBS * l + j - 1)
                        nc.scalar.activation(qkT[:, j % 2, 0:n], bank[2 + j % 2][:, 0:n], ACT.Copy).then_inc(j_qkT, 1)
                    j = step - 1
                    if 0 <= j < JOBS:
                        n = keys(j)
                        act.wait_ge(j_max, JOBS * l + j + 1)
                        if j >= 2:
                            act.wait_ge(j_p, JOBS * l + j - 1)
                        for i in range(2):
                            ins = nc.scalar.activation(e_buf[:, j % 2, i, 0:n], s_bank(j, i)[:, 0:n], ACT.Exp,
                                                       bias=nmx[:, j % 2, i:i + 1], scale=SCALE,
                                                       accum_out=esum[:, j % 2, i:i + 1])
                        ins.then_inc(j_exp, 1)
                    j = step - 4
                    if 0 <= j < JOBS:
                        act.wait_ge(j_oc, JOBS * l + j + 1)
                        if JOBS * l + j:
                            act.wait_ge(j_sq, JOBS * l + j)
                        nc.scalar.activation(cv[:, 0, :], head(B_Q, j), ACT.Square, accum_out=osq[:, j:j + 1]).then_inc(j_sq, 1)
                act.wait_ge(j_sq, JOBS * (l + 1))
                nc.scalar.activation(osd[:, :], osq[:, :], ACT.Sqrt, bias=eps_c[:, 0:1], scale=1.0 / VD).then_inc(osd_ok, 1)
                for i in range(4):
                    act.wait_ge(oT_t, 4 * l + i + 1)
                    nc.scalar.activation(hT_hi[:, 4 * (i // 2):4 * (i // 2) + 4, i % 2, :], four(bank[i]), ACT.Copy,
                                         scale=sublng[:, l:l + 1]).then_inc(oT_hi, 1)
                hi(q0 + 1, 0)
                hi(q0 + 1, 1)
                act.wait_ge(kv_kept, 64 * (l + 1))
                gate_broadcast(2 * l)
                for i in range(4):
                    act.wait_ge(m_t, 4 * l + i + 1)
                    nc.scalar.activation(xT_hi[:, 4 * (i // 2):4 * (i // 2) + 4, i % 2, :], four(bank[i]), ACT.Copy)\
                        .then_inc(m_hi, 1)
                hi(q0 + 1, 2)
                q0 += 2
                hi(q0, 0, kind=KINDS[0])
                gate_broadcast(2 * l + 1)
                ln_std(2 * l + 1)
                modulate(2 * l + 1)
                if l == 0:
                    for e in range(DENSE_PARTS):
                        expert(q0 + e * Q_EXPERT, e, KINDS[0] if e + 1 < DENSE_PARTS else FULL)
                else:
                    act.wait_ge(r_max, 1)
                    for g in range(G):
                        ins = nc.scalar.activation(rt[:, 1, g, :], rt[:, 0, g, :], ACT.Exp, bias=rs[:, 0, g:g + 1],
                                                   accum_out=rs[:, 1, g:g + 1])
                    ins.then_inc(r_exp, 1)
                    for i in range(4):
                        act.wait_ge(xt_t, i + 1)
                        nc.scalar.activation(tokens[:, i // 2, i % 2 * COL:(i % 2 + 1) * COL], bank[4 + i][:, :], ACT.Copy)\
                            .then_inc(xt_ok, 1)
                    gathered(0)
                    act.wait_ge(plan_ok, 1)
                    last_pass = act.value_load(plan[0:1, 0:1], min_val=NE - 1, max_val=PASSES - 1)
                    with act.Fori(0, last_pass) as p:
                        one_pass(p * Q_EXPERT + q0, p, False)
                    one_pass(last_pass * Q_EXPERT + q0, last_pass, True)
                ln_std(2 * l + 2)

        @block.vector
        def _(dve):
            dve_n = [0]
            V = nc.vector

            def then(ins):
                dve_n[0] += 1
                ins.then_inc(dve_s, 1)
                dve.wait_ge(dve_s, dve_n[0])

            def lo(q, s, units=range(PARTS), kind=FULL):
                for unit in units:
                    at, n = cut(kind, unit)
                    dve.wait_ge(hi_done, q * (PARTS * SLOTS) + (PARTS * s + unit + 1))
                    at += unit // 2 * 2 * UNIT
                    V.tensor_tensor(w_lo[:, unit, 0:n], raw[:, s, at:at + n], w_hi[:, unit, 0:n].bitcast(F32),
                                    ALU.subtract).then_inc(lo_done, 1)

            def statistics(g):
                for half in range(2):
                    ins = V.bn_stats(st[:, g, half, :], x[:, g, half * COL:(half + 1) * COL])
                then(ins)
                V.bn_aggr(mv[:, g, :], st[:, g, :, :].rearrange("p a b -> p (a b)")).then_inc(stats_ok, 1)

            def normalise(n, g):
                dve.wait_ge(std_ok, G * n + g + 1)
                then(V.reciprocal(rstd[:, g:g + 1], sd[:, g:g + 1]))
                V.tensor_scalar(xhat[:, g, :], x[:, g, :], mv[:, g, 0:1], rstd[:, g:g + 1], ALU.subtract, ALU.mult)\
                    .then_inc(xhat_ok, 1)

            def rests_by_pool(q, s):
                dve.wait_ge(lo_done, q * (PARTS * SLOTS) + (PARTS * s + PARTS))

            def layer_norm(n):
                for g in range(G):
                    statistics(g)
                for g in range(G):
                    normalise(n, g)

            def modulate(n, g):
                dve.wait_ge(xhat_t, G * n + g + 1)
                for k in range(4, KD):
                    ins = V.tensor_scalar(modulated[:, g, k, :], bank[2 * g + 1][:, (k - 4) * T:(k - 3) * T],
                                          modA[:, n, k, g:g + 1], modB[:, n, k, g:g + 1], ALU.mult, ALU.add)
                ins.then_inc(mod_dve, 1)

            def modulated_rests(n, g):
                dve.wait_ge(mod_hi, G * n + g + 1)
                V.tensor_tensor(xT_lo[:, :, g, :], modulated[:, g, :, :], xT_hi[:, :, g, :].bitcast(F32), ALU.subtract)\
                    .then_inc(mod_ok, 1)

            def residual_norm(n, first_half, second_half):
                dve.wait_ge(bc_ok, 4 * (n + 1))

                def gated(g, half):
                    bc = gate_bc[n % 2][g][:, half * COL:(half + 1) * COL]
                    return V.tensor_tensor(bc, bank[4 + 2 * g + half][:, :], bc, ALU.mult)

                first_half()
                for g in range(G):
                    gated(g, 0)
                second_half()
                def add(g):
                    then(V.scalar_tensor_tensor(out=x[:, g, :], in0=x[:, g, :], scalar=ALPHA, in1=gate_bc[n % 2][g],
                                                op0=ALU.mult, op1=ALU.add))

                then(gated(0, 1))
                dve.wait_ge(x_ok, n + 1)
                add(0)
                statistics(0)
                then(gated(1, 1))
                if n % 2 == 0:
                    dve.wait_ge(kv_kept, 64 * (n // 2 + 1))
                normalise(n + 1, 0)
                add(1)
                statistics(1)
                if n < 2 * DEPTH - 1:
                    modulate(n + 1, 0)
                normalise(n + 1, 1)
                if n < 2 * DEPTH - 1:
                    modulated_rests(n + 1, 0)
                    modulate(n + 1, 1)
                    modulated_rests(n + 1, 1)

            def expert(q, ec, behind):
                sizes = KINDS + [behind]
                for j in range(12):
                    nq, ns, n = q + (j + 1) // SLOTS, (j + 1) % SLOTS, sizes[j + 1]
                    if n:
                        lo(nq, ns, (0, 1), n)
                    if j in (2, 4, 6, 9):
                        c = (2, 4, 6, 9).index(j)
                        k0, k1 = HT[c]
                        dve.wait_ge(hT_hi_ok, ec * 4 + (c + 1))
                        for g in range(G):
                            ins = V.tensor_tensor(hT_lo[:, k0:k1, g, :],
                                                  bank[2 + g][:, 0:(k1 - k0) * T].rearrange("p (k t) -> p k t", t=T),
                                                  hT_hi[:, k0:k1, g, :].bitcast(F32), ALU.subtract)
                        ins.then_inc(hT_ok, 1)
                    if n:
                        lo(nq, ns, (2, 3), n)
                    if j < 8 and j % 2 == 1:
                        c = j // 2
                        multiplied(dve, q + j // SLOTS, j % SLOTS)
                        dve.wait_ge(g_silu, ec * 4 + (c + 1))
                        for g in range(G):
                            hc = h[:, g, c * FCOL:(c + 1) * FCOL]
                            ins = V.tensor_tensor(hc, hc, bank[2 + g][:, 0:FCOL], ALU.mult)
                        ins.then_inc(h_ok, 1)

            def route():
                E = lambda i: rt[:, i, :, :]
                B = lambda i: rs[:, i, :].unsqueeze(2).to_broadcast([P, G, NE])
                dve.wait_ge(r_mm, 1)
                V.tensor_copy(logits[:, :], bank[2][0:NE, 0:G * T]).then_inc(r_row, 1)
                dve.wait_ge(r_col, 1)
                then(V.tensor_copy(E(0), bank[3][:, 0:G * NE].rearrange("p (g e) -> p g e", g=G)))
                then(V.tensor_reduce(rs[:, 0, :], E(0), AX_X, ALU.max, negate=True))
                dve.sem_inc(r_max, 1)
                dve.wait_ge(r_exp, 1)
                then(V.reciprocal(rs[:, 2, :], rs[:, 1, :]))
                then(V.tensor_tensor(E(1), E(1), B(2), ALU.mult))
                far = iota[:, :].unsqueeze(1).to_broadcast([P, G, NE])
                for i, best in ((0, 3), (1, 4)):
                    then(V.tensor_reduce(rs[:, best, :], E(1), AX_X, ALU.max))
                    then(V.tensor_tensor(E(2), E(1), B(best), ALU.is_equal))
                    then(V.tensor_tensor(E(3), E(2), far, ALU.mult))
                    then(V.tensor_reduce(rs[:, 5, :], E(3), AX_X, ALU.min))
                    then(V.tensor_tensor(E(4 + i), far, B(5), ALU.is_equal))
                    if i == 1:
                        then(V.tensor_tensor(one_hot[:, :, :], E(4), E(5), ALU.add))
                        dve.sem_inc(mask_ok, 1)
                    if i == 0:
                        then(V.scalar_tensor_tensor(out=E(1), in0=E(4), scalar=-2.0, in1=E(1), op0=ALU.mult, op1=ALU.add))
                then(V.tensor_tensor(rs[:, 6, :], rs[:, 3, :], rs[:, 4, :], ALU.add))
                then(V.reciprocal(rs[:, 7, :], rs[:, 6, :]))
                for i in (0, 1):
                    then(V.tensor_tensor(rs[:, 3 + i, :], rs[:, 3 + i, :], rs[:, 7, :], ALU.mult))
                    then(V.tensor_tensor(E(4 + i), E(4 + i), B(3 + i), ALU.mult))
                then(V.tensor_tensor(gates[:, :, :], E(4), E(5), ALU.add))

            def first_positions():
                posm = pos_tab[:, :, 0:NE]
                then(V.tensor_scalar(posm, one_hot[:, :, :], FAR, -FAR, ALU.mult, ALU.add))
                V.tensor_copy(gate_tab[:, :, 0:NE], gates[:, :, :])
                dve.wait_ge(pos_mm, 1)
                then(V.tensor_tensor(posm, posm, bank[2][:, 64:64 + G * NE].rearrange("p (g e) -> p g e", g=G), ALU.add))
                V.tensor_copy(over[:, 3, :], bank[2][:, 64 + G * NE:64 + (G + 1) * NE]).then_inc(pos_read, 1)

            def make_plan():
                dve.wait_ge(pos_read, 1)
                ov, rank, chosen, junk = (over[:, i, :] for i in range(4))
                then(V.tensor_scalar(ov, junk, float(T), None, ALU.is_gt))
                then(V.memset(rank[:, 0:1], 0.0))
                for e in range(1, NE):
                    then(V.tensor_tensor(rank[:, e:e + 1], rank[:, e - 1:e], ov[:, e - 1:e], ALU.add))
                V.memset(plan_f[:, 1:2], float(NE - 1))
                V.memset(plan_f[:, 5:8], 0.0)
                V.scalar_tensor_tensor(out=plan_f[:, 0:1], in0=rank[:, NE - 1:NE], scalar=float(NE - 1), in1=ov[:, NE - 1:NE],
                                       op0=ALU.add, op1=ALU.add)
                for i in range(PASSES - NE):
                    then(V.scalar_tensor_tensor(out=chosen, in0=rank, scalar=float(i), in1=ov, op0=ALU.is_equal, op1=ALU.mult))
                    sums = [(iota[:, :], float(NE), plan_f[:, 2 + i:3 + i])]
                    for g in range(G):
                        sums.append((pos_tab[:, g, 0:NE], -float(T), pos_tab[:, g, NE + i:NE + i + 1]))
                        sums.append((gate_tab[:, g, 0:NE], 0.0, gate_tab[:, g, NE + i:NE + i + 1]))
                    for v, start, to in sums:
                        then(V.tensor_tensor_reduce(out=junk, in0=chosen, in1=v, scale=1.0, scalar=start, op0=ALU.mult,
                                                    op1=ALU.add, accum_out=to))
                then(V.tensor_copy(plan[:, :], plan_f[:, :]))
                dve.sem_inc(plan_ok, 1)

            def selection(p):
                at = bass.ds(p, 1)
                V.tensor_copy(gate_col[:, :].unsqueeze(2), gate_tab[:, :, at])
                for g in range(G):
                    ins = V.tensor_scalar(select[:, g, :], slot_no[:, :], pos_tab[:, g, at], None, ALU.is_equal)
                ins.then_inc(sel_ok, 1)

            def gathered(p):
                for i in range(2):
                    dve.wait_ge(gx_hi, p * 2 + (i + 1))
                    V.tensor_tensor(xT_lo[:, 4 * i:4 * i + 4, 0, :], four(bank[2 * i]),
                                    xT_hi[:, 4 * i:4 * i + 4, 0, :].bitcast(F32), ALU.subtract).then_inc(gx_ok, 1)

            def one_pass(q, p, last):
                kinds = KINDS + [KINDS[0]]
                for j in range(12):
                    nq, ns = q + (j + 1) // SLOTS, (j + 1) % SLOTS
                    ahead = j < 11 or not last
                    if ahead:
                        lo(nq, ns, (0, 1), kinds[j + 1])
                    if j in (2, 4, 6, 9):
                        c = (2, 4, 6, 9).index(j)
                        k0, k1 = HT[c]
                        dve.wait_ge(hT_hi_ok, (p + DENSE_PARTS) * 4 + (c + 1))
                        V.tensor_tensor(hT_lo[:, k0:k1, 0, :], t_bank(c)[:, 0:(k1 - k0) * T].rearrange("p (k t) -> p k t", t=T),
                                        hT_hi[:, k0:k1, 0, :].bitcast(F32), ALU.subtract).then_inc(hT_ok, 1)
                    if j == 1:
                        dve.wait_ge(st_ok, p + 1)
                        V.tensor_copy(gate_slot[:, :], bank[3][:, G * T:G * T + 1]).then_inc(ge_ok, 1)
                    if j == 8 and not last:
                        selection(p + 1)
                    if j == 10 and not last:
                        gathered(p + 1)
                    if j == 11:
                        dve.wait_ge(y_hi_ok, p * 2 + 1)
                        V.tensor_tensor(y_lo[:, 0:4], four(bank[1]), y_hi[:, 0:4].bitcast(F32), ALU.subtract).then_inc(y_ok, 1)
                    if ahead:
                        lo(nq, ns, (2, 3), kinds[j + 1])
                    if j == 11:
                        dve.wait_ge(y_hi_ok, p * 2 + 2)
                        V.tensor_tensor(y_lo[:, 4:8], four(bank[3]), y_hi[:, 4:8].bitcast(F32), ALU.subtract).then_inc(y_ok, 1)
                    if j < 8 and j % 2 == 1:
                        c = j // 2
                        multiplied(dve, q + j // SLOTS, j % SLOTS)
                        dve.wait_ge(g_silu, (p + DENSE_PARTS) * 4 + (c + 1))
                        dve.wait_ge(ge_ok, p + 1)
                        hc = h[:, 0, c * FCOL:(c + 1) * FCOL]
                        V.scalar_tensor_tensor(out=hc, in0=hc, scalar=gate_slot[:, 0:1], in1=bank[2][:, 0:FCOL],
                                               op0=ALU.mult, op1=ALU.mult).then_inc(h_ok, 1)

            def rotate(b):
                v = blk(b, 1).rearrange("p (m c h i) -> p m c h i", c=2, h=2, i=16)
                x1, x2 = v[:, :, :, 0, :], v[:, :, :, 1, :]
                t4 = [rope_t[:, i * 256:(i + 1) * 256].rearrange("p (m c i) -> p m c i", c=2, i=16) for i in range(4)]
                cos = rope[:, 0, :].rearrange("p (c i) -> p c i", c=2).unsqueeze(1).to_broadcast([P, 8, 2, 16])
                sin = rope[:, 1, :].rearrange("p (c i) -> p c i", c=2).unsqueeze(1).to_broadcast([P, 8, 2, 16])
                V.tensor_tensor(t4[0], x1, cos, ALU.mult)
                V.tensor_tensor(t4[1], x2, sin, ALU.mult)
                V.tensor_tensor(t4[2], x1, sin, ALU.mult)
                then(V.tensor_tensor(t4[3], x2, cos, ALU.mult))
                V.tensor_tensor(x1, t4[0], t4[1], ALU.subtract)
                then(V.tensor_tensor(x2, t4[2], t4[3], ALU.add))

            dve.sem_inc(in_out1, SLOTS)
            V.memset(c_rows, 0.0).then_inc(c_zero, 1)
            V.memset(cond_st[:, :, :].bitcast(F32), 0.0).then_inc(cond_hi, 1)
            V.memset(r_hi[:, :, :].bitcast(F32), 0.0)
            V.memset(r_lo[:, :, :].bitcast(F32), 0.0).then_inc(r_zero, 1)
            dve.wait_ge(cond_hi, 1 + G)
            for g in range(G):
                V.tensor_tensor(cond_st[:, :, 2 * g + 1:2 * g + 2], cond[:, g * KD:(g + 1) * KD].unsqueeze(2),
                                cond_st[:, :, 2 * g:2 * g + 1].bitcast(F32), ALU.subtract).then_inc(cond_ok, 1)

            ada_blocks = adaT[:, :, :, :, :].rearrange("p l v (h k) g -> p (l v h) (k g)", h=2)

            def keep_columns(b, count, s):
                dve.wait_ge(ada_cols, count)
                V.tensor_copy(ada_blocks[:, b, :], bank[s][:, 0:4 * G].unsqueeze(1)).then_inc(ada_kept, 1)

            def ada_turn(q, first):
                for s in range(SLOTS):
                    lo(q + (s + 1) // SLOTS, (s + 1) % SLOTS)
                    if first and s == 2:
                        keep_columns(slice(0, 1), 1, 0)
                    if not first:
                        keep_columns(bass.ds(q * SLOTS + (s - 2), 1), q * SLOTS + (s - 1), (s + 1) % SLOTS)

            lo(0, 0)
            ada_turn(0, True)
            dve.wait_ge(ld_x, 32)
            layer_norm(0)
            with dve.Fori(1, DEPTH * Q_ADA) as i:
                ada_turn(i, False)
            dve.wait_ge(vec_t, 1)
            V.tensor_copy(vecT[:, :], bank[3][:, 0:P]).then_inc(vec_ok, 1)
            V.tensor_copy(biasT[:, :], bank[3][:, P:2 * P]).then_inc(vec_ok, 1)
            for b in (DEPTH * ADA_BLOCKS - 2, DEPTH * ADA_BLOCKS - 1):
                keep_columns(slice(b, b + 1), b + 1, b % SLOTS)
            dve.wait_ge(ada_kept, DEPTH * ADA_BLOCKS)
            dve.wait_ge(vec_ok, 2)
            by_chunk = adaT[:, :, :, :, :].rearrange("p l v k g -> p (l v k) g")
            then(V.tensor_tensor(by_chunk, by_chunk, biasT[:, 0:DEPTH * 6 * KD].unsqueeze(2).to_broadcast([P, DEPTH * 6 * KD, G]), ALU.add))

            def coefficients(n):
                l, i, ln = n // 2, n % 2, V_LN + n * 2 * KD
                ln_g = vecT[:, ln:ln + KD].unsqueeze(2).to_broadcast([P, KD, G])
                ln_b = vecT[:, ln + KD:ln + 2 * KD].unsqueeze(2).to_broadcast([P, KD, G])
                V.scalar_tensor_tensor(out=modA[:, n], in0=adaT[:, l, 3 * i + 1], scalar=1.0, in1=ln_g, op0=ALU.add, op1=ALU.mult)
                then(V.scalar_tensor_tensor(out=modB[:, n], in0=adaT[:, l, 3 * i + 1], scalar=1.0, in1=ln_b, op0=ALU.add,
                                            op1=ALU.mult))
                then(V.tensor_tensor(modB[:, n], modB[:, n], adaT[:, l, 3 * i], ALU.add))

            coefficients(0)
            dve.sem_inc(coef_ok, 1)
            for l in range(DEPTH):
                q0 = turn0[l]
                if l == 0:
                    for g in range(G):
                        modulate(0, g)
                        modulated_rests(0, g)
                    for n in range(1, 2 * DEPTH):
                        coefficients(n)
                    dve.sem_inc(coef_ok, 1)
                    for i in range(DEPTH):
                        then(V.tensor_scalar(sublng[:, i:i + 1], vecT[:, V_SG + V_LAYER * i:V_SG + V_LAYER * i + 1],
                                             1.0 - lam_init(i), None, ALU.mult))
                    dve.wait_ge(r_parts, 1)
                    V.tensor_tensor(r_lo[:, :, 0:NE], r_raw[:, :, :], r_hi[:, :, 0:NE].bitcast(F32), ALU.subtract).then_inc(r_parts, 1)
                dve.wait_ge(ld_lam, 64 * (l + 1))
                for i in range(2):
                    ins = V.tensor_tensor_reduce(out=lamv[:, 2 * i, :], in0=lamv[:, 2 * i, :], in1=lamv[:, 2 * i + 1, :], scale=1.0,
                                                 scalar=0.0, op0=ALU.mult, op1=ALU.add, accum_out=lams[:, i:i + 1])
                ins.then_inc(lam_dot, 1)
                dve.wait_ge(x_ok, 2 * l + 1)
                if l:
                    rests_by_pool(q0, 0)

                def copied(q, s, b):
                    lo(q + (s + 1) // SLOTS, (s + 1) % SLOTS)
                    multiplied(dve, q, s)
                    V.tensor_copy(work[:, b, COL:2 * COL], bank[2 * s + 1][:, :].unsqueeze(1)).then_inc(in_out1, 1)

                def conv(c):
                    dve.wait_ge(conv_t, KC * l + c + 1)
                    w = [vecT[:, V_CW + V_LAYER * l + 4 * i + c:V_CW + V_LAYER * l + 4 * i + c + 1] for i in range(3)]
                    bias = vecT[:, V_CB + V_LAYER * l + c:V_CB + V_LAYER * l + c + 1]
                    t = bank[6 + c % 2][:, :].rearrange("p (w g t) -> p w g t", w=2, g=G)
                    then(V.tensor_copy(pad[:, :, 1:T + 1], t[:, 1]))
                    then(V.tensor_scalar(cv[:, :, :], pad[:, :, 0:T], w[0], bias, ALU.mult, ALU.add))
                    then(V.scalar_tensor_tensor(out=cv[:, :, :], in0=pad[:, :, 1:T + 1], scalar=w[1], in1=cv[:, :, :],
                                                op0=ALU.mult, op1=ALU.add))
                    then(V.scalar_tensor_tensor(out=cv[:, :, :], in0=pad[:, :, 2:T + 2], scalar=w[2], in1=cv[:, :, :],
                                                op0=ALU.mult, op1=ALU.add))
                    V.tensor_tensor(conv_res(c), t[:, 0], cv[:, :, :], ALU.mult).then_inc(conv_f, 1)

                with dve.Fori(0, RUNS_QKV) as i:
                    for s in range(SLOTS):
                        copied(i + q0, s, bass.ds(i * SLOTS + (B_Q + s), 1))
                q0 += RUNS_QKV
                dve.wait_ge(ld_small, 32)
                dve.wait_ge(in_out1, SLOTS + IN_BLOCKS * l + RUNS_QKV * SLOTS)
                for s in range(SLOTS):
                    copied(q0, s, slice(B_GB + s, B_GB + s + 1))
                    rotate((B_Q, B_Q + 1, B_K)[s])
                q0 += 1
                lo(q0, 1)
                dve.wait_ge(in_out0, SLOTS + IN_BLOCKS * l + B_GCONV)
                dve.wait_ge(in_out1, SLOTS + IN_BLOCKS * l + B_GCONV)
                then(V.tensor_tensor(work[:, B_GC, :], work[:, B_GC, :], work[:, B_U, :], ALU.mult))
                dve.sem_inc(gcu_ok, 1)
                lo(q0, 2)
                rotate(B_K + 1)
                dve.sem_inc(roped, 1)
                q0 += 1
                for c in range(KC):
                    conv(c)
                    if c == 1:
                        lo(q0, 0)
                for c in range(KC):
                    dve.wait_ge(conv_hi, KC * l + c + 1)
                    V.tensor_tensor(hT_lo[:, c, :, :], conv_res(c), hT_hi[:, c, :, :].bitcast(F32), ALU.subtract)\
                        .then_inc(conv_ok, 1)
                lo(q0, 1)
                dve.wait_ge(in_out0, SLOTS + IN_BLOCKS * (l + 1))
                dve.wait_ge(in_out1, SLOTS + IN_BLOCKS * (l + 1))
                for half in range(2):
                    multiplied(dve, q0, 1, 2 * half + 1)
                    for g in range(G):
                        ins = V.tensor_tensor(blk(B_GCONV + half, g), bank[4 + 2 * g + half][:, :], blk(B_GCONV + half, g), ALU.mult)
                    ins.then_inc(conv_out, 1)
                dve.wait_ge(lam_exp, l + 1)
                then(V.tensor_tensor(lams[:, 4:5], lams[:, 3:4], lams[:, 2:3], ALU.subtract))
                then(V.tensor_scalar(lams[:, 4:5], lams[:, 4:5], -lam_init(l), None, ALU.add))
                for step in range(JOBS + 4):
                    j = step - 1
                    if 0 <= j < JOBS:
                        n, y = keys(j), j % 2
                        dve.wait_ge(j_s, JOBS * l + j + 1)
                        for i in range(2):
                            ins = V.tensor_reduce(mx[:, y, i:i + 1], s_bank(j, i)[:, 0:n], AX_X, ALU.max)
                        then(ins)
                        V.tensor_scalar(nmx[:, y, :], mx[:, y, :], -SCALE, None, ALU.mult).then_inc(j_max, 1)
                    j = step - 2
                    if 0 <= j < JOBS:
                        dve.wait_ge(j_exp, JOBS * l + j + 1)
                        y = j % 2
                        then(V.reciprocal(rsum[:, y, :], esum[:, y, :]))
                        then(V.tensor_tensor(rsum[:, y, 1:2], rsum[:, y, 1:2], lams[:, 4:5], ALU.mult))
                        n = keys(j)
                        then(V.tensor_scalar(p_buf[:, y, 0:n], e_buf[:, y, 0, 0:n], rsum[:, y, 0:1], None, ALU.mult))
                        V.scalar_tensor_tensor(out=p_buf[:, y, 0:n], in0=e_buf[:, y, 1, 0:n], scalar=rsum[:, y, 1:2],
                                               in1=p_buf[:, y, 0:n], op0=ALU.mult, op1=ALU.add).then_inc(j_p, 1)
                    j = step - 3
                    if 0 <= j < JOBS:
                        y = j % 2
                        dve.wait_ge(j_pT, JOBS * l + j + 1)
                        V.tensor_copy(pT_buf[:, y, 0:keys(j)], bank[4 + y][:, 0:keys(j)]).then_inc(j_pTc, 1)
                    j = step - 4
                    if 0 <= j < JOBS:
                        dve.wait_ge(j_o, JOBS * l + j + 1)
                        V.tensor_copy(head(B_Q, j), bank[4 + j % 2][:, 2 * T:2 * T + VD]).then_inc(j_oc, 1)
                dve.wait_ge(osd_ok, l + 1)
                dve.wait_ge(j_oc, JOBS * (l + 1))
                then(V.reciprocal(ors[:, :], osd[:, :]))
                for half in range(2):
                    o = work[:, B_Q + half, :].rearrange("p (j d) -> p j d", j=8)
                    V.tensor_tensor(o, o, ors[:, 8 * half:8 * half + 8].unsqueeze(2).to_broadcast([P, 8, VD]), ALU.mult)\
                        .then_inc(on_ok, 1)
                for i in range(4):
                    dve.wait_ge(oT_hi, 4 * l + i + 1)
                    at = (slice(None), slice(4 * (i // 2), 4 * (i // 2) + 4), i % 2, slice(None))
                    V.scalar_tensor_tensor(out=hT_lo[at], in0=four(bank[i]), scalar=sublng[:, l:l + 1],
                                           in1=hT_hi[at].bitcast(F32), op0=ALU.mult, op1=ALU.subtract).then_inc(oT_ok, 1)
                rests_by_pool(q0, 2)
                lo(q0 + 1, 0)
                for half in range(2):
                    multiplied(dve, q0 + 1, 0, 2 * half + 1)
                    for g in range(G):
                        ins = V.tensor_tensor(blk(B_GATTN + half, g), bank[4 + 2 * g + half][:, :], blk(B_GATTN + half, g), ALU.mult)
                    then(ins)
                    V.tensor_tensor(work[:, B_GCONV + half, :], work[:, B_GCONV + half, :], work[:, B_GATTN + half, :], ALU.add)\
                        .then_inc(merged, 1)
                for i in range(4):
                    dve.wait_ge(m_hi, 4 * l + i + 1)
                    at = (slice(None), slice(4 * (i // 2), 4 * (i // 2) + 4), i % 2, slice(None))
                    V.tensor_tensor(xT_lo[at], four(bank[i]), xT_hi[at].bitcast(F32), ALU.subtract).then_inc(m_ok, 1)
                rests_by_pool(q0 + 1, 1)
                lo(q0 + 1, 2)
                q0 += 2
                residual_norm(2 * l, lambda: multiplied(dve, q0 - 1, 2, 1), lambda: multiplied(dve, q0 - 1, 2))
                if l == 0:
                    for e in range(DENSE_PARTS):
                        if e == 0:
                            rests_by_pool(q0, 0)
                        expert(q0 + e * Q_EXPERT, e, KINDS[0] if e + 1 < DENSE_PARTS else None)
                    end = q0 + DENSE_PARTS * Q_EXPERT - 1
                    residual_norm(1, lambda: multiplied(dve, end, 2, 1), lambda: multiplied(dve, end, 2))
                else:
                    V.memset(y_hi.bitcast(F32), 0.0).then_inc(y_zero, 1)
                    route()
                    rests_by_pool(q0, 0)
                    first_positions()
                    selection(0)
                    make_plan()
                    gathered(0)
                    last_pass = dve.value_load(plan[0:1, 0:1], min_val=NE - 1, max_val=PASSES - 1)
                    with dve.Fori(0, last_pass) as p:
                        one_pass(p * Q_EXPERT + q0, p, False)
                    one_pass(last_pass * Q_EXPERT + q0, last_pass, True)
                    residual_norm(3, lambda: dve.wait_ge(scattered, 1), lambda: dve.wait_ge(scattered, 2))
            dve.wait_ge(ld_ln, 32 * (2 * DEPTH + 1))
            for g in range(G):
                dve.wait_ge(xhat_ok, G * 2 * DEPTH + g + 1)
                then(V.tensor_tensor(x[:, g, :], xhat[:, g, :], ln_gb[2 * DEPTH][:, 0, :], ALU.mult))
                V.tensor_tensor(x[:, g, :], x[:, g, :], ln_gb[2 * DEPTH][:, 1, :], ALU.add).then_inc(x_ok, 1)

        @block.tensor
        def _(pe):
            def mm3(o, hi, lo, wh, wl, start, stop):
                pe.matmul(o, hi, wh, start=start, stop=False)
                pe.matmul(o, lo, wh, start=False, stop=False)
                return pe.matmul(o, hi, wl, start=False, stop=stop)

            def unit_ready(q, s, unit):
                pe.wait_ge(lo_done, q * (PARTS * SLOTS) + (PARTS * s + unit + 1))

            def part(w, unit, k, n):
                return w[:, unit, k * n:(k + 1) * n]

            def first_block(q, outs, n, norm):
                for g, o in enumerate(outs):
                    pe.wait_ge(mod_ok, G * norm + g + 1)
                    for unit in range(PARTS):
                        if g == 0:
                            unit_ready(q, 0, unit)
                        for k in range(2):
                            kk = 2 * unit + k
                            ins = mm3(o, xT_hi[:, kk, g, :], xT_lo[:, kk, g, :], part(w_hi, unit, k, n),
                                      part(w_lo, unit, k, n), kk == 0, kk == KD - 1)
                        if g == G - 1:
                            ins.then_inc(parts_free, 1)

            def columns(q, s, units, outs, n):
                for unit in units:
                    unit_ready(q, s, unit)
                    for k in range(2):
                        kk = 2 * unit + k
                        for g, o in enumerate(outs):
                            ins = mm3(o, xT_hi[:, kk, g, :], xT_lo[:, kk, g, :], part(w_hi, unit, k, n),
                                      part(w_lo, unit, k, n), kk == 0, kk == KD - 1)
                    ins.then_inc(parts_free, 1)

            def rows(q, s, outs, lhs_hi, lhs_lo, k0, k1, start, stop):
                first = cut((1, k1 - k0), 0)[1]
                for unit in range(PARTS):
                    unit_ready(q, s, unit)
                    c0, c1 = (k0, k0 + first) if unit % 2 == 0 else (k0 + first, k1)
                    for k in range(c0, c1):
                        for g, o in enumerate(outs):
                            ins = mm3(o[unit // 2][:, :], lhs_hi[:, k, g, :], lhs_lo[:, k, g, :],
                                      part(w_hi, unit, k - c0, COL), part(w_lo, unit, k - c0, COL),
                                      start and k == k0, stop and k == k1 - 1)
                    ins.then_inc(parts_free, 1)
                    yield unit

            def row_block(*args):
                for _ in rows(*args):
                    pass

            def transpose_xhat(n):
                for g in range(G):
                    pe.wait_ge(xhat_ok, G * n + g + 1)
                    for k in range(KD):
                        ins = pe.transpose(bank[2 * g + k // 4][:, (k % 4) * T:(k % 4 + 1) * T],
                                           xhat[:, g, k * P:(k + 1) * P], ident[:, :])
                    ins.then_inc(xhat_t, 1)

            def gate_broadcast(n):
                for i in range(4):
                    for k in range(4):
                        col = adaT[:, n // 2, 2 + 3 * (n % 2), 4 * (i % 2) + k, i // 2:i // 2 + 1]
                        ins = pe.matmul(bank[i][:, k * P:(k + 1) * P], col.to_broadcast([P, T]), ident[:, :],
                                        start=True, stop=True)
                    ins.then_inc(bc_mm, 1)

            def expert(q, ec, start, stop, norm):
                def transpose_h(c):
                    k0, k1 = HT[c]
                    pe.wait_ge(h_ok, ec * 4 + (c + 1))
                    for g in range(G):
                        for k in range(k0, k1):
                            ins = pe.transpose(bank[2 + g][:, (k - k0) * T:(k - k0 + 1) * T], h[:, g, k * P:(k + 1) * P],
                                               ident[:, :])
                    ins.then_inc(hT_t, 1)

                for j in range(8):
                    jq, js, c = q + j // SLOTS, j % SLOTS, j // 2
                    if j % 2 == 0:
                        if c:
                            pe.wait_ge(g_silu, ec * 4 + c)
                        outs = [bank[g][:, 0:FCOL] for g in range(G)]
                        if j == 0 and norm is not None:
                            first_block(jq, outs, FCOL, norm)
                            continue
                        columns(jq, js, (0, 1), outs, FCOL)
                        if c:
                            transpose_h(c - 1)
                        columns(jq, js, (2, 3), outs, FCOL)
                    else:
                        if c:
                            pe.wait_ge(hT_ok, ec * 4 + c)
                        outs = [bank[2 + g][:, 0:FCOL] for g in range(G)]
                        columns(jq, js, range(PARTS), outs, FCOL)
                for d, (k0, k1) in enumerate(DOWN):
                    if d == 2:
                        pe.wait_ge(hT_ok, ec * 4 + 4)
                    for unit in rows(q + (8 + d) // SLOTS, (8 + d) % SLOTS, ACC, hT_hi, hT_lo, k0, k1,
                                     start and d == 0, stop and d == 3):
                        if d == 1 and unit == 1:
                            transpose_h(3)

            def gather(p):
                pe.wait_ge(sel_ok, p + 1)
                for k in range(KD):
                    for g in range(G):
                        ins = pe.matmul(bank[k // 4 * 2][:, (k % 4) * T:(k % 4 + 1) * T], tokens[:, g, k * P:(k + 1) * P],
                                        select[:, g, :], start=g == 0, stop=g == G - 1)
                ins.then_inc(gx_mm, 1)

            def scatter(p, last):
                pe.wait_ge(st_ok, p + 1)
                pe.wait_ge(y_ok, p * 2 + 2)
                for half in range(2):
                    for g in range(G):
                        at = slice(4 * half, 4 * half + 4)
                        pe.matmul(ACC[g][half][:, :], selT[:, g, :], y_hi[:, at], start=False, stop=False)
                        ins = pe.matmul(ACC[g][half][:, :], selT[:, g, :], y_lo[:, at], start=False, stop=last)
                    if last:
                        ins.then_inc(scattered, 1)

            def one_pass(q, p, first, last):
                hc = (p + DENSE_PARTS) * 4
                for j in range(8):
                    jq, js, c = q + j // SLOTS, j % SLOTS, j // 2
                    if j % 2 == 0:
                        if c == 0:
                            pe.wait_ge(gx_ok, p * 2 + 2)
                        else:
                            pe.wait_ge(g_silu, hc + c)
                        columns(jq, js, (0, 1), [bank[0][:, 0:FCOL]], FCOL)
                        if c:
                            transpose_h(c - 1, hc, p)
                        columns(jq, js, (2, 3), [bank[0][:, 0:FCOL]], FCOL)
                        if c == 0 and not first:
                            scatter(p - 1, False)
                    else:
                        columns(jq, js, (0, 1), [bank[2][:, 0:FCOL]], FCOL)
                        if c == 0:
                            for g in range(G):
                                pe.transpose(bank[3][:, g * T:(g + 1) * T], select[:, g, :], ident[:, :])
                            for g in range(G):
                                ins = pe.matmul(bank[3][:, G * T:G * T + 1], select[:, g, :], gate_col[:, g:g + 1],
                                                start=g == 0, stop=g == G - 1)
                            ins.then_inc(st_t, 1)
                        columns(jq, js, (2, 3), [bank[2][:, 0:FCOL]], FCOL)
                for d, (k0, k1) in enumerate(DOWN):
                    if d in (0, 2):
                        pe.wait_ge(hT_ok, hc + (3 + d // 2))
                    for unit in rows(q + (8 + d) // SLOTS, (8 + d) % SLOTS, [[bank[1], bank[3]]], hT_hi, hT_lo, k0, k1,
                                     d == 0, d == 3):
                        if d == 1 and unit == 1:
                            transpose_h(3, hc, p)
                        if d == 2 and unit == 1 and not last:
                            gather(p + 1)

            def transpose_h(c, hc, p):
                k0, k1 = HT[c]
                pe.wait_ge(h_ok, hc + (c + 1))
                if c == 1:
                    pe.wait_ge(st_ok, p + 1)
                    pe.wait_ge(ge_ok, p + 1)
                if c == 2:
                    pe.wait_ge(hT_ok, hc + 1)
                for k in range(k0, k1):
                    ins = pe.transpose(t_bank(c)[:, (k - k0) * T:(k - k0 + 1) * T], h[:, 0, k * P:(k + 1) * P], ident[:, :])
                ins.then_inc(hT_t, 1)

            ACC = [bank[4:6], bank[6:8]]
            pe.sem_inc(parts_free, PARTS)
            pe.wait_ge(ident_ok, 1)
            pe.wait_ge(ld_c, 32)
            pe.transpose(bank[7][:, 0:P], c_rows, ident[:, :]).then_inc(c_t, 1)
            pe.wait_ge(cond_ok, G)
            pe.wait_ge(const_ok, 1)

            def turn_columns(s):
                for c in range(4):
                    ins = pe.matmul(bank[s][:, c * G:(c + 1) * G], ada_rows[:, s, c * P:(c + 1) * P], sel[:, :, 0],
                                    start=True, stop=True)
                ins.then_inc(ada_cols, 1)

            def ada_turn(q, first):
                for s in range(SLOTS):
                    pe.wait_ge(ada_out, q * SLOTS + (s + 1))
                    for unit in range(PARTS):
                        unit_ready(q, s, unit)
                        for k in range(2):
                            kk = 2 * unit + k
                            for w in (w_hi, w_lo):
                                ins = pe.matmul(bank[4 + s][0:66, :], cond_st[:, kk, :], part(w, unit, k, COL),
                                                start=kk == 0 and w is w_hi, stop=kk == KD - 1 and w is w_lo)
                        ins.then_inc(parts_free, 1)
                    if not first or s:
                        pe.wait_ge(ada_out, q * SLOTS + (s + SLOTS))
                        if not first:
                            pe.wait_ge(ada_kept, q * SLOTS + (s - 3))
                        turn_columns((s - 1) % SLOTS)

            ada_turn(0, True)
            with pe.Fori(1, DEPTH * Q_ADA) as i:
                ada_turn(i, False)
            pe.wait_ge(ld_vec, 16 * N_VEC)
            pe.transpose(bank[3][:, 0:P], vec_rows, ident[:, :])
            pe.transpose(bank[3][:, P:2 * P], bias_rows, ident[:, :]).then_inc(vec_t, 1)
            pe.wait_ge(ada_out, DEPTH * ADA_BLOCKS + SLOTS)
            pe.wait_ge(ada_kept, DEPTH * ADA_BLOCKS - SLOTS)
            turn_columns(SLOTS - 1)
            pe.wait_ge(ada_kept, DEPTH * ADA_BLOCKS)
            pe.wait_ge(vec_ok, 2)
            for l in range(DEPTH):
                q0 = turn0[l]
                transpose_xhat(2 * l)

                def in_block(q, s, j, first=False):
                    pe.wait_ge(in_out0, j)
                    pe.wait_ge(in_out1, j)
                    outs = [bank[2 * s][:, :], bank[2 * s + 1][:, :]]
                    if first:
                        first_block(q, outs, COL, 2 * l)
                    else:
                        columns(q, s, range(PARTS), outs, COL)

                def conv_transposes(chunks):
                    for c in chunks:
                        if c >= 2:
                            pe.wait_ge(conv_f, KC * l + c - 1)
                        for i, b in enumerate((B_GB, B_GC)):
                            for g in range(G):
                                ins = pe.transpose(bank[6 + c % 2][:, (2 * i + g) * T:(2 * i + g + 1) * T],
                                                   work[:, b, g * COL + c * P:g * COL + (c + 1) * P], ident[:, :])
                        ins.then_inc(conv_t, 1)

                for s in range(SLOTS):
                    in_block(q0, s, IN_BLOCKS * l + s + 1, s == 0)
                with pe.Fori(1, RUNS_QKV) as i:
                    for s in range(SLOTS):
                        in_block(i + q0, s, i * SLOTS + (IN_BLOCKS * l + s + 1))
                for pos in range(RUNS_QKV * SLOTS, IN_BLOCKS):
                    in_block(q0 + pos // SLOTS, pos % SLOTS, IN_BLOCKS * l + pos + 1)
                    if pos == IN_BLOCKS - 3:
                        pe.wait_ge(gcu_ok, l + 1)
                        conv_transposes((0, 1))
                    if pos == IN_BLOCKS - 2:
                        conv_transposes((2, 3))
                q0 += RUNS_IN
                pe.wait_ge(in_out0, SLOTS + IN_BLOCKS * (l + 1) - 1)
                pe.wait_ge(in_out1, SLOTS + IN_BLOCKS * (l + 1) - 1)
                pe.wait_ge(conv_ok, KC * (l + 1))
                row_block(q0, 1, ACC, hT_hi, hT_lo, 0, 4, True, True)
                pe.wait_ge(roped, l + 1)
                pe.wait_ge(ld_cache, 32 * (l + 1))
                pe.wait_ge(in_out0, SLOTS + IN_BLOCKS * (l + 1))
                pe.wait_ge(in_out1, SLOTS + IN_BLOCKS * (l + 1))
                for step in range(JOBS + 4):
                    j = step
                    if j in (1, 2):
                        pe.wait_ge(conv_out, 2 * l + j)
                    if j < JOBS:
                        if j >= 2:
                            pe.wait_ge(j_qkT, JOBS * l + j - 1)
                        o = bank[2 + j % 2]
                        pe.transpose(o[:, 0:T], head(B_Q, j), ident[:, :])
                        ins = pe.transpose(o[:, T:2 * T], head(B_K, j), ident[:, :])
                        if keys(j) > T:
                            ins = pe.transpose(o[:, 2 * T:3 * T], cache[:, 0, head_of(j), :], ident[:, :])
                        ins.then_inc(j_qk, 1)
                    j = step - 1
                    if 0 <= j < JOBS:
                        n, y = keys(j), j % 2
                        pe.wait_ge(j_qkT, JOBS * l + j + 1)
                        if j >= 2:
                            pe.wait_ge(j_exp, JOBS * l + j - 1)
                        for i in range(2):
                            r = slice(HD * i, HD * (i + 1))
                            ins = pe.matmul(s_bank(j, i)[:, 0:n], qkT[r, y, 0:T], qkT[r, y, T:T + n], start=True, stop=True)
                        ins.then_inc(j_s, 1)
                    j = step - 3
                    if 0 <= j < JOBS:
                        y = j % 2
                        pe.wait_ge(j_p, JOBS * l + j + 1)
                        if j >= 2:
                            pe.wait_ge(j_oc, JOBS * l + j - 1)
                        for k in range(keys(j) // T):
                            ins = pe.transpose(bank[4 + y][:, k * T:(k + 1) * T], p_buf[:, y, k * T:(k + 1) * T], ident[:, :])
                        ins.then_inc(j_pT, 1)
                    j = step - 4
                    if 0 <= j < JOBS:
                        y = j % 2
                        pe.wait_ge(j_pTc, JOBS * l + j + 1)
                        vs = [head(B_V, j)] + [cache[:, 1, head_of(j), :]] * (keys(j) > T)
                        for k, v in enumerate(vs):
                            ins = pe.matmul(bank[4 + y][:, 2 * T:2 * T + VD], pT_buf[:, y, k * T:(k + 1) * T], v,
                                            start=k == 0, stop=k == len(vs) - 1)
                        ins.then_inc(j_o, 1)
                for i in range(4):
                    if i % 2 == 0:
                        pe.wait_ge(on_ok, 2 * l + i // 2 + 1)
                    for k in range(4):
                        ins = pe.transpose(bank[i][:, k * T:(k + 1) * T], head(B_Q, 4 * i + k), ident[:, :])
                    ins.then_inc(oT_t, 1)
                pe.wait_ge(oT_ok, 4 * l + 2)
                row_block(q0, 2, ACC, hT_hi, hT_lo, 0, 4, True, False)
                pe.wait_ge(oT_ok, 4 * l + 4)
                row_block(q0 + 1, 0, ACC, hT_hi, hT_lo, 4, 8, False, True)
                gate_broadcast(2 * l)
                for i in range(4):
                    if i % 2 == 0:
                        pe.wait_ge(merged, 2 * l + i // 2 + 1)
                    pe.wait_ge(bc_ok, 8 * l + i + 1)
                    for k in range(4):
                        ins = pe.transpose(bank[i][:, k * T:(k + 1) * T],
                                           work[:, B_GCONV + i // 2, (i % 2) * COL + k * P:(i % 2) * COL + (k + 1) * P], ident[:, :])
                    ins.then_inc(m_t, 1)
                pe.wait_ge(m_ok, 4 * l + 2)
                row_block(q0 + 1, 1, ACC, xT_hi, xT_lo, 0, 4, True, False)
                pe.wait_ge(m_ok, 4 * l + 4)
                row_block(q0 + 1, 2, ACC, xT_hi, xT_lo, 4, 8, False, True)
                q0 += 2
                gate_broadcast(2 * l + 1)
                pe.wait_ge(bc_ok, 4 * (2 * l + 2))
                transpose_xhat(2 * l + 1)
                if l == 0:
                    for e in range(DENSE_PARTS):
                        expert(q0 + e * Q_EXPERT, e, e == 0, e == DENSE_PARTS - 1, None if e else 1)
                else:
                    pe.wait_ge(r_parts, 2)
                    pe.wait_ge(mod_ok, G * 4)
                    for k in range(KD):
                        x_hi, x_lo = (w[:, k, :, :].rearrange("p g t -> p (g t)") for w in (xT_hi, xT_lo))
                        pe.matmul(bank[2][0:66, 0:G * T], r_hi[:, k, :], x_hi, start=k == 0, stop=False)
                        pe.matmul(bank[2][0:66, 0:G * T], r_lo[:, k, :], x_hi, start=False, stop=False)
                        ins = pe.matmul(bank[2][0:66, 0:G * T], r_hi[:, k, :], x_lo, start=False, stop=k == KD - 1)
                    ins.then_inc(r_mm, 1)
                    pe.wait_ge(r_row, 1)
                    for g in range(G):
                        ins = pe.matmul(bank[3][:, g * NE:(g + 1) * NE], logits[:, g * T:(g + 1) * T], ident[0:NE, 0:NE],
                                        start=True, stop=True)
                    ins.then_inc(r_col, 1)
                    for g in range(G):
                        for k in range(KD):
                            ins = pe.transpose(bank[4 + 2 * g + k // 4][:, (k % 4) * T:(k % 4 + 1) * T], modulated[:, g, k, :],
                                               ident[:, :])
                            if k % 4 == 3:
                                ins.then_inc(xt_t, 1)
                    pe.wait_ge(mask_ok, 1)
                    for i, terms in enumerate((((before, 0),), ((all_ones, 0), (before, 1)), ((all_ones, 0), (all_ones, 1)))):
                        for t, (m, g) in enumerate(terms):
                            ins = pe.matmul(bank[2][:, 64 + i * NE:64 + (i + 1) * NE], m[:, :], one_hot[:, g, :],
                                            start=t == 0, stop=t == len(terms) - 1)
                    ins.then_inc(pos_mm, 1)
                    pe.wait_ge(xt_ok, 4)
                    pe.wait_ge(y_zero, 1)
                    for g in range(G):
                        for half in range(2):
                            pe.matmul(ACC[g][half][:, :], xT_hi[:, 0, 0, :], y_hi[:, 4 * half:4 * half + 4], start=True, stop=False)
                    pe.wait_ge(pos_read, 1)
                    gather(0)
                    one_pass(q0, 0, True, False)
                    pe.wait_ge(plan_ok, 1)
                    last_pass = pe.value_load(plan[0:1, 0:1], min_val=NE - 1, max_val=PASSES - 1)
                    with pe.Fori(1, last_pass) as p:
                        one_pass(p * Q_EXPERT + q0, p, False, False)
                    one_pass(last_pass * Q_EXPERT + q0, last_pass, False, True)
                    scatter(last_pass, True)


_INS = ["x_prompt", "x_sample", "cache_k", "cache_v", "c", "c_ctx", "ln_in_g", "ln_in_b", "ada_w", "ada_b", "w_in",
        "conv_w", "conv_b", "w_conv_out", "lam_q1", "lam_k1", "lam_q2", "lam_k2", "subln_g", "w_attn_out", "w_out",
        "ln1_g", "ln1_b", "ln2_g", "ln2_b", "ffn_w_gate", "ffn_w_up", "ffn_w_down", "moe_router", "moe_w_gate",
        "moe_w_up", "moe_w_down"]
_OUTS = [(1, T, D), (1, T, D), (1, DEPTH, HEADS, T, VD), (1, DEPTH, HEADS, T, VD)]


def rope_table():
    import numpy as np
    f = np.float32
    inv = (f(10000.0) ** (-np.arange(0, 32, 2, dtype=f) / f(32))).astype(f)
    row = np.repeat(np.arange(T // 64, dtype=f), 64)[:, None] * inv
    col = np.tile(np.arange(64, dtype=f), T // 64)[:, None] * inv
    ang = np.concatenate([row, col], axis=1).astype(np.float64)
    return np.stack([np.cos(ang), np.sin(ang)], axis=1).astype(f)


def kernel(**inputs):
    import numpy as np
    import concourse.bacc as bacc
    from concourse.bass_utils import run_bass_kernel_spmd as run

    nc = bacc.Bacc("TRN2", target_bir_lowering=False, num_devices=1)
    arrays, args = {}, {}
    for name, value in [(n, inputs[n]) for n in _INS] + [("rope", rope_table())]:
        v = np.ascontiguousarray(value)
        arrays[f"in_{name}"] = v
        args[name] = nc.dram_tensor(f"in_{name}", v.shape, mybir.dt.from_np(v.dtype), kind="ExternalInput").ap()
    outs = [nc.dram_tensor(f"out_{i}", s, F32, kind="ExternalOutput").ap() for i, s in enumerate(_OUTS)]
    program(nc, args, outs)
    r = run(nc, [arrays], core_ids=[0])
    return tuple(r.results[0][f"out_{i}"] for i in range(len(_OUTS)))
```
